# Optimizing a Trainium2 kernel written in Bass

```python
import math, functools
import jax, jax.numpy as jnp
from jax import lax
import numpy as np

D_MODEL = 1024
BATCH = 1
SEQ = 1024
DEPTH = 1
DEC_BATCH = 8
DEC_SEQ = 8
PAST_LEN = 4096
PAGE_SIZE = 128

N_META = 16
BLOCK = 128
META_PAD = BLOCK - N_META
A_HEADS = 4
A_DK = 128
A_DV = 128
A_KW = A_HEADS * A_DK
A_VW = A_HEADS * A_DV
A_CONV = 4
A_CONV_CH = 2 * A_KW + A_VW
A_CHUNK = 64
B_HEADS = 8
B_KV_HEADS = 2
B_GROUP = B_HEADS // B_KV_HEADS
B_HD = 64
WINDOW = 128
C_CH = 512
C_CONV = 31
N_BRANCH = 3
BRANCH_W = 512
N_GROUPS = 4
EXP_PER_GROUP = 4
N_EXPERTS = N_GROUPS * EXP_PER_GROUP
TOP_K_IN_GROUP = 2
D_EXPERT = 256
EPS = 1e-6
SPLIT_SIZES = (A_KW, A_KW, A_VW, A_VW, A_HEADS, A_HEADS,
               B_HEADS * B_HD, B_KV_HEADS * B_HD, B_KV_HEADS * B_HD,
               2 * C_CH, N_BRANCH * D_MODEL)
IN_W = sum(SPLIT_SIZES)

kernel_name = 'hybrid_gdn_swa_conformer_hmoe_step'

def rms_norm(x, w):
    xf = x.astype(jnp.float32)
    y = xf * lax.rsqrt(jnp.mean(xf * xf, axis=-1, keepdims=True) + EPS)
    return (y * w.astype(jnp.float32)).astype(x.dtype)

def layer_norm(x, w, b):
    xf = x.astype(jnp.float32)
    mu = jnp.mean(xf, axis=-1, keepdims=True)
    var = jnp.mean(jnp.square(xf - mu), axis=-1, keepdims=True)
    y = (xf - mu) * lax.rsqrt(var + EPS)
    return (y * w.astype(jnp.float32) + b.astype(jnp.float32)).astype(x.dtype)

def l2norm(x):
    return x * lax.rsqrt(jnp.sum(x * x, axis=-1, keepdims=True) + EPS)

def split_cols(p):
    out, off = [], 0
    for s in SPLIT_SIZES:
        out.append(p[..., off:off + s])
        off += s
    return out

def causal_dwconv(u, hist, w):
    ext = jnp.concatenate([hist.astype(u.dtype), u], axis=1)
    y = lax.conv_general_dilated(ext, w.astype(u.dtype)[:, None, :], window_strides=(1,), padding='VALID',
                                 dimension_numbers=('NWC', 'WIO', 'NWC'), feature_group_count=u.shape[-1])
    return y, ext[:, ext.shape[1] - (w.shape[0] - 1):]

def gated_delta_chunked(q, k, v, g, beta, S0, chunk):
    N, L, H, DK = q.shape
    n = L // chunk

    def blocks(t):
        return jnp.moveaxis(t.reshape(N, n, chunk, H, *t.shape[3:]), 3, 2)

    q, k, v, g, beta = blocks(q), blocks(k), blocks(v), blocks(g), blocks(beta)
    G = jnp.cumsum(g, axis=-1)
    idx = jnp.arange(chunk)
    incl = idx[:, None] >= idx[None, :]
    strict = idx[:, None] > idx[None, :]
    decay = jnp.exp(jnp.where(incl, G[..., :, None] - G[..., None, :], -jnp.inf))
    kk = jnp.einsum('bnhid,bnhjd->bnhij', k, k)
    tri = jnp.where(strict, kk * decay * beta[..., :, None], 0.0) + jnp.eye(chunk, dtype=kk.dtype)
    u = lax.linalg.triangular_solve(tri, v * beta[..., None], left_side=True, lower=True, unit_diagonal=True)
    w = lax.linalg.triangular_solve(tri, k * (beta * jnp.exp(G))[..., None], left_side=True, lower=True,
                                    unit_diagonal=True)
    qk = jnp.einsum('bnhid,bnhjd->bnhij', q, k) * decay
    q_dec = q * jnp.exp(G)[..., None]
    k_dec = k * jnp.exp(G[..., -1:] - G)[..., None]
    g_last = jnp.exp(G[..., -1])
    xs = tuple(jnp.moveaxis(t, 1, 0) for t in (qk, q_dec, k_dec, u, w, g_last))

    def step(S, blk):
        qk_c, qd_c, kd_c, u_c, w_c, gl_c = blk
        v_new = u_c - jnp.einsum('bhcd,bhde->bhce', w_c, S)
        o = jnp.einsum('bhcd,bhde->bhce', qd_c, S) + jnp.einsum('bhij,bhje->bhie', qk_c, v_new)
        S = S * gl_c[..., None, None] + jnp.einsum('bhcd,bhce->bhde', kd_c, v_new)
        return S, o

    S, o = lax.scan(step, S0, xs)
    o = jnp.moveaxis(jnp.moveaxis(o, 0, 1), 2, 3).reshape(N, L, H, v.shape[-1])
    return o, S

def gdn_branch(q, k, v, z, a, b, valid, state, hist, conv_w, a_log, dt_bias, norm_w, chunk):
    N, L, _ = q.shape
    f32 = jnp.float32
    vm = valid[None, :, None]
    qkv = jnp.where(vm, jnp.concatenate([q, k, v], axis=-1), 0)
    qkv, hist = causal_dwconv(qkv, hist, conv_w)
    qkv = jax.nn.silu(qkv.astype(f32))
    qc = l2norm(qkv[..., :A_KW].reshape(N, L, A_HEADS, A_DK)) * (A_DK ** -0.5)
    kc = l2norm(qkv[..., A_KW:2 * A_KW].reshape(N, L, A_HEADS, A_DK))
    vc = qkv[..., 2 * A_KW:].reshape(N, L, A_HEADS, A_DV)
    beta = jnp.where(vm, jax.nn.sigmoid(b.astype(f32)), 0.0)
    g = jnp.where(vm, -jnp.exp(a_log.astype(f32)) * jax.nn.softplus(a.astype(f32) + dt_bias.astype(f32)), 0.0)
    o, S = gated_delta_chunked(qc, kc, vc, g, beta, state.astype(f32), chunk)
    o = rms_norm(o, norm_w) * jax.nn.silu(z.astype(f32).reshape(N, L, A_HEADS, A_DV))
    return o.reshape(N, L, A_VW).astype(q.dtype), S.astype(state.dtype), hist

def sink_attention(q, k, v, mask, sinks):
    f32 = jnp.float32
    s = jnp.einsum('bnqhgd,bnkhd->bnhgqk', q.astype(f32), k.astype(f32)) * (B_HD ** -0.5)
    s = jnp.where(mask[None, :, None, None], s, -jnp.inf)
    sink = jnp.broadcast_to(sinks.astype(f32).reshape(B_KV_HEADS, B_GROUP)[None, None, :, :, None, None],
                            s.shape[:-1] + (1,))
    p = jax.nn.softmax(jnp.concatenate([s, sink], axis=-1), axis=-1)[..., :-1]
    return jnp.einsum('bnhgqk,bnkhd->bnqhgd', p, v.astype(f32))

def swa_prompt(q, k, v, q_norm_w, k_norm_w, sinks):
    n, lp, _ = q.shape
    nb = lp // BLOCK
    q = rms_norm(q.reshape(n, lp, B_KV_HEADS, B_GROUP, B_HD), q_norm_w)
    k = rms_norm(k.reshape(n, lp, B_KV_HEADS, B_HD), k_norm_w)
    v = v.reshape(n, lp, B_KV_HEADS, B_HD)

    def band(t):
        tb = t.reshape(n, nb, BLOCK, B_KV_HEADS, B_HD)
        prev = jnp.concatenate([jnp.zeros_like(tb[:, :1]), tb[:, :-1]], axis=1)
        meta = jnp.broadcast_to(t[:, None, META_PAD:BLOCK], (n, nb, N_META, B_KV_HEADS, B_HD))
        return jnp.concatenate([meta, prev, tb], axis=2)

    qi = jnp.arange(nb)[:, None] * BLOCK + jnp.arange(BLOCK)[None, :]
    kj = (jnp.arange(nb)[:, None] - 1) * BLOCK + jnp.arange(2 * BLOCK)[None, :]
    mj = META_PAD + jnp.arange(N_META)
    meta_ok = mj[None, None, :] <= qi[:, :, None]
    band_ok = ((kj[:, None, :] <= qi[:, :, None]) & (kj[:, None, :] > qi[:, :, None] - WINDOW)
               & (kj[:, None, :] >= BLOCK))
    mask = jnp.concatenate([meta_ok, band_ok], axis=-1)
    o = sink_attention(q.reshape(n, nb, BLOCK, B_KV_HEADS, B_GROUP, B_HD), band(k), band(v), mask, sinks)
    meta_kv = jnp.stack([k[:, META_PAD:BLOCK], v[:, META_PAD:BLOCK]], axis=2)
    win_kv = jnp.stack([k[:, lp - WINDOW:], v[:, lp - WINDOW:]], axis=2)
    return o.reshape(n, lp, B_HEADS * B_HD).astype(q.dtype), (meta_kv, win_kv)

def swa_sample(q, k, v, q_norm_w, k_norm_w, sinks, win_kv, meta_kv):
    n, t, _ = q.shape
    w = win_kv.shape[1]
    q = rms_norm(q.reshape(n, t, B_KV_HEADS, B_GROUP, B_HD), q_norm_w)
    k = rms_norm(k.reshape(n, t, B_KV_HEADS, B_HD), k_norm_w)
    v = v.reshape(n, t, B_KV_HEADS, B_HD)
    new_kv = jnp.stack([k, v], axis=2).astype(win_kv.dtype)
    kv = jnp.concatenate([meta_kv.astype(win_kv.dtype), win_kv, new_kv], axis=1)
    qpos = PAST_LEN + jnp.arange(t)
    wpos = PAST_LEN - w + jnp.arange(w)
    meta_ok = jnp.ones((t, N_META), dtype=bool)
    win_ok = (wpos[None, :] > qpos[:, None] - WINDOW) & (wpos[None, :] >= N_META)
    new_ok = (qpos[None, :] <= qpos[:, None]) & (qpos[None, :] > qpos[:, None] - WINDOW)
    mask = jnp.concatenate([meta_ok, win_ok, new_ok], axis=-1)[None]
    o = sink_attention(q[:, None], kv[:, None, :, 0], kv[:, None, :, 1], mask, sinks)
    new_win = jnp.concatenate([win_kv, new_kv], axis=1)[:, t:]
    return o.reshape(n, t, B_HEADS * B_HD).astype(q.dtype), new_win

def conformer_branch(u2, valid, hist, dw_w, dw_b, ln_w, ln_b):
    u = jnp.where(valid[None, :, None], u2[..., :C_CH] * jax.nn.sigmoid(u2[..., C_CH:]), 0)
    y, hist = causal_dwconv(u, hist, dw_w)
    y = jax.nn.silu(layer_norm(y + dw_b.astype(y.dtype), ln_w, ln_b))
    return y, hist

def token_mix(h, valid, chunk, swa_fn, gdn_state, gdn_hist, conf_hist, lw):
    n, L, _ = h.shape
    aq, ak, av, az, aa, ab, bq, bk, bv, cu, gl = split_cols(jnp.einsum('nld,de->nle', h, lw['w_in']))
    o_a, gdn_state, gdn_hist = gdn_branch(aq, ak, av, az, aa, ab, valid, gdn_state, gdn_hist, lw['gdn_conv_w'],
                                          lw['gdn_a_log'], lw['gdn_dt_bias'], lw['gdn_norm_w'], chunk)
    o_b, swa_new = swa_fn(bq, bk, bv, lw['swa_q_norm_w'], lw['swa_k_norm_w'], lw['swa_sinks'])
    o_c, conf_hist = conformer_branch(cu, valid, conf_hist, lw['conv_dw_w'], lw['conv_dw_b'],
                                      lw['conv_ln_w'], lw['conv_ln_b'])
    branches = jnp.stack([o_a.astype(h.dtype), o_b.astype(h.dtype), o_c.astype(h.dtype)], axis=0)
    per_branch = jnp.einsum('rnlc,rcd->nlrd', branches, lw['w_branch'])
    gates = jax.nn.sigmoid(gl.reshape(n, L, N_BRANCH, D_MODEL).astype(jnp.float32))
    merged = jnp.sum(gates * per_branch, axis=2).astype(h.dtype)
    return merged @ lw['w_out'], (gdn_state, gdn_hist, swa_new, conf_hist)

def hier_moe(h, wg, bg, we, be, w_gate, w_up, w_down):
    N, L, D = h.shape
    x = h.reshape(N * L, D)
    T = x.shape[0]
    f32 = jnp.float32
    rows = jnp.arange(T)
    g_logits = jnp.dot(x, wg).astype(f32) + bg.astype(f32)
    g_prob = jax.nn.softmax(g_logits, axis=-1)
    g_idx = jnp.argmax(g_logits, axis=-1)
    g_w = g_prob[rows, g_idx]
    e_logits = (jnp.dot(x, we).astype(f32) + be.astype(f32)).reshape(T, N_GROUPS, EXP_PER_GROUP)[rows, g_idx]
    top_v, top_i = lax.top_k(e_logits, TOP_K_IN_GROUP)
    wts = jax.nn.softmax(top_v, axis=-1) * g_w[:, None]
    eid = g_idx[:, None] * EXP_PER_GROUP + top_i
    combine = jnp.einsum('tk,tke->te', wts, jax.nn.one_hot(eid, N_EXPERTS, dtype=f32))
    hidden = jax.nn.silu(jnp.einsum('td,edf->tef', x, w_gate)) * jnp.einsum('td,edf->tef', x, w_up)
    hidden = hidden * combine[:, :, None].astype(hidden.dtype)
    return jnp.einsum('tef,efd->td', hidden, w_down).reshape(N, L, D).astype(h.dtype)

def setup_inputs(seed: int = 0) -> dict:
    key = jax.random.key(seed)
    ks = jax.random.split(key, 40)
    f32 = jnp.float32

    def nrm(k, shape, scale):
        return jax.random.normal(k, shape, f32) * scale

    win_buf = min(WINDOW, PAST_LEN)
    dt = jnp.exp(jax.random.uniform(ks[12], (DEPTH, A_HEADS), f32, math.log(1e-3), math.log(1e-1)))
    return {
        'x_prompt': nrm(ks[0], (BATCH, SEQ, D_MODEL), 1.0),
        'x_sample': nrm(ks[1], (DEC_BATCH, DEC_SEQ, D_MODEL), 1.0),
        'state_gdn': nrm(ks[2], (DEPTH, DEC_BATCH, A_HEADS, A_DK, A_DV), 0.1),
        'cache_gdn_conv': nrm(ks[3], (DEPTH, DEC_BATCH, A_CONV - 1, A_CONV_CH), 1.0),
        'cache_swa_kv': nrm(ks[4], (DEPTH, DEC_BATCH, win_buf, 2, B_KV_HEADS, B_HD), 1.0),
        'cache_meta_kv': nrm(ks[5], (DEPTH, DEC_BATCH, N_META, 2, B_KV_HEADS, B_HD), 1.0),
        'cache_conv': nrm(ks[6], (DEPTH, DEC_BATCH, C_CONV - 1, C_CH), 0.5),
        'meta_tokens': nrm(ks[7], (N_META, D_MODEL), 1.0),
        'norm1_w': 1.0 + nrm(ks[8], (DEPTH, D_MODEL), 0.02),
        'norm2_w': 1.0 + nrm(ks[9], (DEPTH, D_MODEL), 0.02),
        'w_in': nrm(ks[10], (DEPTH, D_MODEL, IN_W), D_MODEL ** -0.5),
        'gdn_conv_w': nrm(ks[11], (DEPTH, A_CONV, A_CONV_CH), A_CONV ** -0.5),
        'gdn_a_log': jnp.log(jax.random.uniform(ks[13], (DEPTH, A_HEADS), f32, 1.0, 16.0)),
        'gdn_dt_bias': dt + jnp.log(-jnp.expm1(-dt)),
        'gdn_norm_w': 1.0 + nrm(ks[14], (DEPTH, A_DV), 0.02),
        'swa_q_norm_w': 1.0 + nrm(ks[15], (DEPTH, B_HD), 0.02),
        'swa_k_norm_w': 1.0 + nrm(ks[16], (DEPTH, B_HD), 0.02),
        'swa_sinks': nrm(ks[17], (DEPTH, B_HEADS), 0.5),
        'conv_dw_w': nrm(ks[18], (DEPTH, C_CONV, C_CH), C_CONV ** -0.5),
        'conv_dw_b': nrm(ks[19], (DEPTH, C_CH), 0.02),
        'conv_ln_w': 1.0 + nrm(ks[20], (DEPTH, C_CH), 0.02),
        'conv_ln_b': nrm(ks[21], (DEPTH, C_CH), 0.02),
        'w_branch': nrm(ks[22], (DEPTH, N_BRANCH, BRANCH_W, D_MODEL), BRANCH_W ** -0.5),
        'w_out': nrm(ks[23], (DEPTH, D_MODEL, D_MODEL), D_MODEL ** -0.5),
        'router_group_w': nrm(ks[24], (DEPTH, D_MODEL, N_GROUPS), D_MODEL ** -0.5),
        'router_group_b': nrm(ks[25], (DEPTH, N_GROUPS), 0.01),
        'router_expert_w': nrm(ks[26], (DEPTH, D_MODEL, N_EXPERTS), D_MODEL ** -0.5),
        'router_expert_b': nrm(ks[27], (DEPTH, N_EXPERTS), 0.01),
        'moe_w_gate': nrm(ks[28], (DEPTH, N_EXPERTS, D_MODEL, D_EXPERT), D_MODEL ** -0.5),
        'moe_w_up': nrm(ks[29], (DEPTH, N_EXPERTS, D_MODEL, D_EXPERT), D_MODEL ** -0.5),
        'moe_w_down': nrm(ks[30], (DEPTH, N_EXPERTS, D_EXPERT, D_MODEL), D_EXPERT ** -0.5),
    }

def reference(x_prompt, x_sample, state_gdn, cache_gdn_conv, cache_swa_kv, cache_meta_kv, cache_conv,
              meta_tokens, norm1_w, norm2_w, w_in, gdn_conv_w, gdn_a_log, gdn_dt_bias, gdn_norm_w,
              swa_q_norm_w, swa_k_norm_w, swa_sinks, conv_dw_w, conv_dw_b, conv_ln_w, conv_ln_b,
              w_branch, w_out, router_group_w, router_group_b, router_expert_w, router_expert_b,
              moe_w_gate, moe_w_up, moe_w_down):
    dtp = x_prompt.dtype
    n_p = x_prompt.shape[0]
    t_s = x_sample.shape[1]
    xp = jnp.concatenate([jnp.zeros((n_p, META_PAD, D_MODEL), dtp),
                          jnp.broadcast_to(meta_tokens.astype(dtp)[None], (n_p, N_META, D_MODEL)),
                          x_prompt], axis=1)
    valid_p = jnp.arange(xp.shape[1]) >= META_PAD
    xs = x_sample
    valid_s = jnp.ones((t_s,), dtype=bool)
    gdn_p, gconv_p, swa_p, meta_p, conv_p = [], [], [], [], []
    gdn_s, gconv_s, swa_s, conv_s = [], [], [], []
    for l in range(DEPTH):
        lw = {'w_in': w_in[l], 'gdn_conv_w': gdn_conv_w[l], 'gdn_a_log': gdn_a_log[l],
              'gdn_dt_bias': gdn_dt_bias[l], 'gdn_norm_w': gdn_norm_w[l], 'swa_q_norm_w': swa_q_norm_w[l],
              'swa_k_norm_w': swa_k_norm_w[l], 'swa_sinks': swa_sinks[l], 'conv_dw_w': conv_dw_w[l],
              'conv_dw_b': conv_dw_b[l], 'conv_ln_w': conv_ln_w[l], 'conv_ln_b': conv_ln_b[l],
              'w_branch': w_branch[l], 'w_out': w_out[l]}
        mix, (s_new, gh_new, (mkv_new, wkv_new), ch_new) = token_mix(
            rms_norm(xp, norm1_w[l]), valid_p, A_CHUNK, swa_prompt,
            jnp.zeros((n_p, A_HEADS, A_DK, A_DV), dtp), jnp.zeros((n_p, A_CONV - 1, A_CONV_CH), dtp),
            jnp.zeros((n_p, C_CONV - 1, C_CH), dtp), lw)
        xp = xp + mix
        xp = xp + hier_moe(rms_norm(xp, norm2_w[l]), router_group_w[l], router_group_b[l], router_expert_w[l],
                           router_expert_b[l], moe_w_gate[l], moe_w_up[l], moe_w_down[l])
        gdn_p.append(s_new); gconv_p.append(gh_new); swa_p.append(wkv_new); meta_p.append(mkv_new)
        conv_p.append(ch_new)
        swa_fn = functools.partial(swa_sample, win_kv=cache_swa_kv[l], meta_kv=cache_meta_kv[l])
        mix, (s_new, gh_new, wkv_new, ch_new) = token_mix(
            rms_norm(xs, norm1_w[l]), valid_s, t_s, swa_fn, state_gdn[l], cache_gdn_conv[l], cache_conv[l], lw)
        xs = xs + mix
        xs = xs + hier_moe(rms_norm(xs, norm2_w[l]), router_group_w[l], router_group_b[l], router_expert_w[l],
                           router_expert_b[l], moe_w_gate[l], moe_w_up[l], moe_w_down[l])
        gdn_s.append(s_new); gconv_s.append(gh_new); swa_s.append(wkv_new); conv_s.append(ch_new)
    y_prompt = xp[:, BLOCK:]
    y_sample = xs
    return (y_prompt, y_sample,
            jnp.stack(gdn_p), jnp.stack(gconv_p), jnp.stack(swa_p), jnp.stack(meta_p), jnp.stack(conv_p),
            jnp.stack(gdn_s), jnp.stack(gconv_s), jnp.stack(swa_s), jnp.stack(conv_s))


_drawn_inputs = setup_inputs


def setup_inputs(seed=0):
    import zlib

    import numpy as np

    out = dict(_drawn_inputs(seed))
    spreads = {}
    factors = {'gdn_norm_w': 10.434,
     'swa_q_norm_w': 8.0,
     'swa_k_norm_w': 3.355,
     'swa_sinks': 64.0,
     'conv_ln_b': 3.866,
     'router_expert_b': 15.756,
     'norm2_w': 3.53,
     'conv_dw_b': 4.439,
     'conv_ln_w': 3.962,
     'router_group_b': 4.156}
    for name, (base, spread) in spreads.items():
        noise = np.random.default_rng([zlib.crc32(name.encode()), seed]).standard_normal(out[name].shape)
        drawn = base * np.exp(spread * noise) if base else spread * noise
        out[name] = __import__('jax').numpy.asarray(drawn.astype(out[name].dtype))
    for name, factor in factors.items():
        out[name] = (out[name] * factor).astype(out[name].dtype)
    return out
```

```python
import numpy as np
import concourse.bass as bass
from concourse import mybir

F32 = mybir.dt.float32
ALU = mybir.AluOpType
ACT = mybir.ActivationFunctionType
AX = mybir.AxisListType

P = 128
D = 1024
KD = D // P
SEQ, NS, TS, NM = 1024, 8, 8, 16
S = NS * TS
TOK = S + SEQ
ALL = TOK + NM
NT = 1 + SEQ // P
H, DK = 4, 128
CONV, QKV = 4, 3 * H * DK
HB, KVH, HD = 8, 2, 64
W = 128
CC, CT = 512, 31
NG, EPG, E, F = 4, 4, 16, 256
EPS = 1e-6
C_Z = QKV
C_AB = C_Z + H * DK
C_U = C_AB + 2 * H + (HB + 2 * KVH) * HD
C_G = C_U + 2 * CC
NAT = C_U - C_AB
NQK = (HB + KVH) * HD
CH = 368
CHS = [(0, CH), (CH, CH), (2 * CH, CH)]
CHP = [(0, CH), (CH, CH), (2 * CH, TOK - 2 * CH)]
EXS, EXP_ = NS * (CONV - 1 + TS), CONV - 1 + NM + SEQ
UXS, UXP = NS * (CT - 1 + TS), CT - 1 + NM + SEQ
NEG = -1.0e30
NHR = NS * (CONV - 1) + CONV
CI = 0
CU = CI + P
CN = CU + 2 * P
CS = CN + 2 * P
CSS = CS + 2 * P
CL = CSS + 2 * P
CQ = CL + 7 * P
C1 = CQ + NS + 1
CB = C1 + P
CM = CB + 2 * P
CR = CM + W + NM + TS
NCST = CR + HB


def constants():
    i = np.arange(P)
    seq0 = np.where(i < S, i // TS, np.where(i < S + NM, NS, -1 - i))
    c = np.zeros((P, NCST), np.float32)
    c[:, CI:CU] = np.eye(P)
    for n, seq in enumerate((seq0, np.zeros(P, int))):
        same = seq[:, None] == seq[None, :]
        upto = same & (i[:, None] <= i[None, :])
        c[:, CU + n * P:CU + (n + 1) * P] = upto
        c[:, CN + n * P:CN + (n + 1) * P] = np.where(upto, 0, NEG)
        c[:, CS + n * P:CS + (n + 1) * P] = upto & (i[:, None] < i[None, :])
        c[:, CSS + n * P:CSS + (n + 1) * P] = same
    for l in range(7):
        s = 1 << l
        c[:, CL + l * P:CL + (l + 1) * P] = ((i[:, None] // s) % 2 == 1) & (i[None, :] // s == i[:, None] // s - 1)
    c[:, CQ:C1] = seq0[:, None] == np.arange(NS + 1)[None, :]
    c[:, C1:CB] = 1.0
    d = i[:, None] + P - np.arange(2 * P)[None, :]
    c[:, CB:CM] = np.where((d >= 0) & (d < W), 0, NEG)
    t = (i % TS)[:, None]
    j = np.arange(W + NM + TS)[None, :]
    ok = np.where(j < W, j > t, np.where(j < W + NM, True, j - W - NM <= t))
    c[:, CM:CR] = np.where(ok, 0, NEG)
    head = (i // 32 % 2) * 4 + i % 32 // TS
    c[:, CR:] = head[:, None] == np.arange(HB)[None, :]
    return c


class Steps:

    def __init__(self, sem, names):
        self.sem, self.names, self.next = sem, names.split(), 0

    def __call__(self, name):
        assert self.names[self.next % len(self.names)] == name, (name, self.names, self.next)
        self.next += 1
        return self.sem, 1

    def at(self, n, name):
        return self.sem, n * len(self.names) + (self.names.index(name) + 1)


def wait(e, value):
    sem, v = value
    if not isinstance(v, int) or v > 0:
        e.wait_ge(sem, v)


def build(nc, A, O):
    names = {}

    def place(name, at, *shape, parts=P):
        n = int(np.prod(shape))
        assert at + n <= WORDS, (name, at + n, WORDS)
        names[name] = (at, n)
        return nc.alloc_sbuf_tensor_at(name, [parts, *shape], F32, offset=BASE + 4 * at)

    def up(n):
        return (n + 7) // 8 * 8

    def small(name, *shape):
        at = cursor[0]
        cursor[0] = up(at + int(np.prod(shape)))
        return place(name, at, *shape)

    cursor = [up(NCST)]
    BASE = (nc.sbuf_base + 63) // 64 * 64
    WORDS = (nc.sbuf_usable_end - BASE) // 4
    sems = {}

    def sem(name):
        sems[name] = nc.alloc_semaphore(name)
        return sems[name]

    ps = nc.alloc_psum_tensor("psum", [P, 8, 512], F32)

    cst = place("cst", 0, NCST)
    nvec = small("nvec", KD + 2)
    n2w = small("n2w", KD)
    dvec = small("dvec", 4, CT + 3)
    qw = small("qw", 1)
    eps = small("eps", 2)
    sink = small("sink", HB)
    sinkr = small("sinkr", 1)
    alog = small("alog", H)
    dtb = small("dtb", H)
    kw = small("kw", HD)
    ab = small("ab", NT, 2 * H)
    rbias = small("rbias", NG + E)
    st1 = small("st1", 12)
    st2 = small("st2", 48)
    tmp36 = small("tmp36", NT, H)
    tmq36 = small("tmq36", NT, H)
    histT = small("histT", 12, NHR)
    R1 = up(cursor[0])
    R2 = R1 + KD * ALL
    R3 = R2 + 12 * ALL
    R4, R5, R6 = R3 + 4 * TOK, R3 + 8 * TOK, R3 + 12 * TOK
    RW = R3 + 16 * TOK

    hT = place("hT", R1, KD, ALL)
    qkv = place("qkv", R2, 12, ALL)
    z = place("z", R3, 4, TOK)
    oc = place("oc", R4, 4, TOK)
    ob = place("ob", R5, 4, TOK)
    oa = place("oa", R6, 4, TOK)
    qT = place("qT", RW, 4, NT * P)
    kT = place("kT", RW + 4 * NT * P, NT * P)
    kv = place("kv", RW + 5 * NT * P, NT, 2 * P)
    RX = RW + 7 * NT * P
    wat = place("wat", R2, KD, NAT)
    xt = place("xt", R3, D)
    ht = place("ht", R3 + D, D)
    sqj = place("sqj", R3 + 2 * D, D)
    hTt = place("hTt", R3 + 3 * D, KD, P)
    at = place("at", R3 + 4 * D, NAT)
    sq2 = place("sq2", R3 + 5 * D, NQK)
    qp = place("qp", R3 + 5 * D + NQK, 4, 2, HD)
    hrow = place("hrow", R5, QKV, parts=NHR)
    urow = place("urow", R5 + QKV, 2, CC, parts=NS * (CT - 1) // 2)
    vrow = place("vrow", R5 + QKV + 2 * CC, CC, parts=CT + 3)
    nrow = place("nrow", R5 + QKV + 3 * CC, P, parts=KD + 2)
    wB = place("wB", R5, 4, KD, P)
    ext = place("ext", R6, 2, EXS + EXP_)
    sig = place("sig", R6 + up(2 * (EXS + EXP_)), ALL)
    chistT = place("chistT", R6 + up(2 * (EXS + EXP_)) + ALL, 4, NS * (CT - 1))
    uxt = place("uxt", RX, UXS + UXP)
    tailT = place("tailT", RX + up(UXS + UXP), 12, 27)
    utail = place("utail", RX + up(UXS + UXP) + up(324), 4, S + CT - 1)
    sqb = place("sqb", R6, 4, CH)
    rsb = place("rsb", R6 + 4 * CH, 2, CH)
    hq = place("hq", R5, 2, QKV, parts=24)
    hu = place("hu", R5 + 2 * QKV, CC, parts=S + CT - 1)
    sc = place("sc", R6, HB, NM + 2 * P)
    PT = place("PT", R6 + HB * (NM + 2 * P), HB, 2 * P)
    PTm = place("PTm", RX, HB, P, parts=NM)
    otok = place("otok", R6, HB, HD)
    qst = place("qst", RX + D + 512, 4, P)
    vm = place("vm", RX + D + 1024, P, parts=NM)
    kst = place("kst", RX + D, 2 * P)
    win = place("win", R6, NS, 2 * P)
    mk = place("mk", R6 + 2048, P)
    kTw = place("kTw", R6 + 2176, NS, W + NM + TS)
    scs = place("scs", R6 + 2176 + 1216, 4, W + NM + TS)
    odup = place("odup", R6 + 2176, 4, 2, HD)
    PTw = place("PTw", RX, 4, P)
    PTn = place("PTn", RX + 512, 4, P, parts=NM + TS)
    vmn = place("vmn", RX + 1024, NS, P, parts=NM + TS)
    qs = place("qs", R6 + 4000, NS, 4, TS)
    g_names = "eG dec AtT PT2 Am B0 B1 Dm Dt Wt vb kbg kdec qdec vnew"
    G = {n: place("g_" + n, RW + 12 * P + 512 * k, H, P) for k, n in enumerate(g_names.split())}
    G["nwT"] = G["kbg"]
    stg = place("stg", RW, 12, P)
    St = place("St", RW + 12 * P + 512 * 15, H, P)
    gsm = place("gsm", RW + 12 * P + 512 * 16, 32)
    vexp = place("vexp", names["g_Am"][0], NS + 1, P)
    S0 = place("S0", R6, NS, H, P)
    gnt = place("gnt", RW, ALL)
    gstd = place("gstd", RW + ALL, TOK)
    mT = place("mT", R2, KD, TOK)
    gw = place("gw", RW, 2, 3, KD, P)
    bw = place("bw", R2 + KD * TOK, 2, 3, 4, P)
    gs = place("gs", RW + 6 * KD * P, 2, CH)
    gm = place("gm", RW + 6 * KD * P + 2 * CH, 2, CH)
    wo = place("wo", RW, KD, D)
    x2 = place("x2", R3, NT, D)
    wr = place("wr", RW + 8 * D, KD, NG + E)
    mst = place("mst", R2 + KD * TOK, KD, P)
    xe = place("xe", R2 + KD * TOK + D, D)
    he = place("he", R2 + KD * TOK + 2 * D, D)
    h2t = place("h2t", R2 + KD * TOK + 3 * D, KD, P)
    h2 = place("h2", R1, KD, TOK)
    rl = place("rl", RW + 8 * D + 160, NT, NG + E)
    RC = RW + 8 * D + 160 + 184
    comb = place("comb", RC, NT, E)
    esel = place("esel", RC + 144, NT, EPG)
    ra = place("ra", RC + 184, NT, E)
    rb = place("rb", RC + 328, NT, EPG)
    rc = place("rc", RC + 368, NT, EPG)
    rd = place("rd", RC + 408, NT, EPG)
    goh = place("goh", RC + 448, NT, NG)
    r1 = place("r1", RC + 488, 8, NT)
    iota4 = place("iota4", RC + 560, EPG)
    ew = [place("ew0", R2, 3, 2048), place("ew1", R3 + NT * D, 3, 2048)]
    hid = place("hid", R2 + 6144, 2, TOK)
    sg = place("sg", R2 + 6144 + 2 * TOK, 2, CH)
    assert R2 + 6144 + 2 * TOK + 2 * CH <= R3 and R3 + NT * D + 6144 <= RW

    def cc(a, n=P):
        return cst[:, a:a + n]

    ident = cc(CI)
    w_in = A["w_in"][0]

    s_small, s_wat, s_out = sem("small_loaded"), sem("wat_loaded"), sem("outputs_written")
    s_hist, s_x, s_x0 = sem("hist_loaded"), sem("x_loaded"), sem("x0_loaded")
    s_w = [sem(f"w_slot{k}_loaded") for k in range(4)]
    s_end = sem("phase_ended")
    s_vm, s_win, s_S0 = sem("vm_loaded"), sem("win_loaded"), sem("state_loaded")
    s_gw = [sem(f"merge_w{k}_loaded") for k in range(2)]
    s_wo, s_xe = sem("wo_loaded"), sem("xe_loaded")
    s_ew = [sem(f"expert_w{k}_loaded") for k in range(2)]
    s_vnT, s_vnP, s_vx, s_dS0, s_vx2 = (sem(n) for n in ("samples_wS_out", "samples_v_new", "v_spread", "samples_dS", "samples_S_done"))
    N_SMALL, N_HIST, N_WIN = 12, 7, 3 + NS
    s_init, s_hq, s_sT = sem("init_done"), sem("cache_rows_done"), sem("state_out_done")
    st = {}

    def steps(key, pe="", act="", dve="", pool=""):
        st[key] = tuple(Steps(sem(f"{key}_{n}"), s) if s else None
                        for n, s in (("pe", pe), ("act", act), ("dve", dve), ("pool", pool)))

    steps("pre", pe="hist", act="histT chistT", dve="vec")
    steps("A1", pe="tr proj", act="sq std", dve="rs h hTt", pool="hT")
    steps("A2", pe="qkT", act="at sq2 std2 qT", dve="ssq rs2 qk keep")
    steps("gb", act="lse sig", dve="x m g")
    steps("bq", pe="proj", act="ev silu", dve="conv", pool="hist tail")
    steps("bz", pe="proj", act="z")
    steps("bu", pe="gate value", act="sig", dve="u conv", pool="hist tail")
    steps("ln", pe="mu var", act="sq std silu", dve="cent rs norm")
    steps("rows", pe="q u", act="q", dve="u")
    steps("l2", pe="ss", act="sq std", dve="norm")
    steps("at", pe="sc trm tra trb pv oT", act="exp PTa oT", dve="sc max den PTm PTb o", pool="q")
    steps("sa", pe="kT sc tr pv oT", act="kT exp PT", dve="qs sc max den o oT")
    steps("gd", pe="G kkpq kv At D1 " + " ".join(f"W{l} X{l}" for l in range(1, 7)) + " u v2 o dS",
          act="eG dec D1 " + " ".join(f"W{l}" for l in range(1, 7)) + " nw o",
          dve="cols arg At PT2 kq A D1 " + "B1 B2 X1 B3 X2 B4 X3 B5 X4 B6 X5 X6" + " vn S",
          pool="stage")
    steps("gn", pe="ss", act="sq std", dve="a b")
    steps("mg", pe="g0 b0 g1 b1 g2 b2", act="s0 s1 s2", dve="m0 m1 m2")
    steps("op", pe="mix tr rt", act="sq std", dve="x2 rs h hT rl", pool="stage h2")
    steps("rt", act="eg es", dve="gm em w")
    steps("ch", pe="c", act="s", dve="h")
    steps("dn", pe="y", dve="acc")

    phase = {"n": 0}
    marks = {}

    def end_phase(e, k):
        e.drain().then_inc(s_end, 1)
        e.wait_ge(s_end, 4 * k)

    def tile_cols(t):
        return bass.ds(S + P * (t - 1), P) if not isinstance(t, int) else slice(S + P * (t - 1), S + P * t)

    def ds(start, n):
        return slice(start, start + n) if isinstance(start, int) else bass.ds(start, n)

    def b3(ap, n):
        return ap.unsqueeze(2).to_broadcast([ap.shape[0], ap.shape[1], n])

    def b2(ap, n):
        return ap.unsqueeze(1).to_broadcast([ap.shape[0], n, ap.shape[1]])

    block = nc.Block()
    block.__enter__()

    @block.sync
    def _(sp):
        def load(dst, src, s):
            sp.dma_start(dst, src).then_inc(s, 16)

        def store(dst, src):
            st_out["n"] += 16
            sp.dma_start(dst, src).then_inc(s_out, 16)

        st_out = {"n": 0}
        load(cst[:], A["consts"], s_small)
        load(nrow[0:KD, :], A["norm1_w"][0].rearrange("(k p) -> k p", p=P), s_small)
        load(nrow[KD:KD + 1, :], A["gdn_norm_w"], s_small)
        load(nrow[KD + 1:KD + 2, 0:HD], A["swa_q_norm_w"], s_small)
        load(nrow[KD + 1:KD + 2, HD:P], A["swa_q_norm_w"], s_small)
        load(n2w[:], A["norm2_w"][0].rearrange("(p k) -> p k", k=KD), s_small)
        load(sink[:], A["swa_sinks"][0].partition_broadcast(P), s_small)
        load(alog[:], A["gdn_a_log"][0].partition_broadcast(P), s_small)
        load(dtb[:], A["gdn_dt_bias"][0].partition_broadcast(P), s_small)
        load(kw[:], A["swa_k_norm_w"][0].partition_broadcast(P), s_small)
        load(rbias[:, 0:NG], A["router_group_b"][0].partition_broadcast(P), s_small)
        load(rbias[:, NG:NG + E], A["router_expert_b"][0].partition_broadcast(P), s_small)
        assert N_SMALL == 12
        sp.wait_ge(s_init, 1)
        load(xt[0:S, :], A["x_sample"].rearrange("b t d -> (b t) d"), s_x0)
        load(xt[S:S + NM, :], A["meta_tokens"], s_x0)
        load(wat[:], w_in[:, C_AB:C_U].rearrange("(k p) n -> p k n", p=P), s_wat)
        load(hrow[0:NHR - CONV, :], A["cache_gdn_conv"][0].rearrange("b t c -> (b t) c"), s_hist)
        load(hrow[NHR - CONV:NHR, :], A["gdn_conv_w"][0], s_hist)
        load(urow[:], A["cache_conv"][0].rearrange("(a b) t c -> (b t) a c", a=2), s_hist)
        load(vrow[0:CT, :], A["conv_dw_w"][0], s_hist)
        load(vrow[CT:CT + 1, :], A["conv_dw_b"], s_hist)
        load(vrow[CT + 1:CT + 2, :], A["conv_ln_w"], s_hist)
        load(vrow[CT + 2:CT + 3, :], A["conv_ln_b"], s_hist)
        assert N_HIST == 7
        store(O["cache_swa_kv_s"][0][:, 0:W - TS].rearrange("b w c h d -> b (w c h d)"),
              A["cache_swa_kv"][0][:, TS:W].rearrange("b w c h d -> b (w c h d)"))
        store(O["cache_conv_s"][0][:, 0:CT - 1 - TS].rearrange("b w c -> b (w c)"),
              A["cache_conv"][0][:, TS:CT - 1].rearrange("b w c -> b (w c)"))
        with sp.Fori(1, NT) as t:
            sp.wait_ge(*st["A1"][2].at(t - 1, "h"))
            load(xt[:], A["x_prompt"][0][ds(P * (t - 1), P), :], s_x)

        def load_w(col, k):
            load(wB[:, k], w_in[:, col].rearrange("(k p) n -> p k n", p=P), s_w[k])

        sp.wait_ge(*st["pre"][1].at(0, "chistT"))
        for k in range(4):
            load_w(ds(P * k, P), k)
        with sp.Fori(1, 3) as i:
            for k in range(4):
                sp.wait_ge(*st["bq"][0].at(i * 4 + k - 4, "proj"))
                load_w(ds(i * 4 * P + k * P, P), k)
        for k in range(4):
            sp.wait_ge(*st["bq"][0].at(8 + k, "proj"))
            load_w(ds(C_Z + P * k, P), k)
        for j in range(4):
            for g in range(2):
                k = 2 * (j % 2) + g
                sp.wait_ge(*(st["bz"][0].at(k, "proj") if j < 2 else
                             st["bu"][0].at(j - 2, ("gate", "value")[g])))
                load_w(ds(C_U + CC * (1 - g) + P * j, P), k)
        sp.wait_ge(*st["rows"][2].at(0, "u"))
        sp.wait_ge(*st["rows"][1].at(0, "q"))
        store(O["cache_gdn_conv_s"][0].rearrange("b t c -> (b t) c"), hq[:, 0, :])
        store(O["cache_gdn_conv_p"][0, 0], hq[0:CONV - 1, 1, :])
        for b in range(NS):
            store(O["cache_conv_s"][0, b, CT - 1 - TS:CT - 1, :], hu[TS * b:TS * (b + 1), :])
        store(O["cache_conv_p"][0, 0], hu[S:S + CT - 1, :])
        sp.wait_ge(s_out, st_out["n"])
        sp.sem_inc(s_hq, 1)
        sp.wait_ge(s_end, 4)
        for b in range(NS):
            store(O["cache_swa_kv_s"][0, b, W - TS:W].rearrange("t c h d -> t (c h d)"),
                  kv[TS * b:TS * (b + 1), 0, :])
        store(O["cache_meta_kv_p"][0, 0].rearrange("t c h d -> t (c h d)"), kv[S:S + NM, 0, :])
        store(O["cache_swa_kv_p"][0, 0].rearrange("t c h d -> t (c h d)"), kv[:, NT - 1, :])
        sp.wait_ge(s_end, 8)
        load(vm[:], kv[S:S + NM, 0, P:2 * P], s_vm)
        sp.wait_ge(s_end, 12)
        load(win[:], A["cache_swa_kv"][0].rearrange("b w c h d -> w b (c h d)"), s_win)
        load(mk[:], A["cache_meta_kv"][0][:, :, 0].rearrange("b m h d -> (b m) (h d)"), s_win)
        load(vmn[0:NM], A["cache_meta_kv"][0][:, :, 1].rearrange("b m h d -> m b (h d)"), s_win)
        for b in range(NS):
            load(vmn[NM:NM + TS, b, :], kv[TS * b:TS * (b + 1), 0, P:2 * P], s_win)
        assert N_WIN == 3 + NS
        sp.wait_ge(s_end, 16)
        load(S0[:], A["state_gdn"][0].rearrange("b h k v -> k b h v"), s_S0)
        sp.wait_ge(*st["gd"][2].at(0, "S"))
        store(O["state_gdn_s"][0].rearrange("b h k v -> k b h v"), S0[:])
        sp.wait_ge(*st["gd"][2].at(NT - 1, "S"))
        store(O["state_gdn_p"][0, 0].rearrange("h k v -> k h v"), St[:])
        sp.wait_ge(s_out, st_out["n"])
        sp.sem_inc(s_sT, 1)

        def load_m(n, k):
            load(gw[:, k, 0], w_in[:, ds(C_G + P * n, P)].rearrange("(k p) n -> p k n", p=P), s_gw[k])
            load(gw[:, k, 1], w_in[:, ds(C_G + D + P * n, P)].rearrange("(k p) n -> p k n", p=P), s_gw[k])
            load(gw[:, k, 2], w_in[:, ds(C_G + 2 * D + P * n, P)].rearrange("(k p) n -> p k n", p=P), s_gw[k])
            for r in range(3):
                load(bw[:, k, r], A["w_branch"][0, r][:, ds(P * n, P)].rearrange("(k p) n -> p k n", p=P), s_gw[k])

        sp.wait_ge(s_end, 24)
        load_m(0, 0)
        load_m(1, 1)
        with sp.Fori(1, 4) as i:
            for k in range(2):
                sp.wait_ge(*st["mg"][0].at(3 * (2 * i + k) - 4, "b2"))
                load_m(2 * i + k, k)
        def load_e(e, k):
            for m, name in enumerate(("moe_w_gate", "moe_w_up")):
                load(ew[k][:, m, :], A[name][0][ds(e, 1)].rearrange("e (p k) f -> p (e k f)", k=KD), s_ew[k])
            load(ew[k][:, 2, :].rearrange("p (k n) -> p k n", k=2),
                 A["moe_w_down"][0][ds(e, 1)].rearrange("e (k p) n -> p (e k) n", p=P), s_ew[k])

        sp.wait_ge(s_end, 28)
        load(wo[:], A["w_out"][0].rearrange("(k p) n -> p k n", p=P), s_wo)
        load(wr[:, :, 0:NG], A["router_group_w"][0].rearrange("(p k) n -> p k n", k=KD), s_wo)
        load(wr[:, :, NG:NG + E], A["router_expert_w"][0].rearrange("(p k) n -> p k n", k=KD), s_wo)
        load_e(1, 1)
        load(xe[0:S, :], A["x_sample"].rearrange("b t d -> (b t) d"), s_xe)
        with sp.Fori(1, NT) as t:
            sp.wait_ge(*st["op"][2].at(t - 1, "x2"))
            load(xe[:], A["x_prompt"][0][ds(P * (t - 1), P), :], s_xe)

        sp.wait_ge(s_end, 32)
        load_e(0, 0)
        with sp.Fori(1, E // 2) as i:
            for k in range(2):
                sp.wait_ge(*st["dn"][0].at((2 * i + k - 1) * 2 * NT - 1, "y"))
                load_e(2 * i + k, k)
        sp.wait_ge(s_end, 36)
        store(O["y_sample"].rearrange("b t d -> (b t) d"), x2[0:S, 0, :])
        store(O["y_prompt"][0].rearrange("(t p) d -> p t d", p=P), x2[:, 1:NT, :])
        sp.wait_ge(s_out, st_out["n"])

    @block.tensor
    def _(pe):
        def mm(out, lhsT, rhs, start=True, stop=True):
            return pe.matmul(out, lhsT, rhs, start=start, stop=stop, skip_group_check=True)

        def tr(out, in_):
            n = in_.shape[0]
            return pe.transpose(out, in_, cst[0:n, CI:CI + n])

        pe.wait_ge(s_small, 16 * N_SMALL)
        pe.wait_ge(s_hist, 16 * N_HIST)
        for c in range(12):
            tr(ps[:, 0, NHR * c:NHR * (c + 1)], hrow[:, P * c:P * (c + 1)])
        for j in range(4):
            for a in range(2):
                tr(ps[:, 1 + j // 2, 240 * (j % 2) + 120 * a:240 * (j % 2) + 120 * (a + 1)],
                   urow[:, a, P * j:P * (j + 1)])
            tr(ps[:, 3, (CT + 3) * j:(CT + 3) * (j + 1)], vrow[:, P * j:P * (j + 1)])
        tr(ps[:, 4, 0:KD + 2], nrow[:]).then_inc(*st["pre"][0]("hist"))

        PA1, AA1, DA1, LA1 = st["A1"]
        PA2, AA2, DA2, _ = st["A2"]

        def a1(t):
            pe.wait_ge(*DA1.at(t, "h"))
            if isinstance(t, int):
                pe.wait_ge(*st["pre"][1].at(0, "chistT"))
                pe.wait_ge(*st["pre"][2].at(0, "vec"))
            for k in range(KD):
                m = tr(ps[:, k // 4, P * (k % 4):P * (k % 4 + 1)], ht[:, P * k:P * (k + 1)])
            m.then_inc(*PA1("tr"))
            pe.wait_ge(*DA1.at(t, "hTt"))
            if isinstance(t, int):
                pe.wait_ge(s_wat, 16)
            else:
                pe.wait_ge(*AA2.at(t - 1, "at"))
            for f in range(2):
                for k in range(KD):
                    m = mm(ps[:, 2 + f, 0:NAT // 2], hTt[:, k], wat[:, k, f * (NAT // 2):(f + 1) * (NAT // 2)],
                           k == 0, k == KD - 1)
            m.then_inc(*PA1("proj"))

        def a2(t):
            pe.wait_ge(*DA2.at(t, "qk"))
            if not (isinstance(t, int) and t == 0):
                pe.wait_ge(*AA2.at(t - 1, "qT"))
            for j in range(4):
                tr(ps[:, 4, P * j:P * (j + 1)], qp[:, j].rearrange("p g d -> p (g d)"))
            tr(ps[:, 5, 0:P], at[:, 520:648]).then_inc(*PA2("qkT"))

        a1(0)
        with pe.Fori(1, NT) as t:
            a1(t)
            a2(t - 1)
        a2(NT - 1)
        end_phase(pe, 1)

        def proj(slot, half, chunks, free):
            for c, (c0, n) in enumerate(chunks):
                if free and c == 0:
                    pe.wait_ge(*free)
                for k in range(KD):
                    m = mm(ps[:, 3 * half + c, 0:n], wB[:, slot, k], hT[:, k, c0:c0 + n], k == 0, k == KD - 1)
            return m

        PB, AB, DB, LB = st["bq"]

        def bq(n, k):
            pe.wait_ge(s_w[k], 16 * (n // 4) + 16 if isinstance(n, int) else n * 4 + 16 - 4 * k)
            free = AB.at(n - 2, "ev") if not isinstance(n, int) or n >= 2 else None
            proj(k, k % 2, CHS, free).then_inc(*PB("proj"))

        for k in range(4):
            bq(k, k)
        with pe.Fori(1, 3) as i:
            for k in range(4):
                bq(i * 4 + k, k)
        PZ, AZ, _, _ = st["bz"]
        for k in range(4):
            pe.wait_ge(s_w[k], 64)
            proj(k, k % 2, CHP, AB.at(10 + k, "ev") if k < 2 else AZ.at(k - 2, "z")).then_inc(*PZ("proj"))
        PU, AU, DU, LU = st["bu"]
        for j in range(4):
            for g in range(2):
                k = 2 * (j % 2) + g
                pe.wait_ge(s_w[k], 80 + 16 * (j // 2))
                free = AZ.at(2 + g, "z") if j == 0 else (AU.at(j - 1, "sig"), DU.at(j - 1, "u"))[g]
                proj(k, g, CHS, free).then_inc(*PU(("gate", "value")[g]))
        PL, AL, DL, _ = st["ln"]
        pe.wait_ge(*DU.at(3, "conv"))
        for c, (c0, n) in enumerate(CHP):
            if c:
                pe.wait_ge(*AL.at(c - 1, "std"))
            for j in range(4):
                m = mm(ps[:, 6, 0:n], cc(C1), oc[:, j, c0:c0 + n], j == 0, j == 3)
            m.then_inc(*PL("mu"))
            pe.wait_ge(*AL.at(c, "sq"))
            for j in range(4):
                m = mm(ps[:, 7, 0:n], cc(C1), sqb[:, j, 0:n], j == 0, j == 3)
            m.then_inc(*PL("var"))
        PR, AR, DR, _ = st["rows"]
        pe.wait_ge(*LB.at(11, "tail"))
        for c in range(12):
            tr(ps[0:24, c // 4, P * (c % 4):P * (c % 4 + 1)], tailT[:, c, 0:24])
        for c in range(12):
            m = tr(ps[0:3, 3 + c // 4, P * (c % 4):P * (c % 4 + 1)], tailT[:, c, 24:27])
        m.then_inc(*PR("q"))
        pe.wait_ge(*LU.at(3, "tail"))
        pe.wait_ge(*AL.at(2, "std"))
        for j in range(4):
            m = tr(ps[0:S + CT - 1, 6, P * j:P * (j + 1)], utail[:, j])
        m.then_inc(*PR("u"))
        P2, A2, D2, _ = st["l2"]

        def l2(n):
            pe.wait_ge(*A2.at(n, "sq"))
            if isinstance(n, int) and n == 0:
                pe.wait_ge(*AR.at(0, "q"))
            for c, (c0, w) in enumerate(CHS):
                m = mm(ps[:, c, 0:w], cc(C1), uxt[:, c0:c0 + w])
            m.then_inc(*P2("ss"))

        l2(0)
        with pe.Fori(1, 2 * H) as n:
            l2(n)
        end_phase(pe, 2)

        PT_, AT_, DT_, LT_ = st["at"]

        def attend(t, n):
            first = isinstance(n, int)
            pe.wait_ge(*LT_.at(n, "q"))
            if not first:
                pe.wait_ge(*AT_.at(n - 1, "oT"))
            for h in range(HB):
                g, j = h // 4, h % 4
                r = slice(HD * g, HD * (g + 1))
                mm(ps[:, h // 2, 2 * P * (h % 2):2 * P * (h % 2 + 1)], qst[r, j, :],
                   kst[r, :])
                m = mm(ps[:, 4 + g, NM * j:NM * (j + 1)], qst[r, j, :], kT[r, S:S + NM])
            m.then_inc(*PT_("sc"))
            pe.wait_ge(*AT_.at(n, "exp"))
            for h in range(HB):
                m = tr(ps[0:NM, 6 + h // 4, P * (h % 4):P * (h % 4 + 1)], sc[:, h, 0:NM])
            m.then_inc(*PT_("trm"))
            for h in range(4):
                for b in range(2):
                    m = tr(ps[:, h // 2, 2 * P * (h % 2) + P * b:2 * P * (h % 2) + P * (b + 1)],
                           sc[:, h, NM + P * b:NM + P * (b + 1)])
            m.then_inc(*PT_("tra"))
            for h in range(4, 8):
                for b in range(2):
                    m = tr(ps[:, h // 2, 2 * P * (h % 2) + P * b:2 * P * (h % 2) + P * (b + 1)],
                           sc[:, h, NM + P * b:NM + P * (b + 1)])
            m.then_inc(*PT_("trb"))
            pe.wait_ge(*DT_.at(n, "PTm"))
            pe.wait_ge(*AT_.at(n, "PTa"))
            pe.wait_ge(*DT_.at(n, "PTb"))
            if first:
                pe.wait_ge(s_vm, 16)
            for h in range(HB):
                g = h // 4
                o = ps[:, 5, HD * h:HD * (h + 1)]
                mm(o, PTm[:, h, :], vm[:, HD * g:HD * (g + 1)], True, False)
                for b in range(2):
                    m = mm(o, PT[:, h, P * b:P * (b + 1)],
                           kv[:, ds(t - 1 + b, 1), P + HD * g:P + HD * (g + 1)].rearrange("p a d -> p (a d)"),
                           False, b == 1)
            m.then_inc(*PT_("pv"))
            pe.wait_ge(*DT_.at(n, "o"))
            for j in range(4):
                m = tr(ps[:, 4, P * j:P * (j + 1)], otok[:, 2 * j:2 * j + 2, :].rearrange("p h d -> p (h d)"))
            m.then_inc(*PT_("oT"))

        attend(1, 0)
        with pe.Fori(2, NT) as t:
            attend(t, t - 1)
        end_phase(pe, 3)

        PS, AS, DS, _ = st["sa"]
        pe.wait_ge(s_win, 16 * N_WIN)
        for b in range(NS):
            tr(ps[:, b // 4, P * (b % 4):P * (b % 4 + 1)], win[:, b, 0:P])
        tr(ps[:, 2, 0:P], mk[:]).then_inc(*PS("kT"))
        pe.wait_ge(*AS.at(0, "kT"))
        pe.wait_ge(*DS.at(0, "qs"))
        for b in range(NS):
            for g in range(KVH):
                r = slice(HD * g, HD * (g + 1))
                m0 = 32 * (2 * (b % 2) + g)
                c0 = (W + NM + TS) * (b // 2 % 3)
                m = mm(ps[m0:m0 + 32, 3 + 2 * g + b // 6, c0:c0 + W + NM + TS],
                       qs[r, b].rearrange("p j t -> p (j t)"), kTw[r, b, :])
        m.then_inc(*PS("sc"))
        pe.wait_ge(*AS.at(0, "exp"))
        for q in range(4):
            tr(ps[:, 0, P * q:P * (q + 1)], scs[:, q, 0:W])
            m = tr(ps[0:NM + TS, 1, P * q:P * (q + 1)], scs[:, q, W:W + NM + TS])
        m.then_inc(*PS("tr"))
        pe.wait_ge(*AS.at(0, "PT"))
        for b in range(NS):
            for g in range(KVH):
                m0 = 32 * (2 * (b % 2) + g)
                o = ps[m0:m0 + 32, 7, HD * (b // 2):HD * (b // 2 + 1)]
                mm(o, PTw[:, b // 2, m0:m0 + 32], win[:, b, P + HD * g:P + HD * (g + 1)], True, False)
                m = mm(o, PTn[:, b // 2, m0:m0 + 32], vmn[:, b, HD * g:HD * (g + 1)], False, True)
        m.then_inc(*PS("pv"))
        pe.wait_ge(*DS.at(0, "o"))
        for q in range(4):
            m = tr(ps[:, 2, P * q:P * (q + 1)], odup[:, q].rearrange("p a d -> p (a d)"))
        m.then_inc(*PS("oT"))
        end_phase(pe, 4)

        PG, AG, DG, LG = st["gd"]

        def heads(f):
            for h in range(H):
                m = f(h)
            return m

        def bank(b, h):
            return ps[:, b, P * h:P * (h + 1)]

        def delta(t):
            first = isinstance(t, int)
            v = 0 if first else 1
            if not first:
                pe.wait_ge(*DG.at(t - 1, "S"))
                pe.wait_ge(*AG.at(t - 1, "o"))
            pe.wait_ge(*LG.at(t, "stage"))
            heads(lambda h: mm(bank(0, h), gsm[:, 16 + h:17 + h].to_broadcast([P, P]), cc(CU + v * P)))
            g = gsm[:, 16:16 + H]
            mm(ps[:, 7, 0:H], cc(CU + v * P), g)
            mm(ps[:, 7, H:2 * H], cc(CSS + v * P), g).then_inc(*PG("G"))
            heads(lambda h: mm(bank(1, h), stg[:, H + h], stg[:, H + h]))
            heads(lambda h: mm(bank(2, h), stg[:, H + h], stg[:, h])).then_inc(*PG("kkpq"))
            heads(lambda h: tr(bank(3, h), stg[:, H + h]))
            heads(lambda h: tr(bank(4, h), stg[:, 2 * H + h])).then_inc(*PG("kv"))
            pe.wait_ge(*DG.at(t, "At"))
            heads(lambda h: tr(bank(5, h), G["AtT"][:, h])).then_inc(*PG("At"))
            pe.wait_ge(*DG.at(t, "D1"))
            heads(lambda h: tr(bank(6, h), G["Dm"][:, h])).then_inc(*PG("D1"))
            pe.wait_ge(*AG.at(t, "D1"))
            for l in range(1, 7):
                pe.wait_ge(*DG.at(t, f"B{l}"))
                if l > 1:
                    pe.wait_ge(*DG.at(t, f"X{l - 1}"))
                heads(lambda h: mm(bank(5, h), G[f"B{l % 2}"][:, h], G["Dt"][:, h])).then_inc(*PG(f"W{l}"))
                pe.wait_ge(*AG.at(t, f"W{l}"))
                if l < 6:
                    heads(lambda h: mm(bank(6, h), G["Wt"][:, h], G["Dm"][:, h]))
                heads(lambda h: mm(bank(7, h), G["Dm"][:, h], G["Wt"][:, h])).then_inc(*PG(f"X{l}"))
            pe.wait_ge(*DG.at(t, "X6"))
            heads(lambda h: mm(bank(4, h), G["kbg"][:, h], G["Dt"][:, h])).then_inc(*PG("u"))
            pe.wait_ge(*AG.at(t, "nw"))
            if first:
                pe.wait_ge(s_S0, 16)
                for h in range(H):
                    for b in range(NS):
                        m = mm(ps[:, 5, P * h + TS * b:P * h + TS * (b + 1)], S0[:, b, h],
                               G["nwT"][:, h, TS * b:TS * (b + 1)])
                m.then_inc(*PG("v2"))
            else:
                for h in range(H):
                    mm(bank(3, h), G["Dt"][:, h], G["vb"][:, h], True, False)
                    m = mm(bank(3, h), G["nwT"][:, h], St[:, h], False, True)
                m.then_inc(*PG("v2"))
            if first:
                pe.wait_ge(s_vnT, 1)
                for h in range(H):
                    mm(bank(3, h), G["Dt"][:, h], G["vb"][:, h], True, False)
                    m = mm(bank(3, h), G["Wt"][:, h], ident, False, True)
                m.then_inc(s_vnP, 1)
            pe.wait_ge(*DG.at(t, "vn"))
            for h in range(H):
                if first:
                    mm(bank(1, h), G["vnew"][:, h], G["PT2"][:, h], True, False)
                    for b in range(NS):
                        m = mm(ps[:, 1, P * h + TS * b:P * h + TS * (b + 1)], S0[:, b, h],
                               G["qdec"][:, h, TS * b:TS * (b + 1)], False, b == NS - 1)
                else:
                    mm(bank(1, h), G["vnew"][:, h], G["PT2"][:, h], True, False)
                    m = mm(bank(1, h), St[:, h], G["qdec"][:, h], False, True)
            m.then_inc(*PG("o"))
            if first:
                for h in range(H):
                    pe.wait_ge(s_vx, h + 1)
                    for f in range(2):
                        mm(ps[:, 4 + f, :], G["kdec"][:, h], vexp[:, 4 * f:4 * f + 4, :].rearrange("p s d -> p (s d)"))
                    m = mm(bank(6, 0), G["kdec"][:, h], vexp[:, NS, :])
                    if h < H - 1:
                        m.then_inc(s_dS0, 1)
                        pe.wait_ge(s_vx2, h + 1)
                m.then_inc(*PG("dS"))
            else:
                heads(lambda h: mm(bank(2, h), G["kdec"][:, h], G["vnew"][:, h])).then_inc(*PG("dS"))

        delta(0)
        with pe.Fori(1, NT) as t:
            delta(t)
        end_phase(pe, 5)

        PN, AN, DN, _ = st["gn"]
        with pe.Fori(0, H) as h:
            pe.wait_ge(*AN.at(h, "sq"))
            for c, (c0, n) in enumerate(((0, S), (S + NM, 512), (S + NM + 512, 512))):
                m = mm(ps[:, c, 0:n], cc(C1), gnt[:, c0:c0 + n])
            m.then_inc(*PN("ss"))
            pe.wait_ge(*AN.at(h, "std"))
        end_phase(pe, 6)

        PM, AM, DM, _ = st["mg"]

        def merge(n, k):
            for c, (c0, w) in enumerate(CHP):
                q = 3 * n + c
                for r, br in enumerate((oa, ob, oc)):
                    if not (isinstance(n, int) and n == 0 and c == 0):
                        pe.wait_ge(*AM.at(q - 1, f"s{r}"))
                    for a in range(KD):
                        m = mm(ps[:, 2 * r, 0:w], gw[:, k, r, a], hT[:, a, c0:c0 + w], a == 0, a == KD - 1)
                    m.then_inc(*PM(f"g{r}"))
                    if not (isinstance(n, int) and n == 0 and c == 0):
                        pe.wait_ge(*DM.at(q - 1, f"m{r}"))
                    for a in range(4):
                        m = mm(ps[:, 2 * r + 1, 0:w], bw[:, k, r, a], br[:, a, c0:c0 + w], a == 0, a == 3)
                    m.then_inc(*PM(f"b{r}"))

        for n in range(2):
            pe.wait_ge(s_gw[n], 96)
            merge(n, n)
        with pe.Fori(1, 4) as i:
            for k in range(2):
                pe.wait_ge(s_gw[k], 96 * i + 96)
                merge(2 * i + k, k)
        end_phase(pe, 7)

        PO, AO, DO, LO = st["op"]
        pe.wait_ge(s_wo, 48)

        def outproj(t):
            first = isinstance(t, int)
            rows = S if first else P
            pe.wait_ge(*LO.at(t, "stage"))
            for f in range(2):
                for k in range(KD):
                    m = mm(ps[0:rows, f, :], mst[:, k, 0:rows], wo[:, k, 512 * f:512 * (f + 1)], k == 0, k == KD - 1)
            m.then_inc(*PO("mix"))
            pe.wait_ge(*DO.at(t, "h"))
            for k in range(KD):
                m = tr(ps[:, 2 + k // 4, P * (k % 4):P * (k % 4) + rows], he[0:rows, k:D:KD])
            m.then_inc(*PO("tr"))
            pe.wait_ge(*DO.at(t, "hT"))
            for k in range(KD):
                m = mm(ps[0:rows, 4, 0:NG + E], h2t[:, k, 0:rows], wr[:, k], k == 0, k == KD - 1)
            m.then_inc(*PO("rt"))

        outproj(0)
        with pe.Fori(1, NT) as t:
            outproj(t)
        end_phase(pe, 8)

        PXC, _, DXC, _ = st["ch"]
        PY, _, DY, _ = st["dn"]

        def expert(e, k, w):
            first = isinstance(e, int) and e == 0
            pe.wait_ge(s_ew[k], w)
            for ft in range(2):
                for c, (c0, n) in enumerate(CHP):
                    q = (e * 2 + ft) * 3 + c
                    b = (3 * ft + c) % 2
                    if not (first and ft == 0 and c < 2):
                        pe.wait_ge(*DXC.at(q - 2, "h"))
                    for m_ in range(2):
                        for a in range(KD):
                            m = mm(ps[:, 2 * b + m_, 0:n],
                                   ew[k][:, m_, F * a + P * ft:F * a + P * (ft + 1)], h2[:, a, c0:c0 + n],
                                   a == 0, a == KD - 1)
                    m.then_inc(*PXC("c"))
            pe.wait_ge(*DXC.at(e * 6 + 5, "h"))
            for t in range(NT):
                rows = S if t == 0 else P
                for f in range(2):
                    q = (e * NT + t) * 2 + f
                    if not (first and t < 2):
                        pe.wait_ge(*DY.at(q - (2 if t == 0 else 4), "acc"))
                    for a in range(2):
                        m = mm(ps[0:rows, 4 + 2 * (t % 2) + f, :], hid[:, a, 0:S] if t == 0 else hid[:, a, tile_cols(t)],
                               ew[k][:, 2, D * a + 512 * f:D * a + 512 * (f + 1)], a == 0, a == 1)
                    m.then_inc(*PY("y"))

        for k in range(2):
            expert(k, k, 48)
        with pe.Fori(1, E // 2) as i:
            for k in range(2):
                expert(2 * i + k, k, 48 * i + 48)
        end_phase(pe, 9)

    @block.scalar
    def _(act):
        def f(out, in_, fn, **kw):
            return act.activation(out, in_, fn, **kw)

        e1, e128 = eps[:, 0:1], eps[:, 1:2]
        act.wait_ge(*st["pre"][0].at(0, "hist"))
        f(histT[:].rearrange("p c n -> p (c n)"), ps[:, 0, 0:12 * NHR], ACT.Copy).then_inc(*st["pre"][1]("histT"))
        f(chistT[:, 0:2].rearrange("p c n -> p (c n)"), ps[:, 1, 0:480], ACT.Copy)
        f(chistT[:, 2:4].rearrange("p c n -> p (c n)"), ps[:, 2, 0:480], ACT.Copy).then_inc(*st["pre"][1]("chistT"))

        PA1, AA1, DA1, _ = st["A1"]
        PA2, AA2, DA2, _ = st["A2"]
        act.wait_ge(s_init, 2)

        def a1(t):
            if isinstance(t, int):
                act.wait_ge(s_x0, 32)
            else:
                act.wait_ge(s_x, t * 16)
                act.wait_ge(*DA1.at(t - 1, "rs"))
            f(sqj[:], xt[:], ACT.Square, accum_out=st1[:, 0:1]).then_inc(*AA1("sq"))
            act.drain()
            f(st1[:, 1:2], st1[:, 0:1], ACT.Sqrt, scale=1.0 / D, bias=e1).then_inc(*AA1("std"))

        def a2(t):
            act.wait_ge(*PA1.at(t, "proj"))
            if not (isinstance(t, int) and t == 0):
                act.wait_ge(*DA2.at(t - 1, "keep"))
                act.wait_ge(*PA2.at(t - 1, "qkT"))
            f(at[:, 0:NAT // 2], ps[:, 2, 0:NAT // 2], ACT.Copy)
            f(at[:, NAT // 2:NAT], ps[:, 3, 0:NAT // 2], ACT.Copy).then_inc(*AA2("at"))
            act.drain()
            f(sq2[:], at[:, 8:8 + NQK], ACT.Square).then_inc(*AA2("sq2"))
            act.wait_ge(*DA2.at(t, "ssq"))
            f(st2[:, 10:20], st2[:, 0:10], ACT.Sqrt, scale=1.0 / HD, bias=e1).then_inc(*AA2("std2"))
            act.wait_ge(*PA2.at(t, "qkT"))
            f(qT[:, :, ds(P * t, P)], ps[:, 4, :].rearrange("p (j n) -> p j n", j=4), ACT.Copy, scale=qw[:])
            f(kT[:, ds(P * t, P)], ps[:, 5, 0:P], ACT.Copy).then_inc(*AA2("qT"))

        a1(0)
        with act.Fori(1, NT) as t:
            a1(t)
            a2(t - 1)
        a2(NT - 1)
        _, AGB, DGB, _ = st["gb"]
        act.wait_ge(*DGB.at(0, "x"))
        f(tmq36[:], tmq36[:], ACT.Exp, scale=-1.0)
        act.drain()
        f(tmq36[:], tmq36[:], ACT.Ln, bias=1.0).then_inc(*AGB("lse"))
        f(alog[:], alog[:], ACT.Exp)
        f(ab[:, :, H:2 * H], ab[:, :, H:2 * H], ACT.Sigmoid).then_inc(*AGB("sig"))
        end_phase(act, 1)

        PB, AB, DB, LB = st["bq"]
        exP = lambda p: ext[:, p, EXS:]
        exS = lambda p: ext[:, p, 0:EXS].rearrange("p (b n) -> p b n", b=NS)

        def bq(n, k):
            p, q = k % 2, 3 * (k % 2)
            early = isinstance(n, int) and n < 2
            act.wait_ge(*PB.at(n, "proj"))
            if not early:
                act.wait_ge(*DB.at(n - 2, "conv"))
                act.wait_ge(*LB.at(n - 2, "tail"))
            o = CONV - 1 + NM
            f(exS(p)[:, :, CONV - 1:], ps[:, q, 0:S].rearrange("p (b n) -> p b n", b=NS), ACT.Copy)
            f(exP(p)[:, o:o + CH - S], ps[:, q, S:CH], ACT.Copy)
            f(exP(p)[:, o + CH - S:o + 2 * CH - S], ps[:, q + 1, 0:CH], ACT.Copy)
            f(exP(p)[:, o + 2 * CH - S:o + SEQ], ps[:, q + 2, 0:CH - NM], ACT.Copy)
            f(exP(p)[:, CONV - 1:o], ps[:, q + 2, CH - NM:CH], ACT.Copy).then_inc(*AB("ev"))

        def silu(n):
            act.wait_ge(*DB.at(n, "conv"))
            f(qkv[:, ds(n, 1), :], qkv[:, ds(n, 1), :], ACT.Silu).then_inc(*AB("silu"))

        for k in range(4):
            bq(k, k)
            silu(k)
        with act.Fori(1, 3) as i:
            for k in range(4):
                bq(i * 4 + k, k)
                silu(i * 4 + k)
        PZ, AZ, _, _ = st["bz"]
        for k in range(4):
            act.wait_ge(*PZ.at(k, "proj"))
            for c, (c0, n) in enumerate(CHP):
                m = f(z[:, k, c0:c0 + n], ps[:, 3 * (k % 2) + c, 0:n], ACT.Silu)
            m.then_inc(*AZ("z"))
        PU, AU, DU, LU = st["bu"]
        for j in range(4):
            act.wait_ge(*PU.at(j, "gate"))
            if j:
                act.wait_ge(*DU.at(j - 1, "u"))
            for c, (c0, n) in enumerate(CHS):
                m = f(sig[:, c0:c0 + n], ps[:, c, 0:n], ACT.Sigmoid)
            m.then_inc(*AU("sig"))
        PL, AL, DL, _ = st["ln"]
        for c, (c0, n) in enumerate(CHP):
            act.wait_ge(*DL.at(c, "cent"))
            f(sqb[:, :, 0:n], oc[:, :, c0:c0 + n], ACT.Square).then_inc(*AL("sq"))
            act.wait_ge(*PL.at(c, "var"))
            f(rsb[:, 0, 0:n], ps[:, 7, 0:n], ACT.Sqrt, scale=1.0 / CC, bias=e1).then_inc(*AL("std"))
            act.wait_ge(*DL.at(c, "norm"))
            for j in range(4):
                m = f(oc[:, j, c0:c0 + n], oc[:, j, c0:c0 + n], ACT.Silu, scale=dvec[:, j, CT + 1:CT + 2],
                      bias=dvec[:, j, CT + 2:CT + 3])
            m.then_inc(*AL("silu"))
        PR, AR, DR, _ = st["rows"]
        act.wait_ge(*PR.at(0, "q"))
        f(hq[:, 0, :], ps[0:24, 0:3, :].rearrange("p b n -> p (b n)"), ACT.Copy)
        f(hq[0:3, 1, :], ps[0:3, 3:6, :].rearrange("p b n -> p (b n)"), ACT.Copy).then_inc(*AR("q"))
        P2, A2, D2, _ = st["l2"]

        def l2(n, scale, bias):
            f(uxt[:, 0:ALL], qkv[:, ds(n, 1), :].rearrange("p a n -> p (a n)"), ACT.Square).then_inc(*A2("sq"))
            act.wait_ge(*P2.at(n, "ss"))
            if not (isinstance(n, int) and n == 0):
                act.wait_ge(*D2.at(n - 1, "norm"))
            for c, (c0, w) in enumerate(CHS):
                m = f(sig[:, c0:c0 + w], ps[:, c, 0:w], ACT.Sqrt, scale=scale, bias=bias)
            m.then_inc(*A2("std"))

        act.wait_ge(*LU.at(3, "tail"))
        act.wait_ge(*DU.at(3, "conv"))
        act.drain()
        l2(0, float(DK), e128)
        with act.Fori(1, H) as n:
            l2(n, float(DK), e128)
        with act.Fori(H, 2 * H) as n:
            l2(n, 1.0, e1)
        end_phase(act, 2)

        PT_, AT_, DT_, LT_ = st["at"]

        def attend(t, n):
            act.wait_ge(*DT_.at(n, "max"))
            for h in range(HB):
                f(sc[:, h, :], sc[:, h, :], ACT.Exp, bias=st2[:, 8 + h:9 + h], accum_out=st2[:, 16 + h:17 + h])
            f(st2[:, 24:32], st2[:, 24:32], ACT.Exp).then_inc(*AT_("exp"))
            act.wait_ge(*PT_.at(n, "tra"))
            f(PT[:, 0:4].rearrange("p h n -> p (h n)"), ps[:, 0:2, :].rearrange("p b n -> p (b n)"),
              ACT.Copy).then_inc(*AT_("PTa"))
            act.wait_ge(*PT_.at(n, "oT"))
            if isinstance(n, int):
                act.wait_ge(s_hq, 1)
            f(ob[:, :, tile_cols(t)], ps[:, 4, :].rearrange("p (j n) -> p j n", j=4), ACT.Copy)\
                .then_inc(*AT_("oT"))

        attend(1, 0)
        with act.Fori(2, NT) as t:
            attend(t, t - 1)
        end_phase(act, 3)

        PS, AS, DS, _ = st["sa"]
        act.wait_ge(*PS.at(0, "kT"))
        f(kTw[:, :, 0:W], ps[:, 0:2, :].rearrange("p c (b n) -> p (c b) n", b=4), ACT.Copy)
        f(kTw[:, :, W:W + NM], ps[:, 2, 0:P].rearrange("p (b n) -> p b n", b=NS), ACT.Copy)
        f(kTw[:, :, W + NM:], kT[:, 0:S].rearrange("p (b n) -> p b n", b=NS), ACT.Copy).then_inc(*AS("kT"))
        act.wait_ge(*DS.at(0, "max"))
        for q in range(4):
            f(scs[:, q], scs[:, q], ACT.Exp, bias=st2[:, 4 + q:5 + q], accum_out=st2[:, 8 + q:9 + q])
        f(st2[:, 12:16], st2[:, 12:16], ACT.Exp).then_inc(*AS("exp"))
        act.wait_ge(*PS.at(0, "tr"))
        f(PTw[:].rearrange("p q n -> p (q n)"), ps[:, 0, :], ACT.Copy)
        f(PTn[:].rearrange("p q n -> p (q n)"), ps[0:NM + TS, 1, :], ACT.Copy).then_inc(*AS("PT"))
        end_phase(act, 4)

        PG, AG, DG, LG = st["gd"]

        def flat(x):
            return x.rearrange("p h n -> p (h n)")

        def delta(t):
            first = isinstance(t, int)
            act.wait_ge(*PG.at(t, "G"))
            if not first:
                act.wait_ge(*DG.at(t - 1, "S"))
            f(flat(G["eG"][:]), ps[:, 0, :], ACT.Exp)
            act.wait_ge(*DG.at(t, "cols"))
            f(gsm[:, 8:8 + H], gsm[:, 0:H], ACT.Exp).then_inc(*AG("eG"))
            act.wait_ge(*DG.at(t, "arg"))
            f(flat(G["dec"][:]), flat(G["dec"][:]), ACT.Exp)
            f(gsm[:, 12:12 + H], gsm[:, 12:12 + H], ACT.Exp).then_inc(*AG("dec"))
            act.wait_ge(*PG.at(t, "D1"))
            f(flat(G["Dt"][:]), ps[:, 6, :], ACT.Copy).then_inc(*AG("D1"))
            for l in range(1, 7):
                act.wait_ge(*PG.at(t, f"W{l}"))
                f(flat(G["Wt"][:]), ps[:, 5, :], ACT.Copy).then_inc(*AG(f"W{l}"))
            act.wait_ge(*PG.at(t, "u"))
            f(flat(G["nwT"][:]), ps[:, 4, :], ACT.Copy, scale=-1.0).then_inc(*AG("nw"))
            if first:
                act.wait_ge(*PG.at(t, "v2"))
                act.wait_ge(s_init, 3)
                f(G["Wt"][:, :, 0:S], ps[:, 5, :].rearrange("p (h n) -> p h n", h=H)[:, :, 0:S], ACT.Copy)\
                    .then_inc(s_vnT, 1)
            act.wait_ge(*PG.at(t, "o"))
            n = S + NM if first else P
            cols = slice(0, n) if first else bass.ds(S + NM + P * (t - 1), P)
            f(qkv[:, 0:H, cols], ps[:, 1, :].rearrange("p (h n) -> p h n", h=H)[:, :, 0:n], ACT.Copy)\
                .then_inc(*AG("o"))

        delta(0)
        with act.Fori(1, NT) as t:
            delta(t)
        end_phase(act, 5)

        PN, AN, DN, _ = st["gn"]

        def gnorm(h):
            f(gnt[:], qkv[:, ds(h, 1), :].rearrange("p a n -> p (a n)"), ACT.Square).then_inc(*AN("sq"))
            act.wait_ge(*PN.at(h, "ss"))
            if not isinstance(h, int):
                act.wait_ge(*DN.at(h - 1, "b"))
            for c, (c0, n) in enumerate(((0, S), (S, 512), (S + 512, 512))):
                m = f(gstd[:, c0:c0 + n], ps[:, c, 0:n], ACT.Sqrt, scale=1.0 / DK, bias=e1)
            m.then_inc(*AN("std"))

        gnorm(0)
        with act.Fori(1, H) as h:
            gnorm(h)
        end_phase(act, 6)

        PM, AM, DM, _ = st["mg"]

        def merge(n):
            for c, (c0, w) in enumerate(CHP):
                q = 3 * n + c
                for r in range(3):
                    act.wait_ge(*PM.at(q, f"g{r}"))
                    if r < 2:
                        if not (isinstance(n, int) and n == 0 and c == 0):
                            act.wait_ge(*DM.at(q - 1, "m2" if r == 0 else "m1"))
                    else:
                        act.wait_ge(*DM.at(q, "m0"))
                    f(gs[:, r % 2, 0:w], ps[:, 2 * r, 0:w], ACT.Sigmoid).then_inc(*AM(f"s{r}"))

        merge(0)
        with act.Fori(1, KD) as n:
            merge(n)
        end_phase(act, 7)

        PO, AO, DO, _ = st["op"]

        def outproj(t):
            rows = S if isinstance(t, int) else P
            act.wait_ge(*DO.at(t, "x2"))
            f(he[0:rows, :], x2[0:rows, ds(t, 1), :].rearrange("p a n -> p (a n)"), ACT.Square,
              accum_out=st1[0:rows, 0:1]).then_inc(*AO("sq"))
            act.drain()
            f(st1[0:rows, 1:2], st1[0:rows, 0:1], ACT.Sqrt, scale=1.0 / D, bias=eps[0:rows, 0:1]).then_inc(*AO("std"))

        outproj(0)
        with act.Fori(1, NT) as t:
            outproj(t)
        _, AR_, DR_, _ = st["rt"]
        act.wait_ge(*DR_.at(0, "gm"))
        f(ra[:, :, 0:NG], ra[:, :, 0:NG], ACT.Exp).then_inc(*AR_("eg"))
        act.wait_ge(*DR_.at(0, "em"))
        f(r1[:, 4], r1[:, 4], ACT.Exp).then_inc(*AR_("es"))
        end_phase(act, 8)

        PXC, AXC, DXC, _ = st["ch"]

        def expert(e):
            for ft in range(2):
                for c, (c0, n) in enumerate(CHP):
                    q = (e * 2 + ft) * 3 + c
                    b = (3 * ft + c) % 2
                    act.wait_ge(*PXC.at(q, "c"))
                    if not (isinstance(e, int) and e == 0 and ft == 0 and c < 2):
                        act.wait_ge(*DXC.at(q - 2, "h"))
                    f(sg[:, b, 0:n], ps[:, 2 * b, 0:n], ACT.Silu).then_inc(*AXC("s"))

        expert(0)
        with act.Fori(1, E) as e:
            expert(e)
        end_phase(act, 9)

    @block.vector
    def _(ve):
        def tt(out, a, b, op):
            return ve.tensor_tensor(out, a, b, op)

        def ts(out, a, s1, op0, s2=None, op1=ALU.bypass):
            return ve.tensor_scalar(out, a, s1, s2, op0, op1)

        def stt(out, a, s, b, op0, op1):
            return ve.scalar_tensor_tensor(out=out, in0=a, scalar=s, in1=b, op0=op0, op1=op1)

        ve.memset(xt[:], 0.0).then_inc(s_init, 1)
        ve.memset(eps[:, 0:1], EPS)
        ve.memset(eps[:, 1:2], EPS * DK).then_inc(s_init, 1)
        ve.wait_ge(*st["pre"][0].at(0, "hist"))
        ve.tensor_copy(dvec[:].rearrange("p j n -> p (j n)"), ps[:, 3, 0:4 * (CT + 3)])
        ve.tensor_copy(nvec[:], ps[:, 4, 0:KD + 2])
        ve.drain()
        ts(qw[:], nvec[:, KD + 1:KD + 2], HD ** -0.5, ALU.mult)
        tt(st2[:, 0:HB], cst[:, CR:CR + HB], sink[:], ALU.mult)
        ve.drain()
        ve.tensor_reduce(sinkr[:], st2[:, 0:HB], AX.X, ALU.add)
        ve.drain().then_inc(*st["pre"][2]("vec"))

        PA1, AA1, DA1, LA1 = st["A1"]
        PA2, AA2, DA2, _ = st["A2"]

        def a1(t):
            ve.wait_ge(*AA1.at(t, "std"))
            ve.reciprocal(st1[:, 2:3], st1[:, 1:2]).then_inc(*DA1("rs"))
            ve.drain()
            ts(ht[:], xt[:], st1[:, 2:3], ALU.mult).then_inc(*DA1("h"))
            ve.wait_ge(*PA1.at(t, "tr"))
            if not isinstance(t, int):
                ve.wait_ge(*PA1.at(t - 1, "proj"))
                ve.wait_ge(*LA1.at(t - 1, "hT"))
            for f in range(2):
                m = tt(hTt[:, 4 * f:4 * f + 4], ps[:, f, :].rearrange("p (k n) -> p k n", k=4),
                       b3(nvec[:, 4 * f:4 * f + 4], P), ALU.mult)
            m.then_inc(*DA1("hTt"))

        def a2(t):
            ve.wait_ge(*AA2.at(t, "sq2"))
            ve.tensor_reduce(st2[:, 0:10], sq2[:].rearrange("p (h d) -> p h d", d=HD), AX.X, ALU.add)\
                .then_inc(*DA2("ssq"))
            ve.wait_ge(*AA2.at(t, "std2"))
            ve.reciprocal(st2[:, 20:30], st2[:, 10:20]).then_inc(*DA2("rs2"))
            ve.drain()
            if not (isinstance(t, int) and t == 0):
                ve.wait_ge(*PA2.at(t - 1, "qkT"))
            rs = st2[:, 20:28].rearrange("p (g j) -> p g j", g=2).unsqueeze(3).to_broadcast([P, 2, 4, HD])
            tt(qp[:].rearrange("p j g d -> p g j d"),
               at[:, 8:520].rearrange("p (g j d) -> p g j d", g=2, j=4), rs, ALU.mult)
            kk = at[:, 520:648].rearrange("p (h d) -> p h d", d=HD)
            tt(kk, kk, b3(st2[:, 28:30], HD), ALU.mult)
            ve.drain()
            tt(kk, kk, b2(kw[:], KVH), ALU.mult).then_inc(*DA2("qk"))
            ve.drain()
            ve.tensor_copy(kv[:, ds(t, 1), :].rearrange("p a n -> p (a n)"), at[:, 520:NAT])
            ve.tensor_copy(ab[:, ds(t, 1), :].rearrange("p a n -> p (a n)"), at[:, 0:8]).then_inc(*DA2("keep"))

        a1(0)
        with ve.Fori(1, NT) as t:
            a1(t)
            a2(t - 1)
        a2(NT - 1)
        _, AGB, DGB, _ = st["gb"]
        ve.drain()
        tt(tmp36[:], ab[:, :, 0:H], b2(dtb[:], NT), ALU.add)
        ve.drain()
        ts(tmq36[:], tmp36[:], -1.0, ALU.mult)
        ve.drain()
        tt(tmq36[:], tmq36[:], tmp36[:], ALU.max).then_inc(*DGB("x"))
        ts(tmp36[:], tmp36[:], 0.0, ALU.max).then_inc(*DGB("m"))
        ve.drain()
        ve.wait_ge(*AGB.at(0, "lse"))
        tt(tmp36[:], tmp36[:], tmq36[:], ALU.add)
        ve.drain()
        ve.wait_ge(*AGB.at(0, "sig"))
        stt(ab[:, :, 0:H], tmp36[:], -1.0, b2(alog[:], NT), ALU.mult, ALU.mult).then_inc(*DGB("g"))
        end_phase(ve, 1)

        PB, AB, DB, LB = st["bq"]

        def bq(n, k):
            p = k % 2
            ve.wait_ge(*AB.at(n, "ev"))
            ve.wait_ge(*LB.at(n, "hist"))
            es = ext[:, p, 0:EXS].rearrange("p (b n) -> p b n", b=NS)
            outs = qkv[:, ds(n, 1), 0:S].rearrange("p a (b n) -> p (a b) n", b=NS)
            outp = qkv[:, ds(n, 1), S:ALL].rearrange("p a n -> p (a n)")
            for j in range(CONV):
                w = histT[:, ds(n, 1), NHR - CONV + j:NHR - CONV + j + 1].rearrange("p a b -> p (a b)")
                i_s, ip = es[:, :, j:j + TS], ext[:, p, EXS + j:EXS + j + NM + SEQ]
                if j == 0:
                    ts(outs, i_s, w, ALU.mult)
                    m = ts(outp, ip, w, ALU.mult)
                else:
                    ve.drain()
                    stt(outs, i_s, w, outs, ALU.mult, ALU.add)
                    m = stt(outp, ip, w, outp, ALU.mult, ALU.add)
            m.then_inc(*DB("conv"))

        for k in range(4):
            bq(k, k)
        with ve.Fori(1, 3) as i:
            for k in range(4):
                bq(i * 4 + k, k)
        PU, AU, DU, LU = st["bu"]
        us = uxt[:, 0:UXS].rearrange("p (b n) -> p b n", b=NS)
        for j in range(4):
            ve.wait_ge(*AU.at(j, "sig"))
            ve.wait_ge(*PU.at(j, "value"))
            if j:
                ve.wait_ge(*LU.at(j - 1, "tail"))
                ve.drain()
            o = UXS + CT - 1 + NM
            tt(us[:, :, CT - 1:], ps[:, 3, 0:S].rearrange("p (b n) -> p b n", b=NS),
               sig[:, 0:S].rearrange("p (b n) -> p b n", b=NS), ALU.mult)
            tt(uxt[:, o:o + CH - S], ps[:, 3, S:CH], sig[:, S:CH], ALU.mult)
            tt(uxt[:, o + CH - S:o + 2 * CH - S], ps[:, 4, 0:CH], sig[:, CH:2 * CH], ALU.mult)
            tt(uxt[:, o + 2 * CH - S:o + SEQ], ps[:, 5, 0:CH - NM], sig[:, 2 * CH:TOK], ALU.mult)
            tt(uxt[:, o - NM:o], ps[:, 5, CH - NM:CH], sig[:, TOK:ALL], ALU.mult).then_inc(*DU("u"))
            ve.wait_ge(*LU.at(j, "hist"))
            ve.drain()
            outs = oc[:, j, 0:S].rearrange("p (b n) -> p b n", b=NS)
            outp = oc[:, j, S:TOK]
            for k in range(CT):
                i_s, ip, w = us[:, :, k:k + TS], uxt[:, UXS + NM + k:UXS + NM + k + SEQ], dvec[:, j, k:k + 1]
                if k == 0:
                    bias = dvec[:, j, CT:CT + 1]
                    ts(outs, i_s, w, ALU.mult, bias, ALU.add)
                    m = ts(outp, ip, w, ALU.mult, bias, ALU.add)
                else:
                    ve.drain()
                    stt(outs, i_s, w, outs, ALU.mult, ALU.add)
                    m = stt(outp, ip, w, outp, ALU.mult, ALU.add)
            m.then_inc(*DU("conv"))
        ve.drain()
        PL, AL, DL, _ = st["ln"]
        for c, (c0, n) in enumerate(CHP):
            ve.wait_ge(*PL.at(c, "mu"))
            for j in range(4):
                o = oc[:, j, c0:c0 + n]
                m = stt(o, ps[:, 6, 0:n], -1.0 / CC, o, ALU.mult, ALU.add)
            m.then_inc(*DL("cent"))
            ve.drain()
            ve.wait_ge(*AL.at(c, "std"))
            ve.reciprocal(rsb[:, 1, 0:n], rsb[:, 0, 0:n]).then_inc(*DL("rs"))
            ve.drain()
            tt(oc[:, :, c0:c0 + n], oc[:, :, c0:c0 + n], b2(rsb[:, 1, 0:n], 4), ALU.mult).then_inc(*DL("norm"))
        PR, AR, DR, _ = st["rows"]
        ve.wait_ge(*PR.at(0, "u"))
        ve.tensor_copy(hu[:], ps[0:S + CT - 1, 6, :]).then_inc(*DR("u"))
        P2, A2, D2, _ = st["l2"]
        with ve.Fori(0, 2 * H) as n:
            ve.wait_ge(*A2.at(n, "std"))
            ve.reciprocal(sig[:], sig[:])
            ve.drain()
            q = qkv[:, ds(n, 1), :].rearrange("p a n -> p (a n)")
            tt(q, q, sig[:], ALU.mult).then_inc(*D2("norm"))
        end_phase(ve, 2)

        PT_, AT_, DT_, LT_ = st["at"]

        def attend(t, n):
            ve.wait_ge(*PT_.at(n, "sc"))
            for b in range(4):
                o = sc[:, 2 * b:2 * b + 2, NM:]
                i = ps[:, b, :].rearrange("p (h n) -> p h n", h=2)
                if isinstance(n, int):
                    ve.memset(o[:, :, 0:P], NEG)
                    tt(o[:, :, P:], i[:, :, P:], b2(cst[:, CB + P:CB + 2 * P], 2), ALU.add)
                else:
                    tt(o, i, b2(cst[:, CB:CB + 2 * P], 2), ALU.add)
            for g in range(KVH):
                m = ve.tensor_copy(sc[:, 4 * g:4 * g + 4, 0:NM],
                                   ps[:, 4 + g, 0:4 * NM].rearrange("p (h n) -> p h n", h=4))
            m.then_inc(*DT_("sc"))
            ve.drain()
            ve.tensor_reduce(st2[:, 0:8], sc[:], AX.X, ALU.max)
            ve.drain()
            tt(st2[:, 0:8], st2[:, 0:8], sink[:], ALU.max)
            ve.drain()
            ts(st2[:, 8:16], st2[:, 0:8], -1.0, ALU.mult)
            tt(st2[:, 24:32], sink[:], st2[:, 0:8], ALU.subtract).then_inc(*DT_("max"))
            ve.wait_ge(*AT_.at(n, "exp"))
            tt(st2[:, 32:40], st2[:, 16:24], st2[:, 24:32], ALU.add)
            ve.drain()
            ve.reciprocal(st2[:, 40:48], st2[:, 32:40]).then_inc(*DT_("den"))
            ve.wait_ge(*PT_.at(n, "trm"))
            ve.tensor_copy(PTm[:].rearrange("p h n -> p (h n)"), ps[0:NM, 6:8, :].rearrange("p b n -> p (b n)"))\
                .then_inc(*DT_("PTm"))
            ve.wait_ge(*PT_.at(n, "trb"))
            ve.tensor_copy(PT[:, 4:8].rearrange("p h n -> p (h n)"), ps[:, 2:4, :].rearrange("p b n -> p (b n)"))\
                .then_inc(*DT_("PTb"))
            ve.drain()
            ve.wait_ge(*PT_.at(n, "pv"))
            tt(otok[:], ps[:, 5, :].rearrange("p (h d) -> p h d", h=HB), b3(st2[:, 40:48], HD), ALU.mult)\
                .then_inc(*DT_("o"))

        attend(1, 0)
        with ve.Fori(2, NT) as t:
            attend(t, t - 1)
        end_phase(ve, 3)

        PS, AS, DS, _ = st["sa"]
        for j in range(4):
            m = ve.tensor_copy(qs[:, :, j, :], qT[:, j, 0:S].rearrange("p (b t) -> p b t", b=NS))
        m.then_inc(*DS("qs"))
        ve.wait_ge(*PS.at(0, "sc"))
        for r in range(4):
            rows, g, n = slice(32 * r, 32 * r + 32), r % 2, W + NM + TS
            tt(scs[rows, 0:3], ps[rows, 3 + 2 * g, 0:3 * n].rearrange("p (q n) -> p q n", q=3),
               b2(cst[rows, CM:CR], 3), ALU.add)
            m = tt(scs[rows, 3], ps[rows, 4 + 2 * g, 0:n], cst[rows, CM:CR], ALU.add)
        m.then_inc(*DS("sc"))
        ve.drain()
        ve.tensor_reduce(st2[:, 0:4], scs[:], AX.X, ALU.max)
        ve.drain()
        ts(st2[:, 4:8], st2[:, 0:4], sinkr[:], ALU.max, -1.0, ALU.mult)
        ve.drain()
        ts(st2[:, 12:16], st2[:, 4:8], sinkr[:], ALU.add).then_inc(*DS("max"))
        ve.wait_ge(*AS.at(0, "exp"))
        tt(st2[:, 16:20], st2[:, 8:12], st2[:, 12:16], ALU.add)
        ve.drain()
        ve.reciprocal(st2[:, 20:24], st2[:, 16:20]).then_inc(*DS("den"))
        ve.drain()
        ve.wait_ge(*PS.at(0, "pv"))
        for a in range(2):
            m = tt(odup[:, :, a, :], ps[:, 7, 0:4 * HD].rearrange("p (q d) -> p q d", q=4), b3(st2[:, 20:24], HD),
                   ALU.mult)
        m.then_inc(*DS("o"))
        ve.wait_ge(*PS.at(0, "oT"))
        oT = ps[:, 2, :].rearrange("p (s g h t) -> p s g h t", g=2, h=4, t=TS)
        for g in range(KVH):
            for h in range(4):
                half = slice(HD * (h % 2), HD * (h % 2 + 1))
                m = ve.tensor_copy(ob[half, 2 * g + h // 2, 0:S].rearrange("p (s t) -> p s t", t=TS),
                                   oT[half, :, g, h, :])
        m.then_inc(*DS("oT"))
        end_phase(ve, 4)

        PG, AG, DG, LG = st["gd"]

        def flat(x):
            return x.rearrange("p h n -> p (h n)")

        def hb(b):
            return ps[:, b, :].rearrange("p (h n) -> p h n", h=H)

        beta = gsm[:, 20:24]

        def delta(t):
            first = isinstance(t, int)
            v = 0 if first else 1
            ve.wait_ge(*PG.at(t, "G"))
            ve.wait_ge(*LG.at(t, "stage"))
            ve.tensor_copy(gsm[:, 0:8], ps[:, 7, 0:8]).then_inc(*DG("cols"))
            ve.drain()
            ve.wait_ge(*AG.at(t, "eG"))
            for h in range(H):
                stt(G["dec"][:, h], ps[:, 0, P * h:P * (h + 1)], gsm[:, h:h + 1], cc(CN + v * P),
                    ALU.subtract, ALU.add)
            tt(gsm[:, 12:16], gsm[:, 4:8], gsm[:, 0:4], ALU.subtract).then_inc(*DG("arg"))
            ve.wait_ge(*AG.at(t, "dec"))
            ve.wait_ge(*PG.at(t, "kkpq"))
            tt(G["AtT"][:], hb(1), G["dec"][:], ALU.mult)
            ve.drain()
            tt(G["AtT"][:], G["AtT"][:], b2(cc(CS + v * P), H), ALU.mult).then_inc(*DG("At"))
            tt(G["PT2"][:], hb(2), G["dec"][:], ALU.mult).then_inc(*DG("PT2"))
            ve.wait_ge(*PG.at(t, "kv"))
            tt(G["vb"][:], hb(4), b3(beta, P), ALU.mult)
            tt(gsm[:, 24:28], beta, gsm[:, 8:12], ALU.mult)
            ve.drain()
            tt(G["kbg"][:], hb(3), b3(gsm[:, 24:28], P), ALU.mult)
            tt(G["kdec"][:], hb(3), b3(gsm[:, 12:16], P), ALU.mult)
            tt(G["qdec"][:], stg[:, 0:H], G["eG"][:], ALU.mult).then_inc(*DG("kq"))
            ve.wait_ge(*PG.at(t, "At"))
            tt(G["Am"][:], hb(5), b3(beta, P), ALU.mult).then_inc(*DG("A"))
            ve.drain()
            tt(G["B0"][:], G["Am"][:], b2(cc(CL), H), ALU.mult)
            ve.drain()
            tt(G["Dm"][:], b2(ident, H), G["B0"][:], ALU.subtract).then_inc(*DG("D1"))
            tt(G["B1"][:], G["Am"][:], b2(cc(CL + P), H), ALU.mult).then_inc(*DG("B1"))
            for l in range(1, 7):
                if l < 6:
                    ve.drain()
                    tt(G[f"B{(l + 1) % 2}"][:], G["Am"][:], b2(cc(CL + (l + 1) * P), H), ALU.mult)\
                        .then_inc(*DG(f"B{l + 1}"))
                ve.drain()
                ve.wait_ge(*PG.at(t, f"X{l}"))
                if l < 6:
                    tt(flat(G["Dm"][:]), flat(G["Dm"][:]), ps[:, 6, :], ALU.subtract)
                tt(flat(G["Dt"][:]), flat(G["Dt"][:]), ps[:, 7, :], ALU.subtract).then_inc(*DG(f"X{l}"))
            if first:
                ve.memset(G["Wt"][:], 0.0).then_inc(s_init, 1)
                ve.wait_ge(s_vnP, 1)
            else:
                ve.wait_ge(*PG.at(t, "v2"))
            ve.tensor_copy(flat(G["vnew"][:]), ps[:, 3, :]).then_inc(*DG("vn"))
            if not first:
                ve.wait_ge(*PG.at(t, "dS"))
                for h in range(H):
                    m = stt(St[:, h], St[:, h], G["eG"][:, h, P - 1:P], ps[:, 2, P * h:P * (h + 1)],
                            ALU.mult, ALU.add)
                m.then_inc(*DG("S"))
                return
            ve.drain()
            ve.wait_ge(*PG.at(t, "o"))
            for h in range(H):
                tt(vexp[:], b2(G["vnew"][:, h], NS + 1), b3(cst[:, CQ:CQ + NS + 1], P), ALU.mult)\
                    .then_inc(s_vx, 1)
                if h < H - 1:
                    ve.wait_ge(s_dS0, h + 1)
                else:
                    ve.wait_ge(*PG.at(t, "dS"))
                for b in range(NS):
                    stt(S0[:, b, h], S0[:, b, h], G["eG"][:, h, TS * b + TS - 1:TS * (b + 1)],
                        ps[:, 4 + b // 4, P * (b % 4):P * (b % 4 + 1)], ALU.mult, ALU.add)
                m = ve.tensor_copy(St[:, h], ps[:, 6, 0:P])
                m.then_inc(s_vx2, 1) if h < H - 1 else m.then_inc(*DG("S"))

        delta(0)
        with ve.Fori(1, NT) as t:
            delta(t)
        end_phase(ve, 5)

        PN, AN, DN, _ = st["gn"]
        ve.wait_ge(s_sT, 1)
        with ve.Fori(0, H) as h:
            ve.wait_ge(*AN.at(h, "std"))
            ve.reciprocal(gstd[:], gstd[:])
            ve.drain()
            tt(gstd[:], gstd[:], z[:, ds(h, 1), :].rearrange("p a n -> p (a n)"), ALU.mult).then_inc(*DN("a"))
            ve.drain()
            raw = qkv[:, ds(h, 1), :].rearrange("p a n -> p (a n)")
            o = oa[:, ds(h, 1), :].rearrange("p a n -> p (a n)")
            stt(o[:, 0:S], raw[:, 0:S], nvec[:, KD:KD + 1], gstd[:, 0:S], ALU.mult, ALU.mult)
            stt(o[:, S:], raw[:, S + NM:], nvec[:, KD:KD + 1], gstd[:, S:], ALU.mult, ALU.mult).then_inc(*DN("b"))
        end_phase(ve, 6)

        PM, AM, DM, _ = st["mg"]
        with ve.Fori(0, KD) as n:
            for c, (c0, w) in enumerate(CHP):
                q = 3 * n + c
                o = mT[:, ds(n, 1), c0:c0 + w].rearrange("p a n -> p (a n)")
                for r in range(3):
                    ve.wait_ge(*AM.at(q, f"s{r}"))
                    ve.wait_ge(*PM.at(q, f"b{r}"))
                    if r == 0:
                        tt(o, ps[:, 1, 0:w], gs[:, 0, 0:w], ALU.mult).then_inc(*DM("m0"))
                        ve.drain()
                        continue
                    tt(gm[:, r % 2, 0:w], ps[:, 2 * r + 1, 0:w], gs[:, r % 2, 0:w], ALU.mult).then_inc(*DM(f"m{r}"))
                    ve.drain()
                    tt(o, o, gm[:, r % 2, 0:w], ALU.add)
                    ve.drain()
        end_phase(ve, 7)

        PO, AO, DO, LO = st["op"]
        ve.memset(rl[:], 0.0)
        for k in range(EPG):
            ve.memset(iota4[:, k:k + 1], float(k - EPG))
        ve.drain()

        def outproj(t):
            first = isinstance(t, int)
            rows = S if first else P
            x = x2[0:rows, ds(t, 1), :].rearrange("p a n -> p (a n)")
            ve.wait_ge(*PO.at(t, "mix"))
            ve.wait_ge(s_xe, 16 * t + 16)
            tt(x, ps[0:rows, 0:2, :].rearrange("p b n -> p (b n)"), xe[0:rows, :], ALU.add).then_inc(*DO("x2"))
            ve.wait_ge(*AO.at(t, "std"))
            ve.reciprocal(st1[0:rows, 2:3], st1[0:rows, 1:2]).then_inc(*DO("rs"))
            ve.drain()
            ts(he[0:rows, :], x, st1[0:rows, 2:3], ALU.mult).then_inc(*DO("h"))
            ve.wait_ge(*PO.at(t, "tr"))
            if not first:
                ve.wait_ge(*LO.at(t - 1, "h2"))
            for f in range(2):
                m = tt(h2t[:, 4 * f:4 * f + 4, 0:rows], ps[:, 2 + f, :].rearrange("p (k n) -> p k n", k=4)[:, :, 0:rows],
                       b3(n2w[:, 4 * f:4 * f + 4], rows), ALU.mult)
            m.then_inc(*DO("hT"))
            ve.wait_ge(*PO.at(t, "rt"))
            tt(rl[0:rows, ds(t, 1), :].rearrange("p a n -> p (a n)"), ps[0:rows, 4, 0:NG + E], rbias[0:rows, :], ALU.add)\
                .then_inc(*DO("rl"))

        outproj(0)
        with ve.Fori(1, NT) as t:
            outproj(t)
        _, AR_, DR_, _ = st["rt"]

        def d(ins):
            ve.drain()
            return ins

        def first_max(hot, x, m, i):
            ve.tensor_reduce(m, x, AX.X, ALU.max)
            ve.drain()
            tt(hot, x, b3(m, EPG), ALU.is_equal)
            ve.drain()
            tt(hot, hot, b2(iota4[:], NT), ALU.mult)
            ve.drain()
            ve.tensor_reduce(i, hot, AX.X, ALU.min)
            ve.drain()
            tt(hot, b2(iota4[:], NT), b3(i, EPG), ALU.is_equal)
            ve.drain()

        ve.drain()
        gl = rl[:, :, 0:NG]
        first_max(goh[:], gl, r1[:, 0], r1[:, 1])
        tt(ra[:, :, 0:NG], gl, b3(r1[:, 0], NG), ALU.subtract).then_inc(*DR_("gm"))
        g4 = goh[:].unsqueeze(3).to_broadcast([P, NT, NG, EPG])
        c4 = comb[:].rearrange("p t (g k) -> p t g k", g=NG)
        tt(c4, rl[:, :, NG:].rearrange("p t (g k) -> p t g k", g=NG), g4, ALU.mult)
        ve.drain()
        ve.tensor_reduce(esel[:], comb[:].rearrange("p t (g k) -> p t k g", g=NG), AX.X, ALU.add)
        ve.drain()
        first_max(rb[:], esel[:], r1[:, 2], r1[:, 3])
        stt(rc[:], rb[:], NEG, esel[:], ALU.mult, ALU.add)
        ve.drain()
        first_max(rd[:], rc[:], r1[:, 4], r1[:, 5])
        tt(r1[:, 4], r1[:, 4], r1[:, 2], ALU.subtract).then_inc(*DR_("em"))
        ve.wait_ge(*AR_.at(0, "es"))
        ve.tensor_reduce(r1[:, 6], ra[:, :, 0:NG], AX.X, ALU.add)
        tt(rc[:], rd[:], b3(r1[:, 4], EPG), ALU.mult)
        ve.drain()
        stt(r1[:, 7], r1[:, 4], 1.0, r1[:, 6], ALU.add, ALU.mult)
        tt(rc[:], rc[:], rb[:], ALU.add)
        ve.drain()
        ve.reciprocal(r1[:, 7], r1[:, 7])
        ve.drain()
        tt(rc[:], rc[:], b3(r1[:, 7], EPG), ALU.mult)
        ve.drain()
        tt(c4, g4, rc[:].unsqueeze(2).to_broadcast([P, NT, NG, EPG]), ALU.mult).then_inc(*DR_("w"))
        end_phase(ve, 8)

        PXC, AXC, DXC, _ = st["ch"]
        PY, _, DY, _ = st["dn"]
        with ve.Fori(0, E) as e:
            for ft in range(2):
                for c, (c0, n) in enumerate(CHP):
                    b = (3 * ft + c) % 2
                    ve.wait_ge(*AXC.at((e * 2 + ft) * 3 + c, "s"))
                    tt(hid[:, ft, c0:c0 + n], ps[:, 2 * b + 1, 0:n], sg[:, b, 0:n], ALU.mult).then_inc(*DXC("h"))
            for t in range(NT):
                rows = S if t == 0 else P
                for f in range(2):
                    ve.wait_ge(*PY.at((e * NT + t) * 2 + f, "y"))
                    x = x2[0:rows, t, 512 * f:512 * (f + 1)]
                    stt(x, ps[0:rows, 4 + 2 * (t % 2) + f, :], comb[0:rows, t, ds(e, 1)], x, ALU.mult, ALU.add)\
                        .then_inc(*DY("acc"))
        end_phase(ve, 9)

    @block.gpsimd
    def _(po):
        cp = po.tensor_copy
        for p in range(2):
            po.memset(ext[:, p, EXS:EXS + CONV - 1], 0.0)
        po.memset(uxt[:, UXS:UXS + CT - 1], 0.0)
        PA1, AA1, DA1, LA1 = st["A1"]

        def a1(t):
            po.wait_ge(*DA1.at(t, "hTt"))
            if isinstance(t, int):
                cp(hT[:, :, 0:S], hTt[:, :, 0:S])
                cp(hT[:, :, TOK:ALL], hTt[:, :, S:S + NM]).then_inc(*LA1("hT"))
            else:
                cp(hT[:, :, tile_cols(t)], hTt[:]).then_inc(*LA1("hT"))

        a1(0)
        with po.Fori(1, NT) as t:
            a1(t)
        end_phase(po, 1)

        PB, AB, DB, LB = st["bq"]

        def bq(n, k):
            es = ext[:, k % 2, 0:EXS].rearrange("p (b n) -> p b n", b=NS)
            if not (isinstance(n, int) and n < 2):
                po.wait_ge(*DB.at(n - 2, "conv"))
            cp(es[:, :, 0:CONV - 1],
               histT[:, ds(n, 1), 0:NS * (CONV - 1)].rearrange("p a (b n) -> p (a b) n", b=NS)).then_inc(*LB("hist"))
            po.wait_ge(*AB.at(n, "ev"))
            cp(tailT[:, ds(n, 1), 0:24].rearrange("p a (b n) -> p (a b) n", b=NS), es[:, :, TS:])
            cp(tailT[:, ds(n, 1), 24:27].rearrange("p a n -> p (a n)"),
               ext[:, k % 2, EXS + NM + SEQ:EXS + EXP_]).then_inc(*LB("tail"))

        for k in range(4):
            bq(k, k)
        with po.Fori(1, 3) as i:
            for k in range(4):
                bq(i * 4 + k, k)
        PU, AU, DU, LU = st["bu"]
        us = uxt[:, 0:UXS].rearrange("p (b n) -> p b n", b=NS)
        for j in range(4):
            if j:
                po.wait_ge(*DU.at(j - 1, "conv"))
            cp(us[:, :, 0:CT - 1], chistT[:, j].rearrange("p (b n) -> p b n", b=NS)).then_inc(*LU("hist"))
            po.wait_ge(*DU.at(j, "u"))
            cp(utail[:, j, 0:S].rearrange("p (b n) -> p b n", b=NS), us[:, :, CT - 1:])
            cp(utail[:, j, S:], uxt[:, UXS + UXP - (CT - 1):]).then_inc(*LU("tail"))
        end_phase(po, 2)

        PT_, AT_, DT_, LT_ = st["at"]
        cp(kst[:], kT[:, 0:2 * P])
        cp(qst[:], qT[:, :, P:2 * P]).then_inc(*LT_("q"))
        with po.Fori(2, NT) as t:
            po.wait_ge(*PT_.at(t - 2, "sc"))
            cp(kst[:], kT[:, ds(P * (t - 1), 2 * P)])
            cp(qst[:], qT[:, :, ds(P * t, P)]).then_inc(*LT_("q"))
        end_phase(po, 3)
        end_phase(po, 4)

        PG, AG, DG, LG = st["gd"]
        po.memset(stg[:], 0.0)
        po.drain()
        cp(gsm[:, 16:24], ab[:, 0, :])
        cp(stg[:, :, 0:S + NM], qkv[:, :, 0:S + NM]).then_inc(*LG("stage"))
        with po.Fori(1, NT) as t:
            po.wait_ge(*DG.at(t - 1, "A"))
            po.wait_ge(*PG.at(t - 1, "kv"))
            cp(gsm[:, 16:24], ab[:, ds(t, 1), :].rearrange("p a n -> p (a n)"))
            cp(stg[:], qkv[:, :, bass.ds(S + NM + P * (t - 1), P)]).then_inc(*LG("stage"))
        end_phase(po, 5)
        end_phase(po, 6)
        end_phase(po, 7)

        PO, AO, DO, LO = st["op"]

        def outproj(t):
            first = isinstance(t, int)
            rows = S if first else P
            cols = slice(0, S) if first else tile_cols(t)
            if not first:
                po.wait_ge(*PO.at(t - 1, "mix"))
            cp(mst[:, :, 0:rows], mT[:, :, cols]).then_inc(*LO("stage"))
            po.wait_ge(*DO.at(t, "hT"))
            cp(h2[:, :, cols], h2t[:, :, 0:rows]).then_inc(*LO("h2"))

        outproj(0)
        with po.Fori(1, NT) as t:
            outproj(t)
        end_phase(po, 8)
        end_phase(po, 9)

    block.__exit__(None, None, None)


def launch_io():
    outs = {
        "y_prompt": (1, SEQ, D), "y_sample": (NS, TS, D), "state_gdn_p": (1, 1, H, DK, DK),
        "cache_gdn_conv_p": (1, 1, CONV - 1, QKV), "cache_swa_kv_p": (1, 1, W, 2, KVH, HD),
        "cache_meta_kv_p": (1, 1, NM, 2, KVH, HD), "cache_conv_p": (1, 1, CT - 1, CC),
        "state_gdn_s": (1, NS, H, DK, DK), "cache_gdn_conv_s": (1, NS, CONV - 1, QKV),
        "cache_swa_kv_s": (1, NS, W, 2, KVH, HD), "cache_conv_s": (1, NS, CT - 1, CC)}
    return outs


def kernel(**inputs):
    import concourse.bacc as bacc
    from concourse.bass_utils import run_bass_kernel_spmd

    nc = bacc.Bacc("TRN2", target_bir_lowering=False, num_devices=1)
    arrays = {f"in_{k}": np.ascontiguousarray(v) for k, v in inputs.items()}
    arrays["in_consts"] = constants()
    A = {k[3:]: nc.dram_tensor(k, v.shape, F32, kind="ExternalInput").ap() for k, v in arrays.items()}
    O = {k: nc.dram_tensor(f"out_{k}", s, F32, kind="ExternalOutput").ap() for k, s in launch_io().items()}
    build(nc, A, O)
    r = run_bass_kernel_spmd(nc, [arrays], core_ids=[0])
    return tuple(r.results[0][f"out_{k}"] for k in launch_io())
```

```python
import numpy as np
import concourse.bass as bass
from concourse import mybir

F32 = mybir.dt.float32
U32 = mybir.dt.uint32
I32 = mybir.dt.int32
ALU = mybir.AluOpType
ACT = mybir.ActivationFunctionType
AX = mybir.AxisListType

P = 128
D = 1024
KD = D // P
SEQ, NS, TS, NM = 1024, 8, 8, 16
S = NS * TS
TOK = S + SEQ
ALL = TOK + NM
NT = 1 + SEQ // P
H, DK = 4, 128
CONV, QKV = 4, 3 * H * DK
HB, KVH, HD = 8, 2, 64
W = 128
CC, CT = 512, 31
NG, EPG, E, F = 4, 4, 16, 256
EPS = 1e-6
C_Z = QKV
C_AB = C_Z + H * DK
C_U = C_AB + 2 * H + (HB + 2 * KVH) * HD
C_G = C_U + 2 * CC
NAT = C_U - C_AB
NQK = (HB + KVH) * HD
CH = 368
CHS = [(0, CH), (CH, CH), (2 * CH, CH)]
CHP = [(0, CH), (CH, CH), (2 * CH, TOK - 2 * CH)]
EXS, EXP_ = NS * (CONV - 1 + TS), CONV - 1 + NM + SEQ
UXS, UXP = NS * (CT - 1 + TS), CT - 1 + NM + SEQ
NEG = -1.0e30
NHR = NS * (CONV - 1) + CONV
CI = 0
CU = CI + P
CN = CU + 2 * P
CS = CN + 2 * P
CSS = CS + 2 * P
CL = CSS + 2 * P
CQ = CL + 7 * P
C1 = CQ + NS + 1
CB = C1 + P
CM = CB + 2 * P
CR = CM + W + NM + TS
CV = CR + HB
NSLOT = (2 * TOK - 16) // P + 16
assert NSLOT % 2 == 0
CW = CV + NT
CX = CW + NSLOT
CY = CX + NT
NCST = CY + E * E
NC0 = CV


def constants():
    i = np.arange(P)
    seq0 = np.where(i < S, i // TS, np.where(i < S + NM, NS, -1 - i))
    c = np.zeros((P, NCST), np.float32)
    c[:, CI:CU] = np.eye(P)
    for n, seq in enumerate((seq0, np.zeros(P, int))):
        same = seq[:, None] == seq[None, :]
        upto = same & (i[:, None] <= i[None, :])
        c[:, CU + n * P:CU + (n + 1) * P] = upto
        c[:, CN + n * P:CN + (n + 1) * P] = np.where(upto, 0, NEG)
        c[:, CS + n * P:CS + (n + 1) * P] = upto & (i[:, None] < i[None, :])
        c[:, CSS + n * P:CSS + (n + 1) * P] = same
    for l in range(7):
        s = 1 << l
        c[:, CL + l * P:CL + (l + 1) * P] = ((i[:, None] // s) % 2 == 1) & (i[None, :] // s == i[:, None] // s - 1)
    c[:, CQ:C1] = seq0[:, None] == np.arange(NS + 1)[None, :]
    c[:, C1:CB] = 1.0
    d = i[:, None] + P - np.arange(2 * P)[None, :]
    c[:, CB:CM] = np.where((d >= 0) & (d < W), 0, NEG)
    t = (i % TS)[:, None]
    j = np.arange(W + NM + TS)[None, :]
    ok = np.where(j < W, j > t, np.where(j < W + NM, True, j - W - NM <= t))
    c[:, CM:CR] = np.where(ok, 0, NEG)
    head = (i // 32 % 2) * 4 + i % 32 // TS
    c[:, CV:CW] = P * np.arange(NT)
    c[:, CW:CX] = np.arange(NSLOT)
    c[:, CX:CY] = np.where(np.arange(NT) == 0, i[:, None], S - P + P * np.arange(NT) + i[:, None])
    c[:, CY:] = (np.arange(E)[None, :] < np.arange(E)[:, None]).reshape(1, -1)
    c[:, CR:CV] = head[:, None] == np.arange(HB)[None, :]
    return c


class Steps:

    def __init__(self, sem, names):
        self.sem, self.names, self.next = sem, names.split(), 0

    def __call__(self, name):
        assert self.names[self.next % len(self.names)] == name, (name, self.names, self.next)
        self.next += 1
        return self.sem, 1

    def at(self, n, name):
        return self.sem, n * len(self.names) + (self.names.index(name) + 1)


def wait(e, value):
    sem, v = value
    if not isinstance(v, int) or v > 0:
        e.wait_ge(sem, v)


def build(nc, A, O):
    names = {}

    def place(name, at, *shape, parts=P, dt=F32):
        n = int(np.prod(shape))
        assert at + n <= WORDS, (name, at + n, WORDS)
        names[name] = (at, n)
        return nc.alloc_sbuf_tensor_at(name, [parts, *shape], dt, offset=BASE + 4 * at)

    def up(n):
        return (n + 7) // 8 * 8

    def small(name, *shape):
        at = cursor[0]
        cursor[0] = up(at + int(np.prod(shape)))
        return place(name, at, *shape)

    cursor = [up(NC0)]
    BASE = (nc.sbuf_base + 63) // 64 * 64
    WORDS = (nc.sbuf_usable_end - BASE) // 4
    sems = {}

    def sem(name):
        sems[name] = nc.alloc_semaphore(name)
        return sems[name]

    ps = nc.alloc_psum_tensor("psum", [P, 8, 512], F32)

    cst = place("cst", 0, NC0)
    nvec = small("nvec", KD + 2)
    n2w = small("n2w", KD)
    dvec = small("dvec", 4, CT + 3)
    qw = small("qw", 1)
    eps = small("eps", 2)
    sink = small("sink", HB)
    sinkr = small("sinkr", 1)
    alog = small("alog", H)
    dtb = small("dtb", H)
    kw = small("kw", HD)
    ab = small("ab", NT, 2 * H)
    rbias = small("rbias", NG + E)
    st1 = small("st1", 12)
    st2 = small("st2", 48)
    tmp36 = small("tmp36", NT, H)
    tmq36 = small("tmq36", NT, H)
    histT = small("histT", 12, NHR)
    R1 = up(cursor[0])
    R2 = R1 + KD * ALL
    R3 = R2 + 12 * ALL
    R4, R5, R6 = R3 + 4 * TOK, R3 + 8 * TOK, R3 + 12 * TOK
    RW = R3 + 16 * TOK

    hT = place("hT", R1, KD, ALL)
    qkv = place("qkv", R2, 12, ALL)
    z = place("z", R3, 4, TOK)
    oc = place("oc", R4, 4, TOK)
    ob = place("ob", R5, 4, TOK)
    oa = place("oa", R6, 4, TOK)
    qT = place("qT", RW, 4, NT * P)
    kT = place("kT", RW + 4 * NT * P, NT * P)
    kv = place("kv", RW + 5 * NT * P, NT, 2 * P)
    RX = RW + 7 * NT * P
    wat = place("wat", R2, KD, NAT)
    xt = place("xt", R3, D)
    ht = place("ht", R3 + D, D)
    sqj = place("sqj", R3 + 2 * D, D)
    hTt = place("hTt", R3 + 3 * D, KD, P)
    at = place("at", R3 + 4 * D, NAT)
    sq2 = place("sq2", R3 + 5 * D, NQK)
    qp = place("qp", R3 + 5 * D + NQK, 4, 2, HD)
    hrow = place("hrow", R5, QKV, parts=NHR)
    urow = place("urow", R5 + QKV, 2, CC, parts=NS * (CT - 1) // 2)
    vrow = place("vrow", R5 + QKV + 2 * CC, CC, parts=CT + 3)
    nrow = place("nrow", R5 + QKV + 3 * CC, P, parts=KD + 2)
    wB = place("wB", R5, 3, KD, P)
    RE = R5 + QKV + 3 * CC + P
    RS = up(RE + 3 * (EXS + EXP_))
    ext = place("ext", RE, 3, EXS + EXP_)
    sig = place("sig", RS, ALL)
    chistT = place("chistT", RS + ALL, 4, NS * (CT - 1))
    assert RE >= R5 + 3 * KD * P and RS + ALL + 4 * NS * (CT - 1) <= RW
    uxt = place("uxt", RX, UXS + UXP)
    tailT = place("tailT", RX + up(UXS + UXP), 12, 27)
    utail = place("utail", RX + up(UXS + UXP) + up(324), 4, S + CT - 1)
    sqb = place("sqb", R6, 4, CH)
    rsb = place("rsb", R6 + 4 * CH, 2, CH)
    hq = place("hq", R5, 2, QKV, parts=24)
    hu = place("hu", R5 + 2 * QKV, CC, parts=S + CT - 1)
    sc = place("sc", R6, HB, NM + 2 * P)
    PT = place("PT", R6 + HB * (NM + 2 * P), HB, 2 * P)
    PTm = place("PTm", RX, HB, P, parts=NM)
    otok = place("otok", R6, HB, HD)
    qst = place("qst", RX + D + 512, 4, P)
    vm = place("vm", RX + D + 1024, P, parts=NM)
    kst = place("kst", RX + D, 2 * P)
    win = place("win", R6, NS, 2 * P)
    mk = place("mk", R6 + 2048, P)
    kTw = place("kTw", R6 + 2176, NS, W + NM + TS)
    scs = place("scs", R6 + 2176 + 1216, 4, W + NM + TS)
    odup = place("odup", R6 + 2176, 4, 2, HD)
    PTw = place("PTw", RX, 4, P)
    PTn = place("PTn", RX + 512, 4, P, parts=NM + TS)
    vmn = place("vmn", RX + 1024, NS, P, parts=NM + TS)
    qs = place("qs", R6 + 4000, NS, 4, TS)
    g_names = "eG dec AtT PT2 Am B0 B1 Dm Dt Wt vb kbg kdec qdec vnew"
    G = {n: place("g_" + n, RW + 12 * P + 512 * k, H, P) for k, n in enumerate(g_names.split())}
    G["nwT"] = G["kbg"]
    stg = place("stg", RW, 12, P)
    St = place("St", RW + 12 * P + 512 * 15, H, P)
    gsm = place("gsm", RW + 12 * P + 512 * 16, 32)
    vexp = place("vexp", names["g_Am"][0], NS + 1, P)
    S0 = place("S0", R6, NS, H, P)
    gnt = place("gnt", RW, ALL)
    gstd = place("gstd", RW + ALL, TOK)
    mT = place("mT", R2, KD, TOK)
    gw = place("gw", RW, 2, 3, KD, P)
    bw = place("bw", R2 + KD * TOK, 2, 3, 4, P)
    gs = place("gs", RW + 6 * KD * P, 2, CH)
    gm = place("gm", RW + 6 * KD * P + 2 * CH, 2, CH)
    wo = place("wo", RW, KD, D)
    x2 = place("x2", R3, NT, D)
    wr = place("wr", RW + 8 * D, KD, NG + E)
    mst = place("mst", R2 + KD * TOK, KD, P)
    xe = place("xe", R2 + KD * TOK + D, D)
    he = place("he", R2 + KD * TOK + 2 * D, D)
    h2t = place("h2t", R2 + KD * TOK + 3 * D, KD, P)
    rl = place("rl", RW + 8 * D + 160, NT, NG + E)
    RC = RW + 8 * D + 160 + 184
    comb = place("comb", RC, NT, E)
    esel = place("esel", RC + 144, NT, EPG)
    ra = place("ra", RC + 184, NT, E)
    rb = place("rb", RC + 328, NT, EPG)
    rc = place("rc", RC + 368, NT, EPG)
    rd = place("rd", RC + 408, NT, EPG)
    goh = place("goh", RC + 448, NT, NG)
    r1 = place("r1", RC + 488, 8, NT)
    iota4 = place("iota4", RC + 560, EPG)
    ohs = place("ohs", R1, 2, NT, E)
    ohm = place("ohm", R1 + 288, NT, E)
    cnt = place("cnt", R1 + 432, NT + 1, E)
    slot = place("slot", R1 + 592, NT, E)
    big = place("big", R1 + 736, NSLOT * E)
    til = place("til", R1 + 1264, 4, E)
    slf = place("slf", R1 + 1328, 2, NT)
    texf = place("texf", R1 + 1352, NSLOT)
    wts = place("wts", R1 + 1392, 2, NT)
    sqe = place("sqe", R1 + 1416, D)
    slu = place("slu", R1 + 2440, 2, NT, dt=U32)
    tok = place("tok", R1 + 2464, NT, dt=U32)
    tex = place("tex", R1 + 2480, NSLOT, dt=I32)
    idx = place("idx", R1 + 2520, NSLOT, dt=U32)
    zid = place("zid", R1 + 2560, NSLOT, dt=U32)
    rcs = place("rcs", R1 + 2624 + 4 * D, NCST - NC0)
    slb = place("slb", R1 + 2944 + 4 * D, 2, NT)
    slm = place("slm", R1 + 2968 + 4 * D, 2, NT)
    idc = [place(f"idc{k}", R1 + 2600 + 8 * k, 1, dt=U32) for k in range(2)]
    ew = [place("ew0", R2, 3, 2048), place("ew1", R3 + NT * D, 3, 2048)]
    xg = place("xg", R2 + 6144, 2, D)
    xT = place("xT", R2 + 6144 + 2 * D, KD, P)
    sg = place("sg", R2 + 6144 + 3 * D, 2, P)
    hid = place("hid", R2 + 6144 + 3 * D + 256, 2, 2, P)
    yt = place("yt", R2 + 6144 + 3 * D + 768, 2, D)
    yg = place("yg", R1 + 2624, 2, 2, D)
    assert R2 + 6144 + 5 * D + 768 <= R3 and R3 + NT * D + 6144 <= RW and NCST - NC0 <= 320 and R1 + 3000 + 4 * D <= R2
    h2_rows = nc.dram_tensor("h2_rows", [TOK, D], F32).ap()
    y_slots = nc.dram_tensor("y_slots", [NSLOT * P, D], F32).ap()
    slot_tok = nc.dram_tensor("slot_tok", [NSLOT * P, 1], U32).ap()

    def cc(a, n=P):
        return cst[:, a:a + n]

    ident = cc(CI)
    w_in = A["w_in"][0]

    s_small, s_wat, s_out = sem("small_loaded"), sem("wat_loaded"), sem("outputs_written")
    s_hist, s_x, s_x0 = sem("hist_loaded"), sem("x_loaded"), sem("x0_loaded")
    s_w = [sem(f"w_slot{k}_loaded") for k in range(3)]
    s_end = sem("phase_ended")
    s_vm, s_win, s_S0 = sem("vm_loaded"), sem("win_loaded"), sem("state_loaded")
    s_gw = [sem(f"merge_w{k}_loaded") for k in range(2)]
    s_wo, s_xe, s_rc = sem("wo_loaded"), sem("xe_loaded"), sem("routing_constants_loaded")
    s_ew = [sem(f"gate_up_w{k}_loaded") for k in range(2)]
    s_dw = [sem(f"down_w{k}_loaded") for k in range(2)]
    s_h2, s_zt, s_sc, s_idx = (sem(n) for n in ("h2_rows_stored", "table_cleared", "table_scattered", "table_loaded"))
    s_xg = [sem(f"rows{k}_gathered") for k in range(2)]
    s_ys = [sem(f"y{k}_stored") for k in range(2)]
    s_yg = [sem(f"y{k}_gathered") for k in range(2)]
    s_cast = sem("tables_cast")
    s_vnT, s_vnP, s_vx, s_dS0, s_vx2 = (sem(n) for n in ("samples_wS_out", "samples_v_new", "v_spread", "samples_dS", "samples_S_done"))
    N_SMALL, N_HIST, N_WIN = 12, 7, 3 + NS
    s_init, s_hq, s_sT = sem("init_done"), sem("cache_rows_done"), sem("state_out_done")
    st = {}

    def steps(key, pe="", act="", dve="", pool=""):
        st[key] = tuple(Steps(sem(f"{key}_{n}"), s) if s else None
                        for n, s in (("pe", pe), ("act", act), ("dve", dve), ("pool", pool)))

    steps("pre", pe="hist", act="histT chistT", dve="vec")
    steps("A1", pe="tr proj", act="sq std", dve="rs h hTt", pool="hT")
    steps("A2", pe="qkT", act="at sq2 std2 qT", dve="ssq rs2 qk keep")
    steps("gb", act="lse sig", dve="x m g")
    steps("bq", pe="proj", act="ev silu", dve="conv", pool="hist tail")
    steps("bz", pe="proj", act="z")
    steps("bu", pe="gate value", act="sig", dve="u conv", pool="hist tail")
    steps("ln", pe="mu var", act="sq std silu", dve="cent rs norm")
    steps("rows", pe="q u", act="q", dve="u")
    steps("l2", pe="ss", act="sq std", dve="norm")
    steps("at", pe="sc trm tra trb pv oT", act="exp PTa oT", dve="sc max den PTm PTb o", pool="q")
    steps("sa", pe="kT sc tr pv oT", act="kT exp PT", dve="qs sc max den o oT")
    steps("gd", pe="G kkpq kv At D1 " + " ".join(f"W{l} X{l}" for l in range(1, 7)) + " u v2 o dS",
          act="eG dec D1 " + " ".join(f"W{l}" for l in range(1, 7)) + " nw o",
          dve="cols arg At PT2 kq A D1 " + "B1 B2 X1 B3 X2 B4 X3 B5 X4 B6 X5 X6" + " vn S",
          pool="stage")
    steps("gn", pe="ss", act="sq std", dve="a b")
    steps("mg", pe="g0 b0 g1 b1 g2 b2", act="s0 s1 s2", dve="m0 m1 m2")
    steps("op", pe="mix tr rt", act="sq std", dve="x2 rs h hT rl", pool="stage")
    steps("rt", pe="cnt", act="eg es", dve="gm em oh w tab")
    steps("gu", pe="tr gu", act="s", dve="xT h")
    steps("dn", pe="y", act="y0", dve="y1")
    steps("fin", dve="y")

    phase = {"n": 0}
    marks = {}

    def end_phase(e, k):
        e.drain().then_inc(s_end, 1)
        e.wait_ge(s_end, 4 * k)

    def tile_cols(t):
        return bass.ds(S + P * (t - 1), P) if not isinstance(t, int) else slice(S + P * (t - 1), S + P * t)

    def ds(start, n):
        return slice(start, start + n) if isinstance(start, int) else bass.ds(start, n)

    def b3(ap, n):
        return ap.unsqueeze(2).to_broadcast([ap.shape[0], ap.shape[1], n])

    def b2(ap, n):
        return ap.unsqueeze(1).to_broadcast([ap.shape[0], n, ap.shape[1]])

    block = nc.Block()
    block.__enter__()

    @block.sync
    def _(sp):
        def load(dst, src, s):
            sp.dma_start(dst, src).then_inc(s, 16)

        def store(dst, src):
            st_out["n"] += 16
            sp.dma_start(dst, src).then_inc(s_out, 16)

        st_out = {"n": 0}
        load(cst[:], A["consts"][:, 0:NC0], s_small)
        load(nrow[0:KD, :], A["norm1_w"][0].rearrange("(k p) -> k p", p=P), s_small)
        load(nrow[KD:KD + 1, :], A["gdn_norm_w"], s_small)
        load(nrow[KD + 1:KD + 2, 0:HD], A["swa_q_norm_w"], s_small)
        load(nrow[KD + 1:KD + 2, HD:P], A["swa_q_norm_w"], s_small)
        load(n2w[:], A["norm2_w"][0].rearrange("(p k) -> p k", k=KD), s_small)
        load(sink[:], A["swa_sinks"][0].partition_broadcast(P), s_small)
        load(alog[:], A["gdn_a_log"][0].partition_broadcast(P), s_small)
        load(dtb[:], A["gdn_dt_bias"][0].partition_broadcast(P), s_small)
        load(kw[:], A["swa_k_norm_w"][0].partition_broadcast(P), s_small)
        load(rbias[:, 0:NG], A["router_group_b"][0].partition_broadcast(P), s_small)
        load(rbias[:, NG:NG + E], A["router_expert_b"][0].partition_broadcast(P), s_small)
        assert N_SMALL == 12
        sp.wait_ge(s_init, 1)
        load(xt[0:S, :], A["x_sample"].rearrange("b t d -> (b t) d"), s_x0)
        load(xt[S:S + NM, :], A["meta_tokens"], s_x0)
        load(wat[:], w_in[:, C_AB:C_U].rearrange("(k p) n -> p k n", p=P), s_wat)
        load(hrow[0:NHR - CONV, :], A["cache_gdn_conv"][0].rearrange("b t c -> (b t) c"), s_hist)
        load(hrow[NHR - CONV:NHR, :], A["gdn_conv_w"][0], s_hist)
        load(urow[:], A["cache_conv"][0].rearrange("(a b) t c -> (b t) a c", a=2), s_hist)
        load(vrow[0:CT, :], A["conv_dw_w"][0], s_hist)
        load(vrow[CT:CT + 1, :], A["conv_dw_b"], s_hist)
        load(vrow[CT + 1:CT + 2, :], A["conv_ln_w"], s_hist)
        load(vrow[CT + 2:CT + 3, :], A["conv_ln_b"], s_hist)
        assert N_HIST == 7
        store(O["cache_swa_kv_s"][0][:, 0:W - TS].rearrange("b w c h d -> b (w c h d)"),
              A["cache_swa_kv"][0][:, TS:W].rearrange("b w c h d -> b (w c h d)"))
        store(O["cache_conv_s"][0][:, 0:CT - 1 - TS].rearrange("b w c -> b (w c)"),
              A["cache_conv"][0][:, TS:CT - 1].rearrange("b w c -> b (w c)"))
        with sp.Fori(1, NT) as t:
            sp.wait_ge(*st["A1"][2].at(t - 1, "h"))
            load(xt[:], A["x_prompt"][0][ds(P * (t - 1), P), :], s_x)

        def round_done(j, c):
            return (st["bu"][0].at(j, ("gate", "value")[c]) if c < 2 else
                    st["bz"][0].at(j, "proj") if c == 2 else st["bq"][0].at(3 * j + c - 3, "proj"))

        def load_round(j):
            for c, col in enumerate((C_U + CC, C_U, C_Z, 0, P, 2 * P)):
                if c >= 3:
                    sp.wait_ge(*round_done(j, c - 3))
                elif not isinstance(j, int):
                    sp.wait_ge(*round_done(j - 1, c + 3))
                load(wB[:, c % 3], w_in[:, ds((j * P if c < 3 else j * 3 * P) + col, P)]
                     .rearrange("(k p) n -> p k n", p=P), s_w[c % 3])

        sp.wait_ge(*st["pre"][1].at(0, "chistT"))
        load_round(0)
        with sp.Fori(1, 4) as j:
            load_round(j)
        sp.wait_ge(*st["rows"][2].at(0, "u"))
        sp.wait_ge(*st["rows"][1].at(0, "q"))
        store(O["cache_gdn_conv_s"][0].rearrange("b t c -> (b t) c"), hq[:, 0, :])
        store(O["cache_gdn_conv_p"][0, 0], hq[0:CONV - 1, 1, :])
        for b in range(NS):
            store(O["cache_conv_s"][0, b, CT - 1 - TS:CT - 1, :], hu[TS * b:TS * (b + 1), :])
        store(O["cache_conv_p"][0, 0], hu[S:S + CT - 1, :])
        sp.wait_ge(s_out, st_out["n"])
        sp.sem_inc(s_hq, 1)
        sp.wait_ge(s_end, 4)
        for b in range(NS):
            store(O["cache_swa_kv_s"][0, b, W - TS:W].rearrange("t c h d -> t (c h d)"),
                  kv[TS * b:TS * (b + 1), 0, :])
        store(O["cache_meta_kv_p"][0, 0].rearrange("t c h d -> t (c h d)"), kv[S:S + NM, 0, :])
        store(O["cache_swa_kv_p"][0, 0].rearrange("t c h d -> t (c h d)"), kv[:, NT - 1, :])
        sp.wait_ge(s_end, 8)
        load(vm[:], kv[S:S + NM, 0, P:2 * P], s_vm)
        sp.wait_ge(s_end, 12)
        load(win[:], A["cache_swa_kv"][0].rearrange("b w c h d -> w b (c h d)"), s_win)
        load(mk[:], A["cache_meta_kv"][0][:, :, 0].rearrange("b m h d -> (b m) (h d)"), s_win)
        load(vmn[0:NM], A["cache_meta_kv"][0][:, :, 1].rearrange("b m h d -> m b (h d)"), s_win)
        for b in range(NS):
            load(vmn[NM:NM + TS, b, :], kv[TS * b:TS * (b + 1), 0, P:2 * P], s_win)
        assert N_WIN == 3 + NS
        sp.wait_ge(s_end, 16)
        load(S0[:], A["state_gdn"][0].rearrange("b h k v -> k b h v"), s_S0)
        sp.wait_ge(*st["gd"][2].at(0, "S"))
        store(O["state_gdn_s"][0].rearrange("b h k v -> k b h v"), S0[:])
        sp.wait_ge(*st["gd"][2].at(NT - 1, "S"))
        store(O["state_gdn_p"][0, 0].rearrange("h k v -> k h v"), St[:])
        sp.wait_ge(s_out, st_out["n"])
        sp.sem_inc(s_sT, 1)

        def load_m(n, k):
            load(gw[:, k, 0], w_in[:, ds(C_G + P * n, P)].rearrange("(k p) n -> p k n", p=P), s_gw[k])
            load(gw[:, k, 1], w_in[:, ds(C_G + D + P * n, P)].rearrange("(k p) n -> p k n", p=P), s_gw[k])
            load(gw[:, k, 2], w_in[:, ds(C_G + 2 * D + P * n, P)].rearrange("(k p) n -> p k n", p=P), s_gw[k])
            for r in range(3):
                load(bw[:, k, r], A["w_branch"][0, r][:, ds(P * n, P)].rearrange("(k p) n -> p k n", p=P), s_gw[k])

        sp.wait_ge(s_end, 24)
        load_m(0, 0)
        load_m(1, 1)
        with sp.Fori(1, 4) as i:
            for k in range(2):
                sp.wait_ge(*st["mg"][0].at(3 * (2 * i + k) - 4, "b2"))
                load_m(2 * i + k, k)
        sp.wait_ge(s_end, 28)
        load(rcs[:], A["consts"][:, NC0:NCST], s_rc)
        load(wo[:], A["w_out"][0].rearrange("(k p) n -> p k n", p=P), s_wo)
        load(wr[:, :, 0:NG], A["router_group_w"][0].rearrange("(p k) n -> p k n", k=KD), s_wo)
        load(wr[:, :, NG:NG + E], A["router_expert_w"][0].rearrange("(p k) n -> p k n", k=KD), s_wo)
        load(xe[0:S, :], A["x_sample"].rearrange("b t d -> (b t) d"), s_xe)
        sp.wait_ge(s_cast, 1)
        load(slot_tok.rearrange("(p i) a -> p (i a)", p=P), zid[:], s_zt)
        sp.wait_ge(*st["op"][2].at(0, "x2"))
        load(xe[:], A["x_prompt"][0][0:P, :], s_xe)
        sp.wait_ge(*st["op"][2].at(0, "h"))
        load(h2_rows[0:S, :], he[0:S, :], s_h2)
        with sp.Fori(1, NT - 1) as t:
            sp.wait_ge(*st["op"][2].at(t, "x2"))
            load(xe[:], A["x_prompt"][0][ds(P * t, P), :], s_xe)
            sp.wait_ge(*st["op"][2].at(t, "h"))
            load(h2_rows[ds(S + P * (t - 1), P), :], he[:], s_h2)
        sp.wait_ge(*st["op"][2].at(NT - 1, "h"))
        load(h2_rows[TOK - P:TOK, :], he[:], s_h2)

        def load_gu(i, k):
            e = sp.value_load(tex[0:1, ds(i, 1)], min_val=0, max_val=E - 1)
            for m, name in enumerate(("moe_w_gate", "moe_w_up")):
                load(ew[k][:, m, :], A[name][0][bass.ds(e, 1)].rearrange("e (p k) f -> p (e k f)", k=KD), s_ew[k])
            return e

        def load_d(e, k):
            load(ew[k][:, 2, :].rearrange("p (k n) -> p k n", k=2),
                 A["moe_w_down"][0][bass.ds(e, 1)].rearrange("e (k p) n -> p (e k) n", p=P), s_dw[k])

        def store_y(i, k):
            sp.wait_ge(*st["dn"][1].at(i, "y0"))
            sp.wait_ge(*st["dn"][2].at(i, "y1"))
            load(y_slots.rearrange("(p i) d -> p i d", p=P)[:, ds(i, 1), :], yt[:, k:k + 1], s_ys[k])

        sp.wait_ge(*st["rt"][2].at(0, "tab"))
        for k in range(2):
            load_d(load_gu(k, k), k)
        sp.wait_ge(s_end, 32)
        sp.wait_ge(s_sc, 32 * NT)
        load(idx[:], slot_tok.rearrange("(p i) a -> p (i a)", p=P), s_idx)
        with sp.Fori(0, (NSLOT - 2) // 2) as j:
            for k in range(2):
                i = 2 * j + k
                sp.wait_ge(*st["gu"][0].at(i, "gu"))
                e = load_gu(i + 2, k)
                sp.wait_ge(*st["dn"][0].at(i, "y"))
                load_d(e, k)
                store_y(i, k)
        for k in range(2):
            store_y(NSLOT - 2 + k, k)
        for t in range(NT):
            sp.wait_ge(*st["fin"][2].at(t, "y"))
            if t == 0:
                store(O["y_sample"].rearrange("b t d -> (b t) d"), x2[0:S, 0, :])
            else:
                store(O["y_prompt"][0, P * (t - 1):P * t, :], x2[:, t, :])
        sp.wait_ge(s_out, st_out["n"])

    @block.tensor
    def _(pe):
        def mm(out, lhsT, rhs, start=True, stop=True):
            return pe.matmul(out, lhsT, rhs, start=start, stop=stop, skip_group_check=True)

        def tr(out, in_):
            n = in_.shape[0]
            return pe.transpose(out, in_, cst[0:n, CI:CI + n])

        pe.wait_ge(s_small, 16 * N_SMALL)
        pe.wait_ge(s_hist, 16 * N_HIST)
        for c in range(12):
            tr(ps[:, 0, NHR * c:NHR * (c + 1)], hrow[:, P * c:P * (c + 1)])
        for j in range(4):
            for a in range(2):
                tr(ps[:, 1 + j // 2, 240 * (j % 2) + 120 * a:240 * (j % 2) + 120 * (a + 1)],
                   urow[:, a, P * j:P * (j + 1)])
            tr(ps[:, 3, (CT + 3) * j:(CT + 3) * (j + 1)], vrow[:, P * j:P * (j + 1)])
        tr(ps[:, 4, 0:KD + 2], nrow[:]).then_inc(*st["pre"][0]("hist"))

        PA1, AA1, DA1, LA1 = st["A1"]
        PA2, AA2, DA2, _ = st["A2"]

        def a1(t):
            pe.wait_ge(*DA1.at(t, "h"))
            if isinstance(t, int):
                pe.wait_ge(*st["pre"][1].at(0, "chistT"))
                pe.wait_ge(*st["pre"][2].at(0, "vec"))
            for k in range(KD):
                m = tr(ps[:, k // 4, P * (k % 4):P * (k % 4 + 1)], ht[:, P * k:P * (k + 1)])
            m.then_inc(*PA1("tr"))
            pe.wait_ge(*DA1.at(t, "hTt"))
            if isinstance(t, int):
                pe.wait_ge(s_wat, 16)
            else:
                pe.wait_ge(*AA2.at(t - 1, "at"))
            for f in range(2):
                for k in range(KD):
                    m = mm(ps[:, 2 + f, 0:NAT // 2], hTt[:, k], wat[:, k, f * (NAT // 2):(f + 1) * (NAT // 2)],
                           k == 0, k == KD - 1)
            m.then_inc(*PA1("proj"))

        def a2(t):
            pe.wait_ge(*DA2.at(t, "qk"))
            if not (isinstance(t, int) and t == 0):
                pe.wait_ge(*AA2.at(t - 1, "qT"))
            for j in range(4):
                tr(ps[:, 4, P * j:P * (j + 1)], qp[:, j].rearrange("p g d -> p (g d)"))
            tr(ps[:, 5, 0:P], at[:, 520:648]).then_inc(*PA2("qkT"))

        a1(0)
        with pe.Fori(1, NT) as t:
            a1(t)
            a2(t - 1)
        a2(NT - 1)
        end_phase(pe, 1)

        def proj(slot, half, chunks, free):
            for c, (c0, n) in enumerate(chunks):
                if free and c == 0:
                    pe.wait_ge(*free)
                for k in range(KD):
                    m = mm(ps[:, 3 * half + c, 0:n], wB[:, slot, k], hT[:, k, c0:c0 + n], k == 0, k == KD - 1)
            return m

        PB, AB, DB, LB = st["bq"]
        PZ, AZ, _, _ = st["bz"]
        PU, AU, DU, LU = st["bu"]

        def round_(j):
            first = isinstance(j, int)
            tiles = ((CHS, None if first else AB.at(3 * j - 2, "ev"), PU, "gate"),
                     (CHS, None if first else AB.at(3 * j - 1, "ev"), PU, "value"),
                     (CHP, AU.at(j, "sig"), PZ, "proj"), (CHS, DU.at(j, "u"), PB, "proj"),
                     (CHS, AZ.at(j, "z"), PB, "proj"), (CHS, AB.at(3 * j, "ev"), PB, "proj"))
            for c, (chunks, free, to, step) in enumerate(tiles):
                pe.wait_ge(s_w[c % 3], 32 * j + 16 * (c // 3) + 16)
                proj(c % 3, c % 2, chunks, free).then_inc(*to(step))

        round_(0)
        with pe.Fori(1, 4) as j:
            round_(j)
        PL, AL, DL, _ = st["ln"]
        pe.wait_ge(*DU.at(3, "conv"))
        for c, (c0, n) in enumerate(CHP):
            if c:
                pe.wait_ge(*AL.at(c - 1, "std"))
            for j in range(4):
                m = mm(ps[:, 6, 0:n], cc(C1), oc[:, j, c0:c0 + n], j == 0, j == 3)
            m.then_inc(*PL("mu"))
            pe.wait_ge(*AL.at(c, "sq"))
            for j in range(4):
                m = mm(ps[:, 7, 0:n], cc(C1), sqb[:, j, 0:n], j == 0, j == 3)
            m.then_inc(*PL("var"))
        PR, AR, DR, _ = st["rows"]
        pe.wait_ge(*LB.at(11, "tail"))
        for c in range(12):
            tr(ps[0:24, c // 4, P * (c % 4):P * (c % 4 + 1)], tailT[:, c, 0:24])
        for c in range(12):
            m = tr(ps[0:3, 3 + c // 4, P * (c % 4):P * (c % 4 + 1)], tailT[:, c, 24:27])
        m.then_inc(*PR("q"))
        pe.wait_ge(*LU.at(3, "tail"))
        pe.wait_ge(*AL.at(2, "std"))
        for j in range(4):
            m = tr(ps[0:S + CT - 1, 6, P * j:P * (j + 1)], utail[:, j])
        m.then_inc(*PR("u"))
        P2, A2, D2, _ = st["l2"]

        def l2(n):
            pe.wait_ge(*A2.at(n, "sq"))
            if isinstance(n, int) and n == 0:
                pe.wait_ge(*AR.at(0, "q"))
            for c, (c0, w) in enumerate(CHS):
                m = mm(ps[:, c, 0:w], cc(C1), uxt[:, c0:c0 + w])
            m.then_inc(*P2("ss"))

        l2(0)
        with pe.Fori(1, 2 * H) as n:
            l2(n)
        end_phase(pe, 2)

        PT_, AT_, DT_, LT_ = st["at"]

        def attend(t, n):
            first = isinstance(n, int)
            pe.wait_ge(*LT_.at(n, "q"))
            if not first:
                pe.wait_ge(*AT_.at(n - 1, "oT"))
            for h in range(HB):
                g, j = h // 4, h % 4
                r = slice(HD * g, HD * (g + 1))
                mm(ps[:, h // 2, 2 * P * (h % 2):2 * P * (h % 2 + 1)], qst[r, j, :],
                   kst[r, :])
                m = mm(ps[:, 4 + g, NM * j:NM * (j + 1)], qst[r, j, :], kT[r, S:S + NM])
            m.then_inc(*PT_("sc"))
            pe.wait_ge(*AT_.at(n, "exp"))
            for h in range(HB):
                m = tr(ps[0:NM, 6 + h // 4, P * (h % 4):P * (h % 4 + 1)], sc[:, h, 0:NM])
            m.then_inc(*PT_("trm"))
            for h in range(4):
                for b in range(2):
                    m = tr(ps[:, h // 2, 2 * P * (h % 2) + P * b:2 * P * (h % 2) + P * (b + 1)],
                           sc[:, h, NM + P * b:NM + P * (b + 1)])
            m.then_inc(*PT_("tra"))
            for h in range(4, 8):
                for b in range(2):
                    m = tr(ps[:, h // 2, 2 * P * (h % 2) + P * b:2 * P * (h % 2) + P * (b + 1)],
                           sc[:, h, NM + P * b:NM + P * (b + 1)])
            m.then_inc(*PT_("trb"))
            pe.wait_ge(*DT_.at(n, "PTm"))
            pe.wait_ge(*AT_.at(n, "PTa"))
            pe.wait_ge(*DT_.at(n, "PTb"))
            if first:
                pe.wait_ge(s_vm, 16)
            for h in range(HB):
                g = h // 4
                o = ps[:, 5, HD * h:HD * (h + 1)]
                mm(o, PTm[:, h, :], vm[:, HD * g:HD * (g + 1)], True, False)
                for b in range(2):
                    m = mm(o, PT[:, h, P * b:P * (b + 1)],
                           kv[:, ds(t - 1 + b, 1), P + HD * g:P + HD * (g + 1)].rearrange("p a d -> p (a d)"),
                           False, b == 1)
            m.then_inc(*PT_("pv"))
            pe.wait_ge(*DT_.at(n, "o"))
            for j in range(4):
                m = tr(ps[:, 4, P * j:P * (j + 1)], otok[:, 2 * j:2 * j + 2, :].rearrange("p h d -> p (h d)"))
            m.then_inc(*PT_("oT"))

        attend(1, 0)
        with pe.Fori(2, NT) as t:
            attend(t, t - 1)
        end_phase(pe, 3)

        PS, AS, DS, _ = st["sa"]
        pe.wait_ge(s_win, 16 * N_WIN)
        for b in range(NS):
            tr(ps[:, b // 4, P * (b % 4):P * (b % 4 + 1)], win[:, b, 0:P])
        tr(ps[:, 2, 0:P], mk[:]).then_inc(*PS("kT"))
        pe.wait_ge(*AS.at(0, "kT"))
        pe.wait_ge(*DS.at(0, "qs"))
        for b in range(NS):
            for g in range(KVH):
                r = slice(HD * g, HD * (g + 1))
                m0 = 32 * (2 * (b % 2) + g)
                c0 = (W + NM + TS) * (b // 2 % 3)
                m = mm(ps[m0:m0 + 32, 3 + 2 * g + b // 6, c0:c0 + W + NM + TS],
                       qs[r, b].rearrange("p j t -> p (j t)"), kTw[r, b, :])
        m.then_inc(*PS("sc"))
        pe.wait_ge(*AS.at(0, "exp"))
        for q in range(4):
            tr(ps[:, 0, P * q:P * (q + 1)], scs[:, q, 0:W])
            m = tr(ps[0:NM + TS, 1, P * q:P * (q + 1)], scs[:, q, W:W + NM + TS])
        m.then_inc(*PS("tr"))
        pe.wait_ge(*AS.at(0, "PT"))
        for b in range(NS):
            for g in range(KVH):
                m0 = 32 * (2 * (b % 2) + g)
                o = ps[m0:m0 + 32, 7, HD * (b // 2):HD * (b // 2 + 1)]
                mm(o, PTw[:, b // 2, m0:m0 + 32], win[:, b, P + HD * g:P + HD * (g + 1)], True, False)
                m = mm(o, PTn[:, b // 2, m0:m0 + 32], vmn[:, b, HD * g:HD * (g + 1)], False, True)
        m.then_inc(*PS("pv"))
        pe.wait_ge(*DS.at(0, "o"))
        for q in range(4):
            m = tr(ps[:, 2, P * q:P * (q + 1)], odup[:, q].rearrange("p a d -> p (a d)"))
        m.then_inc(*PS("oT"))
        end_phase(pe, 4)

        PG, AG, DG, LG = st["gd"]

        def heads(f):
            for h in range(H):
                m = f(h)
            return m

        def bank(b, h):
            return ps[:, b, P * h:P * (h + 1)]

        def delta(t):
            first = isinstance(t, int)
            v = 0 if first else 1
            if not first:
                pe.wait_ge(*DG.at(t - 1, "S"))
                pe.wait_ge(*AG.at(t - 1, "o"))
            pe.wait_ge(*LG.at(t, "stage"))
            heads(lambda h: mm(bank(0, h), gsm[:, 16 + h:17 + h].to_broadcast([P, P]), cc(CU + v * P)))
            g = gsm[:, 16:16 + H]
            mm(ps[:, 7, 0:H], cc(CU + v * P), g)
            mm(ps[:, 7, H:2 * H], cc(CSS + v * P), g).then_inc(*PG("G"))
            heads(lambda h: mm(bank(1, h), stg[:, H + h], stg[:, H + h]))
            heads(lambda h: mm(bank(2, h), stg[:, H + h], stg[:, h])).then_inc(*PG("kkpq"))
            heads(lambda h: tr(bank(3, h), stg[:, H + h]))
            heads(lambda h: tr(bank(4, h), stg[:, 2 * H + h])).then_inc(*PG("kv"))
            pe.wait_ge(*DG.at(t, "At"))
            heads(lambda h: tr(bank(5, h), G["AtT"][:, h])).then_inc(*PG("At"))
            pe.wait_ge(*DG.at(t, "D1"))
            heads(lambda h: tr(bank(6, h), G["Dm"][:, h])).then_inc(*PG("D1"))
            pe.wait_ge(*AG.at(t, "D1"))
            for l in range(1, 7):
                pe.wait_ge(*DG.at(t, f"B{l}"))
                if l > 1:
                    pe.wait_ge(*DG.at(t, f"X{l - 1}"))
                heads(lambda h: mm(bank(5, h), G[f"B{l % 2}"][:, h], G["Dt"][:, h])).then_inc(*PG(f"W{l}"))
                pe.wait_ge(*AG.at(t, f"W{l}"))
                if l < 6:
                    heads(lambda h: mm(bank(6, h), G["Wt"][:, h], G["Dm"][:, h]))
                heads(lambda h: mm(bank(7, h), G["Dm"][:, h], G["Wt"][:, h])).then_inc(*PG(f"X{l}"))
            pe.wait_ge(*DG.at(t, "X6"))
            heads(lambda h: mm(bank(4, h), G["kbg"][:, h], G["Dt"][:, h])).then_inc(*PG("u"))
            pe.wait_ge(*AG.at(t, "nw"))
            if first:
                pe.wait_ge(s_S0, 16)
                for h in range(H):
                    for b in range(NS):
                        m = mm(ps[:, 5, P * h + TS * b:P * h + TS * (b + 1)], S0[:, b, h],
                               G["nwT"][:, h, TS * b:TS * (b + 1)])
                m.then_inc(*PG("v2"))
            else:
                for h in range(H):
                    mm(bank(3, h), G["Dt"][:, h], G["vb"][:, h], True, False)
                    m = mm(bank(3, h), G["nwT"][:, h], St[:, h], False, True)
                m.then_inc(*PG("v2"))
            if first:
                pe.wait_ge(s_vnT, 1)
                for h in range(H):
                    mm(bank(3, h), G["Dt"][:, h], G["vb"][:, h], True, False)
                    m = mm(bank(3, h), G["Wt"][:, h], ident, False, True)
                m.then_inc(s_vnP, 1)
            pe.wait_ge(*DG.at(t, "vn"))
            for h in range(H):
                if first:
                    mm(bank(1, h), G["vnew"][:, h], G["PT2"][:, h], True, False)
                    for b in range(NS):
                        m = mm(ps[:, 1, P * h + TS * b:P * h + TS * (b + 1)], S0[:, b, h],
                               G["qdec"][:, h, TS * b:TS * (b + 1)], False, b == NS - 1)
                else:
                    mm(bank(1, h), G["vnew"][:, h], G["PT2"][:, h], True, False)
                    m = mm(bank(1, h), St[:, h], G["qdec"][:, h], False, True)
            m.then_inc(*PG("o"))
            if first:
                for h in range(H):
                    pe.wait_ge(s_vx, h + 1)
                    for f in range(2):
                        mm(ps[:, 4 + f, :], G["kdec"][:, h], vexp[:, 4 * f:4 * f + 4, :].rearrange("p s d -> p (s d)"))
                    m = mm(bank(6, 0), G["kdec"][:, h], vexp[:, NS, :])
                    if h < H - 1:
                        m.then_inc(s_dS0, 1)
                        pe.wait_ge(s_vx2, h + 1)
                m.then_inc(*PG("dS"))
            else:
                heads(lambda h: mm(bank(2, h), G["kdec"][:, h], G["vnew"][:, h])).then_inc(*PG("dS"))

        delta(0)
        with pe.Fori(1, NT) as t:
            delta(t)
        end_phase(pe, 5)

        PN, AN, DN, _ = st["gn"]
        with pe.Fori(0, H) as h:
            pe.wait_ge(*AN.at(h, "sq"))
            for c, (c0, n) in enumerate(((0, S), (S + NM, 512), (S + NM + 512, 512))):
                m = mm(ps[:, c, 0:n], cc(C1), gnt[:, c0:c0 + n])
            m.then_inc(*PN("ss"))
            pe.wait_ge(*AN.at(h, "std"))
        end_phase(pe, 6)

        PM, AM, DM, _ = st["mg"]

        def merge(n, k):
            for c, (c0, w) in enumerate(CHP):
                q = 3 * n + c
                for r, br in enumerate((oa, ob, oc)):
                    if not (isinstance(n, int) and n == 0 and c == 0):
                        pe.wait_ge(*AM.at(q - 1, f"s{r}"))
                    for a in range(KD):
                        m = mm(ps[:, 2 * r, 0:w], gw[:, k, r, a], hT[:, a, c0:c0 + w], a == 0, a == KD - 1)
                    m.then_inc(*PM(f"g{r}"))
                    if not (isinstance(n, int) and n == 0 and c == 0):
                        pe.wait_ge(*DM.at(q - 1, f"m{r}"))
                    for a in range(4):
                        m = mm(ps[:, 2 * r + 1, 0:w], bw[:, k, r, a], br[:, a, c0:c0 + w], a == 0, a == 3)
                    m.then_inc(*PM(f"b{r}"))

        for n in range(2):
            pe.wait_ge(s_gw[n], 96)
            merge(n, n)
        with pe.Fori(1, 4) as i:
            for k in range(2):
                pe.wait_ge(s_gw[k], 96 * i + 96)
                merge(2 * i + k, k)
        end_phase(pe, 7)

        PO, AO, DO, LO = st["op"]
        pe.wait_ge(s_wo, 48)

        def outproj(t):
            first = isinstance(t, int)
            rows = S if first else P
            pe.wait_ge(*LO.at(t, "stage"))
            for f in range(2):
                for k in range(KD):
                    m = mm(ps[0:rows, f, :], mst[:, k, 0:rows], wo[:, k, 512 * f:512 * (f + 1)], k == 0, k == KD - 1)
            m.then_inc(*PO("mix"))
            pe.wait_ge(*DO.at(t, "h"))
            for k in range(KD):
                m = tr(ps[:, 2 + k // 4, P * (k % 4):P * (k % 4) + rows], he[0:rows, k:D:KD])
            m.then_inc(*PO("tr"))
            pe.wait_ge(*DO.at(t, "hT"))
            for k in range(KD):
                m = mm(ps[0:rows, 4, 0:NG + E], h2t[:, k, 0:rows], wr[:, k], k == 0, k == KD - 1)
            m.then_inc(*PO("rt"))

        outproj(0)
        with pe.Fori(1, NT) as t:
            outproj(t)
        pe.wait_ge(*st["rt"][2].at(0, "oh"))
        mm(ps[:, 5, 0:NT * E], cc(CU + P), ohm[:].rearrange("p t e -> p (t e)"))
        mm(ps[:, 6, 0:NT * E], cc(C1), ohm[:].rearrange("p t e -> p (t e)")).then_inc(*st["rt"][0]("cnt"))
        end_phase(pe, 8)

        PGU, AGU, DGU, _ = st["gu"]
        PY, AY, DY, _ = st["dn"]

        def turn(i, k, w):
            pe.wait_ge(s_xg[k], w)
            for a in range(KD):
                m = tr(ps[:, a // 4, P * (a % 4):P * (a % 4 + 1)], xg[:, k, a:D:KD])
            m.then_inc(*PGU("tr"))

        def gate_up(i, k, w):
            pe.wait_ge(s_ew[k], w)
            pe.wait_ge(*DGU.at(i, "xT"))
            for m_ in range(2):
                for ft in range(2):
                    for a in range(KD):
                        m = mm(ps[:, 2 + k, 2 * P * m_ + P * ft:2 * P * m_ + P * (ft + 1)],
                               ew[k][:, m_, F * a + P * ft:F * a + P * (ft + 1)], xT[:, a], a == 0, a == KD - 1)
            m.then_inc(*PGU("gu"))

        def down(i, k, w):
            pe.wait_ge(s_dw[k], w)
            pe.wait_ge(*DGU.at(i, "h"))
            if not (isinstance(i, int) and i < 2):
                pe.wait_ge(*AY.at(i - 2, "y0"))
                pe.wait_ge(*DY.at(i - 2, "y1"))
            for f in range(2):
                for a in range(2):
                    m = mm(ps[:, 4 + 2 * k + f, :], hid[:, k, a], ew[k][:, 2, D * a + 512 * f:D * a + 512 * (f + 1)],
                           a == 0, a == 1)
            m.then_inc(*PY("y"))

        turn(0, 0, 16)
        gate_up(0, 0, 32)
        turn(1, 1, 16)

        def pair(j):
            for k in (1, 0):
                i = 2 * j + 2 - k
                u = j if k else j + 1
                gate_up(i, k, 32 * u + 32)
                turn(i + 1, 1 - k, 16 * (j + 1) + 16)
                down(i - 1, 1 - k, 16 * (j + 1))

        pair(0)
        with pe.Fori(1, (NSLOT - 2) // 2) as j:
            pair(j)
        gate_up(NSLOT - 1, 1, 16 * NSLOT)
        down(NSLOT - 2, 0, 8 * NSLOT)
        down(NSLOT - 1, 1, 8 * NSLOT)

    @block.scalar
    def _(act):
        def f(out, in_, fn, **kw):
            return act.activation(out, in_, fn, **kw)

        e1, e128 = eps[:, 0:1], eps[:, 1:2]
        act.wait_ge(*st["pre"][0].at(0, "hist"))
        f(histT[:].rearrange("p c n -> p (c n)"), ps[:, 0, 0:12 * NHR], ACT.Copy).then_inc(*st["pre"][1]("histT"))
        f(chistT[:, 0:2].rearrange("p c n -> p (c n)"), ps[:, 1, 0:480], ACT.Copy)
        f(chistT[:, 2:4].rearrange("p c n -> p (c n)"), ps[:, 2, 0:480], ACT.Copy).then_inc(*st["pre"][1]("chistT"))

        PA1, AA1, DA1, _ = st["A1"]
        PA2, AA2, DA2, _ = st["A2"]
        act.wait_ge(s_init, 2)

        def a1(t):
            if isinstance(t, int):
                act.wait_ge(s_x0, 32)
            else:
                act.wait_ge(s_x, t * 16)
                act.wait_ge(*DA1.at(t - 1, "rs"))
            f(sqj[:], xt[:], ACT.Square, accum_out=st1[:, 0:1]).then_inc(*AA1("sq"))
            act.drain()
            f(st1[:, 1:2], st1[:, 0:1], ACT.Sqrt, scale=1.0 / D, bias=e1).then_inc(*AA1("std"))

        def a2(t):
            act.wait_ge(*PA1.at(t, "proj"))
            if not (isinstance(t, int) and t == 0):
                act.wait_ge(*DA2.at(t - 1, "keep"))
                act.wait_ge(*PA2.at(t - 1, "qkT"))
            f(at[:, 0:NAT // 2], ps[:, 2, 0:NAT // 2], ACT.Copy)
            f(at[:, NAT // 2:NAT], ps[:, 3, 0:NAT // 2], ACT.Copy).then_inc(*AA2("at"))
            act.drain()
            f(sq2[:], at[:, 8:8 + NQK], ACT.Square).then_inc(*AA2("sq2"))
            act.wait_ge(*DA2.at(t, "ssq"))
            f(st2[:, 10:20], st2[:, 0:10], ACT.Sqrt, scale=1.0 / HD, bias=e1).then_inc(*AA2("std2"))
            act.wait_ge(*PA2.at(t, "qkT"))
            f(qT[:, :, ds(P * t, P)], ps[:, 4, :].rearrange("p (j n) -> p j n", j=4), ACT.Copy, scale=qw[:])
            f(kT[:, ds(P * t, P)], ps[:, 5, 0:P], ACT.Copy).then_inc(*AA2("qT"))

        a1(0)
        with act.Fori(1, NT) as t:
            a1(t)
            a2(t - 1)
        a2(NT - 1)
        _, AGB, DGB, _ = st["gb"]
        act.wait_ge(*DGB.at(0, "x"))
        f(tmq36[:], tmq36[:], ACT.Exp, scale=-1.0)
        act.drain()
        f(tmq36[:], tmq36[:], ACT.Ln, bias=1.0).then_inc(*AGB("lse"))
        f(alog[:], alog[:], ACT.Exp)
        f(ab[:, :, H:2 * H], ab[:, :, H:2 * H], ACT.Sigmoid).then_inc(*AGB("sig"))
        end_phase(act, 1)

        PB, AB, DB, LB = st["bq"]
        exP = lambda p: ext[:, p, EXS:]
        exS = lambda p: ext[:, p, 0:EXS].rearrange("p (b n) -> p b n", b=NS)

        def bq(n, k):
            p, q = k, 3 * ((k + 1) % 2)
            early = isinstance(n, int) and n < 3
            act.wait_ge(*PB.at(n, "proj"))
            if not early:
                act.wait_ge(*DB.at(n - 3, "conv"))
                act.wait_ge(*LB.at(n - 3, "tail"))
            o = CONV - 1 + NM
            f(exS(p)[:, :, CONV - 1:], ps[:, q, 0:S].rearrange("p (b n) -> p b n", b=NS), ACT.Copy)
            f(exP(p)[:, o:o + CH - S], ps[:, q, S:CH], ACT.Copy)
            f(exP(p)[:, o + CH - S:o + 2 * CH - S], ps[:, q + 1, 0:CH], ACT.Copy)
            f(exP(p)[:, o + 2 * CH - S:o + SEQ], ps[:, q + 2, 0:CH - NM], ACT.Copy)
            f(exP(p)[:, CONV - 1:o], ps[:, q + 2, CH - NM:CH], ACT.Copy).then_inc(*AB("ev"))

        def silu(n):
            act.wait_ge(*DB.at(n, "conv"))
            f(qkv[:, ds(n, 1), :], qkv[:, ds(n, 1), :], ACT.Silu).then_inc(*AB("silu"))

        PZ, AZ, _, _ = st["bz"]
        PU, AU, DU, LU = st["bu"]

        def round_(j):
            act.wait_ge(*PU.at(j, "gate"))
            if not isinstance(j, int):
                act.wait_ge(*DU.at(j - 1, "u"))
            for c, (c0, n) in enumerate(CHS):
                m = f(sig[:, c0:c0 + n], ps[:, c, 0:n], ACT.Sigmoid)
            m.then_inc(*AU("sig"))
            act.wait_ge(*PZ.at(j, "proj"))
            for c, (c0, n) in enumerate(CHP):
                m = f(z[:, ds(j, 1), c0:c0 + n], ps[:, c:c + 1, 0:n], ACT.Silu)
            m.then_inc(*AZ("z"))
            for k in range(3):
                bq(3 * j + k, k)
                silu(3 * j + k)

        round_(0)
        with act.Fori(1, 4) as j:
            round_(j)
        PL, AL, DL, _ = st["ln"]
        for c, (c0, n) in enumerate(CHP):
            act.wait_ge(*DL.at(c, "cent"))
            if c == 0:
                act.wait_ge(*LB.at(11, "tail"))
            f(sqb[:, :, 0:n], oc[:, :, c0:c0 + n], ACT.Square).then_inc(*AL("sq"))
            act.wait_ge(*PL.at(c, "var"))
            f(rsb[:, 0, 0:n], ps[:, 7, 0:n], ACT.Sqrt, scale=1.0 / CC, bias=e1).then_inc(*AL("std"))
            act.wait_ge(*DL.at(c, "norm"))
            for j in range(4):
                m = f(oc[:, j, c0:c0 + n], oc[:, j, c0:c0 + n], ACT.Silu, scale=dvec[:, j, CT + 1:CT + 2],
                      bias=dvec[:, j, CT + 2:CT + 3])
            m.then_inc(*AL("silu"))
        PR, AR, DR, _ = st["rows"]
        act.wait_ge(*PR.at(0, "q"))
        f(hq[:, 0, :], ps[0:24, 0:3, :].rearrange("p b n -> p (b n)"), ACT.Copy)
        f(hq[0:3, 1, :], ps[0:3, 3:6, :].rearrange("p b n -> p (b n)"), ACT.Copy).then_inc(*AR("q"))
        P2, A2, D2, _ = st["l2"]

        def l2(n, scale, bias):
            f(uxt[:, 0:ALL], qkv[:, ds(n, 1), :].rearrange("p a n -> p (a n)"), ACT.Square).then_inc(*A2("sq"))
            act.wait_ge(*P2.at(n, "ss"))
            if not (isinstance(n, int) and n == 0):
                act.wait_ge(*D2.at(n - 1, "norm"))
            for c, (c0, w) in enumerate(CHS):
                m = f(sig[:, c0:c0 + w], ps[:, c, 0:w], ACT.Sqrt, scale=scale, bias=bias)
            m.then_inc(*A2("std"))

        act.wait_ge(*LU.at(3, "tail"))
        act.wait_ge(*DU.at(3, "conv"))
        act.drain()
        l2(0, float(DK), e128)
        with act.Fori(1, H) as n:
            l2(n, float(DK), e128)
        with act.Fori(H, 2 * H) as n:
            l2(n, 1.0, e1)
        end_phase(act, 2)

        PT_, AT_, DT_, LT_ = st["at"]

        def attend(t, n):
            act.wait_ge(*DT_.at(n, "max"))
            for h in range(HB):
                f(sc[:, h, :], sc[:, h, :], ACT.Exp, bias=st2[:, 8 + h:9 + h], accum_out=st2[:, 16 + h:17 + h])
            f(st2[:, 24:32], st2[:, 24:32], ACT.Exp).then_inc(*AT_("exp"))
            act.wait_ge(*PT_.at(n, "tra"))
            f(PT[:, 0:4].rearrange("p h n -> p (h n)"), ps[:, 0:2, :].rearrange("p b n -> p (b n)"),
              ACT.Copy).then_inc(*AT_("PTa"))
            act.wait_ge(*PT_.at(n, "oT"))
            if isinstance(n, int):
                act.wait_ge(s_hq, 1)
            f(ob[:, :, tile_cols(t)], ps[:, 4, :].rearrange("p (j n) -> p j n", j=4), ACT.Copy)\
                .then_inc(*AT_("oT"))

        attend(1, 0)
        with act.Fori(2, NT) as t:
            attend(t, t - 1)
        end_phase(act, 3)

        PS, AS, DS, _ = st["sa"]
        act.wait_ge(*PS.at(0, "kT"))
        f(kTw[:, :, 0:W], ps[:, 0:2, :].rearrange("p c (b n) -> p (c b) n", b=4), ACT.Copy)
        f(kTw[:, :, W:W + NM], ps[:, 2, 0:P].rearrange("p (b n) -> p b n", b=NS), ACT.Copy)
        f(kTw[:, :, W + NM:], kT[:, 0:S].rearrange("p (b n) -> p b n", b=NS), ACT.Copy).then_inc(*AS("kT"))
        act.wait_ge(*DS.at(0, "max"))
        for q in range(4):
            f(scs[:, q], scs[:, q], ACT.Exp, bias=st2[:, 4 + q:5 + q], accum_out=st2[:, 8 + q:9 + q])
        f(st2[:, 12:16], st2[:, 12:16], ACT.Exp).then_inc(*AS("exp"))
        act.wait_ge(*PS.at(0, "tr"))
        f(PTw[:].rearrange("p q n -> p (q n)"), ps[:, 0, :], ACT.Copy)
        f(PTn[:].rearrange("p q n -> p (q n)"), ps[0:NM + TS, 1, :], ACT.Copy).then_inc(*AS("PT"))
        end_phase(act, 4)

        PG, AG, DG, LG = st["gd"]

        def flat(x):
            return x.rearrange("p h n -> p (h n)")

        def delta(t):
            first = isinstance(t, int)
            act.wait_ge(*PG.at(t, "G"))
            if not first:
                act.wait_ge(*DG.at(t - 1, "S"))
            f(flat(G["eG"][:]), ps[:, 0, :], ACT.Exp)
            act.wait_ge(*DG.at(t, "cols"))
            f(gsm[:, 8:8 + H], gsm[:, 0:H], ACT.Exp).then_inc(*AG("eG"))
            act.wait_ge(*DG.at(t, "arg"))
            f(flat(G["dec"][:]), flat(G["dec"][:]), ACT.Exp)
            f(gsm[:, 12:12 + H], gsm[:, 12:12 + H], ACT.Exp).then_inc(*AG("dec"))
            act.wait_ge(*PG.at(t, "D1"))
            f(flat(G["Dt"][:]), ps[:, 6, :], ACT.Copy).then_inc(*AG("D1"))
            for l in range(1, 7):
                act.wait_ge(*PG.at(t, f"W{l}"))
                f(flat(G["Wt"][:]), ps[:, 5, :], ACT.Copy).then_inc(*AG(f"W{l}"))
            act.wait_ge(*PG.at(t, "u"))
            f(flat(G["nwT"][:]), ps[:, 4, :], ACT.Copy, scale=-1.0).then_inc(*AG("nw"))
            if first:
                act.wait_ge(*PG.at(t, "v2"))
                act.wait_ge(s_init, 3)
                f(G["Wt"][:, :, 0:S], ps[:, 5, :].rearrange("p (h n) -> p h n", h=H)[:, :, 0:S], ACT.Copy)\
                    .then_inc(s_vnT, 1)
            act.wait_ge(*PG.at(t, "o"))
            n = S + NM if first else P
            cols = slice(0, n) if first else bass.ds(S + NM + P * (t - 1), P)
            f(qkv[:, 0:H, cols], ps[:, 1, :].rearrange("p (h n) -> p h n", h=H)[:, :, 0:n], ACT.Copy)\
                .then_inc(*AG("o"))

        delta(0)
        with act.Fori(1, NT) as t:
            delta(t)
        end_phase(act, 5)

        PN, AN, DN, _ = st["gn"]

        def gnorm(h):
            f(gnt[:], qkv[:, ds(h, 1), :].rearrange("p a n -> p (a n)"), ACT.Square).then_inc(*AN("sq"))
            act.wait_ge(*PN.at(h, "ss"))
            if not isinstance(h, int):
                act.wait_ge(*DN.at(h - 1, "b"))
            for c, (c0, n) in enumerate(((0, S), (S, 512), (S + 512, 512))):
                m = f(gstd[:, c0:c0 + n], ps[:, c, 0:n], ACT.Sqrt, scale=1.0 / DK, bias=e1)
            m.then_inc(*AN("std"))

        gnorm(0)
        with act.Fori(1, H) as h:
            gnorm(h)
        end_phase(act, 6)

        PM, AM, DM, _ = st["mg"]

        def merge(n):
            for c, (c0, w) in enumerate(CHP):
                q = 3 * n + c
                for r in range(3):
                    act.wait_ge(*PM.at(q, f"g{r}"))
                    if r < 2:
                        if not (isinstance(n, int) and n == 0 and c == 0):
                            act.wait_ge(*DM.at(q - 1, "m2" if r == 0 else "m1"))
                    else:
                        act.wait_ge(*DM.at(q, "m0"))
                    f(gs[:, r % 2, 0:w], ps[:, 2 * r, 0:w], ACT.Sigmoid).then_inc(*AM(f"s{r}"))

        merge(0)
        with act.Fori(1, KD) as n:
            merge(n)
        end_phase(act, 7)

        PO, AO, DO, _ = st["op"]

        def outproj(t):
            rows = S if isinstance(t, int) else P
            act.wait_ge(*DO.at(t, "x2"))
            f(sqe[0:rows, :], x2[0:rows, ds(t, 1), :].rearrange("p a n -> p (a n)"), ACT.Square,
              accum_out=st1[0:rows, 0:1]).then_inc(*AO("sq"))
            act.drain()
            f(st1[0:rows, 1:2], st1[0:rows, 0:1], ACT.Sqrt, scale=1.0 / D, bias=eps[0:rows, 0:1]).then_inc(*AO("std"))

        outproj(0)
        with act.Fori(1, NT) as t:
            outproj(t)
        _, AR_, DR_, _ = st["rt"]
        act.wait_ge(*DR_.at(0, "gm"))
        f(ra[:, :, 0:NG], ra[:, :, 0:NG], ACT.Exp).then_inc(*AR_("eg"))
        act.wait_ge(*DR_.at(0, "em"))
        f(r1[:, 4], r1[:, 4], ACT.Exp).then_inc(*AR_("es"))
        end_phase(act, 8)

        PGU, AGU, DGU, _ = st["gu"]
        PY, AY, DY, _ = st["dn"]

        def silu_gate(i, k):
            act.wait_ge(*PGU.at(i, "gu"))
            if not (isinstance(i, int) and i == 0):
                act.wait_ge(*DGU.at(i - 1, "h"))
            f(sg[:].rearrange("p f n -> p (f n)"), ps[:, 2 + k, 0:2 * P], ACT.Silu).then_inc(*AGU("s"))

        def y0(i, k, w):
            act.wait_ge(*PY.at(i, "y"))
            if w is not None:
                act.wait_ge(s_ys[k], w)
            f(yt[:, k, 0:512], ps[:, 4 + 2 * k, :], ACT.Copy).then_inc(*AY("y0"))

        silu_gate(0, 0)
        for i in (1, 2):
            silu_gate(i, i % 2)
            y0(i - 1, (i - 1) % 2, None)
        with act.Fori(1, (NSLOT - 2) // 2) as j:
            for k in (1, 0):
                silu_gate(2 * j + 2 - k, k)
                y0(2 * j + 1 - k, 1 - k, 16 * j)
        silu_gate(NSLOT - 1, 1)
        for k in range(2):
            y0(NSLOT - 2 + k, k, 8 * NSLOT - 16)

    @block.vector
    def _(ve):
        def tt(out, a, b, op):
            return ve.tensor_tensor(out, a, b, op)

        def ts(out, a, s1, op0, s2=None, op1=ALU.bypass):
            return ve.tensor_scalar(out, a, s1, s2, op0, op1)

        def stt(out, a, s, b, op0, op1):
            return ve.scalar_tensor_tensor(out=out, in0=a, scalar=s, in1=b, op0=op0, op1=op1)

        ve.memset(xt[:], 0.0).then_inc(s_init, 1)
        ve.memset(eps[:, 0:1], EPS)
        ve.memset(eps[:, 1:2], EPS * DK).then_inc(s_init, 1)
        ve.wait_ge(*st["pre"][0].at(0, "hist"))
        ve.tensor_copy(dvec[:].rearrange("p j n -> p (j n)"), ps[:, 3, 0:4 * (CT + 3)])
        ve.tensor_copy(nvec[:], ps[:, 4, 0:KD + 2])
        ve.drain()
        ts(qw[:], nvec[:, KD + 1:KD + 2], HD ** -0.5, ALU.mult)
        tt(st2[:, 0:HB], cst[:, CR:CR + HB], sink[:], ALU.mult)
        ve.drain()
        ve.tensor_reduce(sinkr[:], st2[:, 0:HB], AX.X, ALU.add)
        ve.drain().then_inc(*st["pre"][2]("vec"))

        PA1, AA1, DA1, LA1 = st["A1"]
        PA2, AA2, DA2, _ = st["A2"]

        def a1(t):
            ve.wait_ge(*AA1.at(t, "std"))
            ve.reciprocal(st1[:, 2:3], st1[:, 1:2]).then_inc(*DA1("rs"))
            ve.drain()
            ts(ht[:], xt[:], st1[:, 2:3], ALU.mult).then_inc(*DA1("h"))
            ve.wait_ge(*PA1.at(t, "tr"))
            if not isinstance(t, int):
                ve.wait_ge(*PA1.at(t - 1, "proj"))
                ve.wait_ge(*LA1.at(t - 1, "hT"))
            for f in range(2):
                m = tt(hTt[:, 4 * f:4 * f + 4], ps[:, f, :].rearrange("p (k n) -> p k n", k=4),
                       b3(nvec[:, 4 * f:4 * f + 4], P), ALU.mult)
            m.then_inc(*DA1("hTt"))

        def a2(t):
            ve.wait_ge(*AA2.at(t, "sq2"))
            ve.tensor_reduce(st2[:, 0:10], sq2[:].rearrange("p (h d) -> p h d", d=HD), AX.X, ALU.add)\
                .then_inc(*DA2("ssq"))
            ve.wait_ge(*AA2.at(t, "std2"))
            ve.reciprocal(st2[:, 20:30], st2[:, 10:20]).then_inc(*DA2("rs2"))
            ve.drain()
            if not (isinstance(t, int) and t == 0):
                ve.wait_ge(*PA2.at(t - 1, "qkT"))
            rs = st2[:, 20:28].rearrange("p (g j) -> p g j", g=2).unsqueeze(3).to_broadcast([P, 2, 4, HD])
            tt(qp[:].rearrange("p j g d -> p g j d"),
               at[:, 8:520].rearrange("p (g j d) -> p g j d", g=2, j=4), rs, ALU.mult)
            kk = at[:, 520:648].rearrange("p (h d) -> p h d", d=HD)
            tt(kk, kk, b3(st2[:, 28:30], HD), ALU.mult)
            ve.drain()
            tt(kk, kk, b2(kw[:], KVH), ALU.mult).then_inc(*DA2("qk"))
            ve.drain()
            ve.tensor_copy(kv[:, ds(t, 1), :].rearrange("p a n -> p (a n)"), at[:, 520:NAT])
            ve.tensor_copy(ab[:, ds(t, 1), :].rearrange("p a n -> p (a n)"), at[:, 0:8]).then_inc(*DA2("keep"))

        a1(0)
        with ve.Fori(1, NT) as t:
            a1(t)
            a2(t - 1)
        a2(NT - 1)
        _, AGB, DGB, _ = st["gb"]
        ve.drain()
        tt(tmp36[:], ab[:, :, 0:H], b2(dtb[:], NT), ALU.add)
        ve.drain()
        ts(tmq36[:], tmp36[:], -1.0, ALU.mult)
        ve.drain()
        tt(tmq36[:], tmq36[:], tmp36[:], ALU.max).then_inc(*DGB("x"))
        ts(tmp36[:], tmp36[:], 0.0, ALU.max).then_inc(*DGB("m"))
        ve.drain()
        ve.wait_ge(*AGB.at(0, "lse"))
        tt(tmp36[:], tmp36[:], tmq36[:], ALU.add)
        ve.drain()
        ve.wait_ge(*AGB.at(0, "sig"))
        stt(ab[:, :, 0:H], tmp36[:], -1.0, b2(alog[:], NT), ALU.mult, ALU.mult).then_inc(*DGB("g"))
        end_phase(ve, 1)

        PB, AB, DB, LB = st["bq"]

        def bq(n, k):
            p = k
            ve.wait_ge(*AB.at(n, "ev"))
            ve.wait_ge(*LB.at(n, "hist"))
            es = ext[:, p, 0:EXS].rearrange("p (b n) -> p b n", b=NS)
            outs = qkv[:, ds(n, 1), 0:S].rearrange("p a (b n) -> p (a b) n", b=NS)
            outp = qkv[:, ds(n, 1), S:ALL].rearrange("p a n -> p (a n)")
            for j in range(CONV):
                w = histT[:, ds(n, 1), NHR - CONV + j:NHR - CONV + j + 1].rearrange("p a b -> p (a b)")
                i_s, ip = es[:, :, j:j + TS], ext[:, p, EXS + j:EXS + j + NM + SEQ]
                if j == 0:
                    ts(outs, i_s, w, ALU.mult)
                    m = ts(outp, ip, w, ALU.mult)
                else:
                    ve.drain()
                    stt(outs, i_s, w, outs, ALU.mult, ALU.add)
                    m = stt(outp, ip, w, outp, ALU.mult, ALU.add)
            m.then_inc(*DB("conv"))

        PU, AU, DU, LU = st["bu"]
        us = uxt[:, 0:UXS].rearrange("p (b n) -> p b n", b=NS)

        def round_(j):
            ve.drain()
            ve.wait_ge(*AU.at(j, "sig"))
            ve.wait_ge(*PU.at(j, "value"))
            if not isinstance(j, int):
                ve.wait_ge(*LU.at(j - 1, "tail"))
            o = UXS + CT - 1 + NM
            tt(us[:, :, CT - 1:], ps[:, 3, 0:S].rearrange("p (b n) -> p b n", b=NS),
               sig[:, 0:S].rearrange("p (b n) -> p b n", b=NS), ALU.mult)
            tt(uxt[:, o:o + CH - S], ps[:, 3, S:CH], sig[:, S:CH], ALU.mult)
            tt(uxt[:, o + CH - S:o + 2 * CH - S], ps[:, 4, 0:CH], sig[:, CH:2 * CH], ALU.mult)
            tt(uxt[:, o + 2 * CH - S:o + SEQ], ps[:, 5, 0:CH - NM], sig[:, 2 * CH:TOK], ALU.mult)
            tt(uxt[:, o - NM:o], ps[:, 5, CH - NM:CH], sig[:, TOK:ALL], ALU.mult).then_inc(*DU("u"))
            ve.drain()
            ve.wait_ge(*LU.at(j, "hist"))
            outs = oc[:, ds(j, 1), 0:S].rearrange("p a (b n) -> p (a b) n", b=NS)
            outp = oc[:, ds(j, 1), S:TOK].rearrange("p a n -> p (a n)")

            def tap(k):
                return dvec[:, ds(j, 1), k:k + 1].rearrange("p a n -> p (a n)")

            for k in range(CT):
                i_s, ip, w = us[:, :, k:k + TS], uxt[:, UXS + NM + k:UXS + NM + k + SEQ], tap(k)
                if k == 0:
                    bias = tap(CT)
                    ts(outs, i_s, w, ALU.mult, bias, ALU.add)
                    m = ts(outp, ip, w, ALU.mult, bias, ALU.add)
                else:
                    ve.drain()
                    stt(outs, i_s, w, outs, ALU.mult, ALU.add)
                    m = stt(outp, ip, w, outp, ALU.mult, ALU.add)
            m.then_inc(*DU("conv"))
            for k in range(3):
                bq(3 * j + k, k)

        round_(0)
        with ve.Fori(1, 4) as j:
            round_(j)
        ve.drain()
        PL, AL, DL, _ = st["ln"]
        for c, (c0, n) in enumerate(CHP):
            ve.wait_ge(*PL.at(c, "mu"))
            for j in range(4):
                o = oc[:, j, c0:c0 + n]
                m = stt(o, ps[:, 6, 0:n], -1.0 / CC, o, ALU.mult, ALU.add)
            m.then_inc(*DL("cent"))
            ve.drain()
            ve.wait_ge(*AL.at(c, "std"))
            ve.reciprocal(rsb[:, 1, 0:n], rsb[:, 0, 0:n]).then_inc(*DL("rs"))
            ve.drain()
            tt(oc[:, :, c0:c0 + n], oc[:, :, c0:c0 + n], b2(rsb[:, 1, 0:n], 4), ALU.mult).then_inc(*DL("norm"))
        PR, AR, DR, _ = st["rows"]
        ve.wait_ge(*PR.at(0, "u"))
        ve.tensor_copy(hu[:], ps[0:S + CT - 1, 6, :]).then_inc(*DR("u"))
        P2, A2, D2, _ = st["l2"]
        with ve.Fori(0, 2 * H) as n:
            ve.wait_ge(*A2.at(n, "std"))
            ve.reciprocal(sig[:], sig[:])
            ve.drain()
            q = qkv[:, ds(n, 1), :].rearrange("p a n -> p (a n)")
            tt(q, q, sig[:], ALU.mult).then_inc(*D2("norm"))
        end_phase(ve, 2)

        PT_, AT_, DT_, LT_ = st["at"]

        def attend(t, n):
            ve.wait_ge(*PT_.at(n, "sc"))
            for b in range(4):
                o = sc[:, 2 * b:2 * b + 2, NM:]
                i = ps[:, b, :].rearrange("p (h n) -> p h n", h=2)
                if isinstance(n, int):
                    ve.memset(o[:, :, 0:P], NEG)
                    tt(o[:, :, P:], i[:, :, P:], b2(cst[:, CB + P:CB + 2 * P], 2), ALU.add)
                else:
                    tt(o, i, b2(cst[:, CB:CB + 2 * P], 2), ALU.add)
            for g in range(KVH):
                m = ve.tensor_copy(sc[:, 4 * g:4 * g + 4, 0:NM],
                                   ps[:, 4 + g, 0:4 * NM].rearrange("p (h n) -> p h n", h=4))
            m.then_inc(*DT_("sc"))
            ve.drain()
            ve.tensor_reduce(st2[:, 0:8], sc[:], AX.X, ALU.max)
            ve.drain()
            tt(st2[:, 0:8], st2[:, 0:8], sink[:], ALU.max)
            ve.drain()
            ts(st2[:, 8:16], st2[:, 0:8], -1.0, ALU.mult)
            tt(st2[:, 24:32], sink[:], st2[:, 0:8], ALU.subtract).then_inc(*DT_("max"))
            ve.wait_ge(*AT_.at(n, "exp"))
            tt(st2[:, 32:40], st2[:, 16:24], st2[:, 24:32], ALU.add)
            ve.drain()
            ve.reciprocal(st2[:, 40:48], st2[:, 32:40]).then_inc(*DT_("den"))
            ve.wait_ge(*PT_.at(n, "trm"))
            ve.tensor_copy(PTm[:].rearrange("p h n -> p (h n)"), ps[0:NM, 6:8, :].rearrange("p b n -> p (b n)"))\
                .then_inc(*DT_("PTm"))
            ve.wait_ge(*PT_.at(n, "trb"))
            ve.tensor_copy(PT[:, 4:8].rearrange("p h n -> p (h n)"), ps[:, 2:4, :].rearrange("p b n -> p (b n)"))\
                .then_inc(*DT_("PTb"))
            ve.drain()
            ve.wait_ge(*PT_.at(n, "pv"))
            tt(otok[:], ps[:, 5, :].rearrange("p (h d) -> p h d", h=HB), b3(st2[:, 40:48], HD), ALU.mult)\
                .then_inc(*DT_("o"))

        attend(1, 0)
        with ve.Fori(2, NT) as t:
            attend(t, t - 1)
        end_phase(ve, 3)

        PS, AS, DS, _ = st["sa"]
        for j in range(4):
            m = ve.tensor_copy(qs[:, :, j, :], qT[:, j, 0:S].rearrange("p (b t) -> p b t", b=NS))
        m.then_inc(*DS("qs"))
        ve.wait_ge(*PS.at(0, "sc"))
        for r in range(4):
            rows, g, n = slice(32 * r, 32 * r + 32), r % 2, W + NM + TS
            tt(scs[rows, 0:3], ps[rows, 3 + 2 * g, 0:3 * n].rearrange("p (q n) -> p q n", q=3),
               b2(cst[rows, CM:CR], 3), ALU.add)
            m = tt(scs[rows, 3], ps[rows, 4 + 2 * g, 0:n], cst[rows, CM:CR], ALU.add)
        m.then_inc(*DS("sc"))
        ve.drain()
        ve.tensor_reduce(st2[:, 0:4], scs[:], AX.X, ALU.max)
        ve.drain()
        ts(st2[:, 4:8], st2[:, 0:4], sinkr[:], ALU.max, -1.0, ALU.mult)
        ve.drain()
        ts(st2[:, 12:16], st2[:, 4:8], sinkr[:], ALU.add).then_inc(*DS("max"))
        ve.wait_ge(*AS.at(0, "exp"))
        tt(st2[:, 16:20], st2[:, 8:12], st2[:, 12:16], ALU.add)
        ve.drain()
        ve.reciprocal(st2[:, 20:24], st2[:, 16:20]).then_inc(*DS("den"))
        ve.drain()
        ve.wait_ge(*PS.at(0, "pv"))
        for a in range(2):
            m = tt(odup[:, :, a, :], ps[:, 7, 0:4 * HD].rearrange("p (q d) -> p q d", q=4), b3(st2[:, 20:24], HD),
                   ALU.mult)
        m.then_inc(*DS("o"))
        ve.wait_ge(*PS.at(0, "oT"))
        oT = ps[:, 2, :].rearrange("p (s g h t) -> p s g h t", g=2, h=4, t=TS)
        for g in range(KVH):
            for h in range(4):
                half = slice(HD * (h % 2), HD * (h % 2 + 1))
                m = ve.tensor_copy(ob[half, 2 * g + h // 2, 0:S].rearrange("p (s t) -> p s t", t=TS),
                                   oT[half, :, g, h, :])
        m.then_inc(*DS("oT"))
        end_phase(ve, 4)

        PG, AG, DG, LG = st["gd"]

        def flat(x):
            return x.rearrange("p h n -> p (h n)")

        def hb(b):
            return ps[:, b, :].rearrange("p (h n) -> p h n", h=H)

        beta = gsm[:, 20:24]

        def delta(t):
            first = isinstance(t, int)
            v = 0 if first else 1
            ve.wait_ge(*PG.at(t, "G"))
            ve.wait_ge(*LG.at(t, "stage"))
            ve.tensor_copy(gsm[:, 0:8], ps[:, 7, 0:8]).then_inc(*DG("cols"))
            ve.drain()
            ve.wait_ge(*AG.at(t, "eG"))
            for h in range(H):
                stt(G["dec"][:, h], ps[:, 0, P * h:P * (h + 1)], gsm[:, h:h + 1], cc(CN + v * P),
                    ALU.subtract, ALU.add)
            tt(gsm[:, 12:16], gsm[:, 4:8], gsm[:, 0:4], ALU.subtract).then_inc(*DG("arg"))
            ve.wait_ge(*AG.at(t, "dec"))
            ve.wait_ge(*PG.at(t, "kkpq"))
            tt(G["AtT"][:], hb(1), G["dec"][:], ALU.mult)
            ve.drain()
            tt(G["AtT"][:], G["AtT"][:], b2(cc(CS + v * P), H), ALU.mult).then_inc(*DG("At"))
            tt(G["PT2"][:], hb(2), G["dec"][:], ALU.mult).then_inc(*DG("PT2"))
            ve.wait_ge(*PG.at(t, "kv"))
            tt(G["vb"][:], hb(4), b3(beta, P), ALU.mult)
            tt(gsm[:, 24:28], beta, gsm[:, 8:12], ALU.mult)
            ve.drain()
            tt(G["kbg"][:], hb(3), b3(gsm[:, 24:28], P), ALU.mult)
            tt(G["kdec"][:], hb(3), b3(gsm[:, 12:16], P), ALU.mult)
            tt(G["qdec"][:], stg[:, 0:H], G["eG"][:], ALU.mult).then_inc(*DG("kq"))
            ve.wait_ge(*PG.at(t, "At"))
            tt(G["Am"][:], hb(5), b3(beta, P), ALU.mult).then_inc(*DG("A"))
            ve.drain()
            tt(G["B0"][:], G["Am"][:], b2(cc(CL), H), ALU.mult)
            ve.drain()
            tt(G["Dm"][:], b2(ident, H), G["B0"][:], ALU.subtract).then_inc(*DG("D1"))
            tt(G["B1"][:], G["Am"][:], b2(cc(CL + P), H), ALU.mult).then_inc(*DG("B1"))
            for l in range(1, 7):
                if l < 6:
                    ve.drain()
                    tt(G[f"B{(l + 1) % 2}"][:], G["Am"][:], b2(cc(CL + (l + 1) * P), H), ALU.mult)\
                        .then_inc(*DG(f"B{l + 1}"))
                ve.drain()
                ve.wait_ge(*PG.at(t, f"X{l}"))
                if l < 6:
                    tt(flat(G["Dm"][:]), flat(G["Dm"][:]), ps[:, 6, :], ALU.subtract)
                tt(flat(G["Dt"][:]), flat(G["Dt"][:]), ps[:, 7, :], ALU.subtract).then_inc(*DG(f"X{l}"))
            if first:
                ve.memset(G["Wt"][:], 0.0).then_inc(s_init, 1)
                ve.wait_ge(s_vnP, 1)
            else:
                ve.wait_ge(*PG.at(t, "v2"))
            ve.tensor_copy(flat(G["vnew"][:]), ps[:, 3, :]).then_inc(*DG("vn"))
            if not first:
                ve.wait_ge(*PG.at(t, "dS"))
                for h in range(H):
                    m = stt(St[:, h], St[:, h], G["eG"][:, h, P - 1:P], ps[:, 2, P * h:P * (h + 1)],
                            ALU.mult, ALU.add)
                m.then_inc(*DG("S"))
                return
            ve.drain()
            ve.wait_ge(*PG.at(t, "o"))
            for h in range(H):
                tt(vexp[:], b2(G["vnew"][:, h], NS + 1), b3(cst[:, CQ:CQ + NS + 1], P), ALU.mult)\
                    .then_inc(s_vx, 1)
                if h < H - 1:
                    ve.wait_ge(s_dS0, h + 1)
                else:
                    ve.wait_ge(*PG.at(t, "dS"))
                for b in range(NS):
                    stt(S0[:, b, h], S0[:, b, h], G["eG"][:, h, TS * b + TS - 1:TS * (b + 1)],
                        ps[:, 4 + b // 4, P * (b % 4):P * (b % 4 + 1)], ALU.mult, ALU.add)
                m = ve.tensor_copy(St[:, h], ps[:, 6, 0:P])
                m.then_inc(s_vx2, 1) if h < H - 1 else m.then_inc(*DG("S"))

        delta(0)
        with ve.Fori(1, NT) as t:
            delta(t)
        end_phase(ve, 5)

        PN, AN, DN, _ = st["gn"]
        ve.wait_ge(s_sT, 1)
        with ve.Fori(0, H) as h:
            ve.wait_ge(*AN.at(h, "std"))
            ve.reciprocal(gstd[:], gstd[:])
            ve.drain()
            tt(gstd[:], gstd[:], z[:, ds(h, 1), :].rearrange("p a n -> p (a n)"), ALU.mult).then_inc(*DN("a"))
            ve.drain()
            raw = qkv[:, ds(h, 1), :].rearrange("p a n -> p (a n)")
            o = oa[:, ds(h, 1), :].rearrange("p a n -> p (a n)")
            stt(o[:, 0:S], raw[:, 0:S], nvec[:, KD:KD + 1], gstd[:, 0:S], ALU.mult, ALU.mult)
            stt(o[:, S:], raw[:, S + NM:], nvec[:, KD:KD + 1], gstd[:, S:], ALU.mult, ALU.mult).then_inc(*DN("b"))
        end_phase(ve, 6)

        PM, AM, DM, _ = st["mg"]
        with ve.Fori(0, KD) as n:
            for c, (c0, w) in enumerate(CHP):
                q = 3 * n + c
                o = mT[:, ds(n, 1), c0:c0 + w].rearrange("p a n -> p (a n)")
                for r in range(3):
                    ve.wait_ge(*AM.at(q, f"s{r}"))
                    ve.wait_ge(*PM.at(q, f"b{r}"))
                    if r == 0:
                        tt(o, ps[:, 1, 0:w], gs[:, 0, 0:w], ALU.mult).then_inc(*DM("m0"))
                        ve.drain()
                        continue
                    tt(gm[:, r % 2, 0:w], ps[:, 2 * r + 1, 0:w], gs[:, r % 2, 0:w], ALU.mult).then_inc(*DM(f"m{r}"))
                    ve.drain()
                    tt(o, o, gm[:, r % 2, 0:w], ALU.add)
                    ve.drain()
        end_phase(ve, 7)

        PO, AO, DO, LO = st["op"]
        ve.memset(rl[:], 0.0)
        for k in range(EPG):
            ve.memset(iota4[:, k:k + 1], float(k - EPG))
        ve.drain()

        def outproj(t):
            first = isinstance(t, int)
            rows = S if first else P
            x = x2[0:rows, ds(t, 1), :].rearrange("p a n -> p (a n)")
            ve.wait_ge(*PO.at(t, "mix"))
            ve.wait_ge(s_xe, 16 * t + 16)
            tt(x, ps[0:rows, 0:2, :].rearrange("p b n -> p (b n)"), xe[0:rows, :], ALU.add).then_inc(*DO("x2"))
            ve.wait_ge(*AO.at(t, "std"))
            ve.reciprocal(st1[0:rows, 2:3], st1[0:rows, 1:2]).then_inc(*DO("rs"))
            ve.drain()
            if not first:
                ve.wait_ge(s_h2, 16 * t)
            ts(he[0:rows, :], x, st1[0:rows, 2:3], ALU.mult).then_inc(*DO("h"))
            ve.wait_ge(*PO.at(t, "tr"))
            for f in range(2):
                m = tt(h2t[:, 4 * f:4 * f + 4, 0:rows], ps[:, 2 + f, :].rearrange("p (k n) -> p k n", k=4)[:, :, 0:rows],
                       b3(n2w[:, 4 * f:4 * f + 4], rows), ALU.mult)
            m.then_inc(*DO("hT"))
            ve.wait_ge(*PO.at(t, "rt"))
            tt(rl[0:rows, ds(t, 1), :].rearrange("p a n -> p (a n)"), ps[0:rows, 4, 0:NG + E], rbias[0:rows, :], ALU.add)\
                .then_inc(*DO("rl"))

        ve.memset(zid[:], 0)
        ve.wait_ge(s_rc, 16)
        ve.tensor_copy(tok[:], rcs[:, CX - NC0:CY - NC0]).then_inc(s_cast, 1)
        outproj(0)
        with ve.Fori(1, NT) as t:
            outproj(t)
        _, AR_, DR_, _ = st["rt"]

        def d(ins):
            ve.drain()
            return ins

        def first_max(hot, x, m, i):
            ve.tensor_reduce(m, x, AX.X, ALU.max)
            ve.drain()
            tt(hot, x, b3(m, EPG), ALU.is_equal)
            ve.drain()
            tt(hot, hot, b2(iota4[:], NT), ALU.mult)
            ve.drain()
            ve.tensor_reduce(i, hot, AX.X, ALU.min)
            ve.drain()
            tt(hot, b2(iota4[:], NT), b3(i, EPG), ALU.is_equal)
            ve.drain()

        ve.drain()
        gl = rl[:, :, 0:NG]
        first_max(goh[:], gl, r1[:, 0], r1[:, 1])
        ve.memset(goh[S:P, 0, :], 0.0)
        ve.drain()
        tt(ra[:, :, 0:NG], gl, b3(r1[:, 0], NG), ALU.subtract).then_inc(*DR_("gm"))
        g4 = goh[:].unsqueeze(3).to_broadcast([P, NT, NG, EPG])
        c4 = comb[:].rearrange("p t (g k) -> p t g k", g=NG)
        tt(c4, rl[:, :, NG:].rearrange("p t (g k) -> p t g k", g=NG), g4, ALU.mult)
        ve.drain()
        ve.tensor_reduce(esel[:], comb[:].rearrange("p t (g k) -> p t k g", g=NG), AX.X, ALU.add)
        ve.drain()
        first_max(rb[:], esel[:], r1[:, 2], r1[:, 3])
        stt(rc[:], rb[:], NEG, esel[:], ALU.mult, ALU.add)
        ve.drain()
        first_max(rd[:], rc[:], r1[:, 4], r1[:, 5])
        tt(r1[:, 4], r1[:, 4], r1[:, 2], ALU.subtract).then_inc(*DR_("em"))
        for k, hot in enumerate((rb, rd)):
            tt(ohs[:, k].rearrange("p t (g k) -> p t g k", g=NG), g4,
               hot[:].unsqueeze(2).to_broadcast([P, NT, NG, EPG]), ALU.mult)
        ve.drain()
        tt(ohm[:], ohs[:, 0], ohs[:, 1], ALU.add).then_inc(*DR_("oh"))
        ve.wait_ge(*AR_.at(0, "es"))
        ve.tensor_reduce(r1[:, 6], ra[:, :, 0:NG], AX.X, ALU.add)
        ve.drain()
        stt(r1[:, 7], r1[:, 4], 1.0, r1[:, 6], ALU.add, ALU.mult)
        ve.drain()
        ve.reciprocal(r1[:, 7], r1[:, 7])
        ve.drain()
        ts(wts[:, 0], r1[:, 7], 1.0, ALU.mult)
        tt(wts[:, 1], r1[:, 7], r1[:, 4], ALU.mult).then_inc(*DR_("w"))
        ve.wait_ge(*st["rt"][0].at(0, "cnt"))
        ve.memset(cnt[:, 0, :], 0.0)
        tot = ps[:, 6, 0:NT * E].rearrange("p (t e) -> p t e", e=E)
        for t in range(NT):
            ve.drain()
            tt(cnt[:, t + 1, :], cnt[:, t, :], tot[:, t, :], ALU.add)
        ve.drain()
        tt(slot[:], ps[:, 5, 0:NT * E].rearrange("p (t e) -> p t e", e=E), cnt[:, 0:NT, :], ALU.add)
        b16 = big[:, 0:E * NT].rearrange("p (e m) -> p e m", m=NT)
        tt(b16, b3(cnt[:, NT, :], NT), b2(rcs[:, 0:CW - NC0], E), ALU.is_gt)
        ve.drain()
        ve.tensor_reduce(til[:, 0], b16, AX.X, ALU.add)
        ve.drain()
        bee = big[:, 0:E * E].rearrange("p (e f) -> p e f", f=E)
        tt(bee, b2(til[:, 0], E), rcs[:, CY - NC0:].rearrange("p (e f) -> p e f", f=E), ALU.mult)
        ve.drain()
        ve.tensor_reduce(til[:, 1], bee, AX.X, ALU.add)
        ve.drain()
        tt(til[:, 2], til[:, 0], til[:, 1], ALU.add)
        ve.drain()
        bie = big[:].rearrange("p (i e) -> p i e", e=E)
        tt(bie, b2(til[:, 2], NSLOT), b3(rcs[:, CW - NC0:CX - NC0], E), ALU.is_le)
        ve.drain()
        ve.tensor_reduce(texf[:], bie, AX.X, ALU.add)
        ve.drain()
        ts(texf[:], texf[:], float(E - 1), ALU.min)
        for k in range(2):
            for to, x in ((slf, slot[:]), (slb, b2(til[:, 1], NT))):
                tt(ohm[:], ohs[:, k], x, ALU.mult)
                ve.drain()
                ve.tensor_reduce(to[:, k], ohm[:], AX.X, ALU.add)
                ve.drain()
        rank, first, m_ = (x[:].rearrange("p k t -> p (k t)") for x in (slf, slb, slm))
        brm = big[:, 0:2 * NT * NT].rearrange("p (a m) -> p a m", m=NT)
        tt(brm, b3(rank, NT), b2(rcs[:, 0:CW - NC0], 2 * NT), ALU.is_gt)
        ve.drain()
        ve.tensor_reduce(m_, brm, AX.X, ALU.add)
        stt(rank, rank, float(NSLOT), first, ALU.mult, ALU.add)
        ve.drain()
        stt(rank, m_, float(1 - NSLOT * P), rank, ALU.mult, ALU.add)
        ve.drain()
        ts(rank, rank, float(NSLOT * P - 1 - NSLOT), ALU.add)
        ve.drain()
        ve.tensor_copy(slu[:], slf[:])
        ve.tensor_copy(tex[:], texf[:]).then_inc(*DR_("tab"))
        end_phase(ve, 8)

        PGU, AGU, DGU, _ = st["gu"]
        PY, AY, DY, _ = st["dn"]

        def columns(i):
            ve.wait_ge(*PGU.at(i, "tr"))
            for f in range(2):
                m = tt(xT[:, 4 * f:4 * f + 4], ps[:, f, :].rearrange("p (k n) -> p k n", k=4),
                       b3(n2w[:, 4 * f:4 * f + 4], P), ALU.mult)
            m.then_inc(*DGU("xT"))

        def hidden(i, k):
            ve.wait_ge(*AGU.at(i, "s"))
            if not (isinstance(i, int) and i < 2):
                ve.wait_ge(*PY.at(i - 2, "y"))
            tt(hid[:, k], ps[:, 2 + k, 2 * P:4 * P].rearrange("p (f n) -> p f n", f=2), sg[:], ALU.mult)\
                .then_inc(*DGU("h"))

        def y1(i, k, w):
            ve.wait_ge(*PY.at(i, "y"))
            if w is not None:
                ve.wait_ge(s_ys[k], w)
            ve.tensor_copy(yt[:, k, 512:D], ps[:, 5 + 2 * k, :]).then_inc(*DY("y1"))

        columns(0)
        hidden(0, 0)
        for i in (1, 2):
            columns(i)
            hidden(i, i % 2)
            y1(i - 1, (i - 1) % 2, None)
        with ve.Fori(1, (NSLOT - 2) // 2) as j:
            for k in (1, 0):
                columns(2 * j + 2 - k)
                hidden(2 * j + 2 - k, k)
                y1(2 * j + 1 - k, 1 - k, 16 * j)
        columns(NSLOT - 1)
        hidden(NSLOT - 1, 1)
        for k in range(2):
            y1(NSLOT - 2 + k, k, 8 * NSLOT - 16)
        for t in range(NT):
            rows = S if t == 0 else P
            ve.wait_ge(s_yg[t % 2], 32 * (t // 2) + 32)
            x = x2[0:rows, t, :]
            for k in range(2):
                m = stt(x, yg[0:rows, t % 2, k], wts[0:rows, k, t:t + 1], x, ALU.mult, ALU.add)
                if k == 0:
                    ve.drain()
            m.then_inc(*st["fin"][2]("y"))

    @block.gpsimd
    def _(po):
        cp = po.tensor_copy
        for p in range(3):
            po.memset(ext[:, p, EXS:EXS + CONV - 1], 0.0)
        po.memset(uxt[:, UXS:UXS + CT - 1], 0.0)
        PA1, AA1, DA1, LA1 = st["A1"]

        def a1(t):
            po.wait_ge(*DA1.at(t, "hTt"))
            if isinstance(t, int):
                cp(hT[:, :, 0:S], hTt[:, :, 0:S])
                cp(hT[:, :, TOK:ALL], hTt[:, :, S:S + NM]).then_inc(*LA1("hT"))
            else:
                cp(hT[:, :, tile_cols(t)], hTt[:]).then_inc(*LA1("hT"))

        a1(0)
        with po.Fori(1, NT) as t:
            a1(t)
        end_phase(po, 1)

        PB, AB, DB, LB = st["bq"]

        def bq(n, k):
            es = ext[:, k, 0:EXS].rearrange("p (b n) -> p b n", b=NS)
            if not (isinstance(n, int) and n < 3):
                po.wait_ge(*DB.at(n - 3, "conv"))
            cp(es[:, :, 0:CONV - 1],
               histT[:, ds(n, 1), 0:NS * (CONV - 1)].rearrange("p a (b n) -> p (a b) n", b=NS)).then_inc(*LB("hist"))
            po.wait_ge(*AB.at(n, "ev"))
            cp(tailT[:, ds(n, 1), 0:24].rearrange("p a (b n) -> p (a b) n", b=NS), es[:, :, TS:])
            cp(tailT[:, ds(n, 1), 24:27].rearrange("p a n -> p (a n)"),
               ext[:, k, EXS + NM + SEQ:EXS + EXP_]).then_inc(*LB("tail"))

        PU, AU, DU, LU = st["bu"]
        us = uxt[:, 0:UXS].rearrange("p (b n) -> p b n", b=NS)

        def round_(j):
            if not isinstance(j, int):
                po.wait_ge(*DU.at(j - 1, "conv"))
            cp(us[:, :, 0:CT - 1], chistT[:, ds(j, 1)].rearrange("p a (b n) -> p (a b) n", b=NS)).then_inc(*LU("hist"))
            po.wait_ge(*DU.at(j, "u"))
            cp(utail[:, ds(j, 1), 0:S].rearrange("p a (b n) -> p (a b) n", b=NS), us[:, :, CT - 1:])
            cp(utail[:, ds(j, 1), S:].rearrange("p a n -> p (a n)"), uxt[:, UXS + UXP - (CT - 1):]).then_inc(*LU("tail"))
            for k in range(3):
                bq(3 * j + k, k)

        round_(0)
        with po.Fori(1, 4) as j:
            round_(j)
        end_phase(po, 2)

        PT_, AT_, DT_, LT_ = st["at"]
        cp(kst[:], kT[:, 0:2 * P])
        cp(qst[:], qT[:, :, P:2 * P]).then_inc(*LT_("q"))
        with po.Fori(2, NT) as t:
            po.wait_ge(*PT_.at(t - 2, "sc"))
            cp(kst[:], kT[:, ds(P * (t - 1), 2 * P)])
            cp(qst[:], qT[:, :, ds(P * t, P)]).then_inc(*LT_("q"))
        end_phase(po, 3)
        end_phase(po, 4)

        PG, AG, DG, LG = st["gd"]
        po.memset(stg[:], 0.0)
        po.drain()
        cp(gsm[:, 16:24], ab[:, 0, :])
        cp(stg[:, :, 0:S + NM], qkv[:, :, 0:S + NM]).then_inc(*LG("stage"))
        with po.Fori(1, NT) as t:
            po.wait_ge(*DG.at(t - 1, "A"))
            po.wait_ge(*PG.at(t - 1, "kv"))
            cp(gsm[:, 16:24], ab[:, ds(t, 1), :].rearrange("p a n -> p (a n)"))
            cp(stg[:], qkv[:, :, bass.ds(S + NM + P * (t - 1), P)]).then_inc(*LG("stage"))
        end_phase(po, 5)
        end_phase(po, 6)
        end_phase(po, 7)

        PO, AO, DO, LO = st["op"]

        def outproj(t):
            first = isinstance(t, int)
            rows = S if first else P
            cols = slice(0, S) if first else tile_cols(t)
            if not first:
                po.wait_ge(*PO.at(t - 1, "mix"))
            cp(mst[:, :, 0:rows], mT[:, :, cols]).then_inc(*LO("stage"))

        outproj(0)
        with po.Fori(1, NT) as t:
            outproj(t)
        po.wait_ge(*st["rt"][2].at(0, "tab"))
        po.wait_ge(s_zt, 16)
        for t in range(NT):
            rows = S if t == 0 else P
            for k in range(2):
                po.indirect_dma_start(out=slot_tok, out_offset=bass.IndirectOffsetOnAxis(ap=slu[0:rows, k, t:t + 1], axis=0),
                                      in_=tok[0:rows, t:t + 1], in_offset=None).then_inc(s_sc, 16)
        end_phase(po, 8)

        PGU, AGU, DGU, _ = st["gu"]

        def gather(i, k):
            cp(idc[k][:], idx[:, ds(i, 1)])
            po.drain()
            po.indirect_dma_start(out=xg[:, k], out_offset=None, in_=h2_rows,
                                  in_offset=bass.IndirectOffsetOnAxis(ap=idc[k][:], axis=0)).then_inc(s_xg[k], 16)

        po.wait_ge(s_idx, 16)
        po.wait_ge(s_h2, 16 * NT)
        gather(0, 0)
        gather(1, 1)
        with po.Fori(0, (NSLOT - 2) // 2) as j:
            for k in range(2):
                po.wait_ge(*PGU.at(2 * j + k, "tr"))
                gather(2 * j + k + 2, k)
        for k in range(2):
            po.wait_ge(s_ys[k], 8 * NSLOT)
        for t in range(NT):
            rows = S if t == 0 else P
            if t >= 2:
                po.wait_ge(*st["fin"][2].at(t - 2, "y"))
            for k in range(2):
                po.indirect_dma_start(out=yg[0:rows, t % 2, k], out_offset=None, in_=y_slots,
                                      in_offset=bass.IndirectOffsetOnAxis(ap=slu[0:rows, k, t:t + 1], axis=0))\
                    .then_inc(s_yg[t % 2], 16)

    block.__exit__(None, None, None)


def launch_io():
    outs = {
        "y_prompt": (1, SEQ, D), "y_sample": (NS, TS, D), "state_gdn_p": (1, 1, H, DK, DK),
        "cache_gdn_conv_p": (1, 1, CONV - 1, QKV), "cache_swa_kv_p": (1, 1, W, 2, KVH, HD),
        "cache_meta_kv_p": (1, 1, NM, 2, KVH, HD), "cache_conv_p": (1, 1, CT - 1, CC),
        "state_gdn_s": (1, NS, H, DK, DK), "cache_gdn_conv_s": (1, NS, CONV - 1, QKV),
        "cache_swa_kv_s": (1, NS, W, 2, KVH, HD), "cache_conv_s": (1, NS, CT - 1, CC)}
    return outs


def kernel(**inputs):
    import concourse.bacc as bacc
    from concourse.bass_utils import run_bass_kernel_spmd

    nc = bacc.Bacc("TRN2", target_bir_lowering=False, num_devices=1)
    arrays = {f"in_{k}": np.ascontiguousarray(v) for k, v in inputs.items()}
    arrays["in_consts"] = constants()
    A = {k[3:]: nc.dram_tensor(k, v.shape, F32, kind="ExternalInput").ap() for k, v in arrays.items()}
    O = {k: nc.dram_tensor(f"out_{k}", s, F32, kind="ExternalOutput").ap() for k, s in launch_io().items()}
    build(nc, A, O)
    r = run_bass_kernel_spmd(nc, [arrays], core_ids=[0])
    return tuple(r.results[0][f"out_{k}"] for k in launch_io())
```
